# Optimizing a Trainium2 kernel written in Bass

```python
import jax, jax.numpy as jnp
from jax import lax
import numpy as np

D_MODEL = 1024
BATCH = 1
SEQ = 512
DEPTH = 1

PLE_DIM = 256
HEAD_DIM = 64
D_CONF = 3 * D_MODEL // 8
D_SHORT = 3 * D_MODEL // 8
D_POOL = D_MODEL - D_CONF - D_SHORT
D_IN = 2 * D_CONF + 3 * D_SHORT + D_POOL
IN_SPLITS = tuple(int(v) for v in np.cumsum([D_CONF, D_CONF, D_SHORT, D_SHORT, D_SHORT]))
CONF_KERNEL = 31
SHORT_KERNEL = 3
POOL_WINDOWS = (2, 4, 8, 16)
N_POOL_GROUPS = len(POOL_WINDOWS)
POOL_GROUP = D_POOL // N_POOL_GROUPS
N_EXPERTS = 32
TOP_K = 4
D_EXPERT = D_MODEL
SWIGLU_LIMIT = 7.0
SWIGLU_ALPHA = 1.702
MOE_BLOCK = 128
LN_EPS = 1e-5
DEEPNORM_ALPHA = float((2 * DEPTH) ** 0.25)
DEEPNORM_BETA = float((8 * DEPTH) ** -0.25)


def layer_norm(x, g, b):
    xf = x.astype(jnp.float32)
    mu = xf.mean(-1, keepdims=True)
    var = jnp.square(xf - mu).mean(-1, keepdims=True)
    y = (xf - mu) * lax.rsqrt(var + LN_EPS)
    return (y * g.astype(jnp.float32) + b.astype(jnp.float32)).astype(x.dtype)

def causal_depthwise_conv(u, w):
    k, c = w.shape
    return lax.conv_general_dilated(
        u, w[:, None, :].astype(u.dtype), window_strides=(1,), padding=[(k - 1, 0)],
        dimension_numbers=("NWC", "WIO", "NWC"), feature_group_count=c)

def multiscale_pool(v, pool_w, pool_scale):
    b, s, _ = v.shape
    vg = v.astype(jnp.float32).reshape(b, s, N_POOL_GROUPS, POOL_GROUP)
    cs = jnp.cumsum(vg, axis=1)
    means = []
    for g, w in enumerate(POOL_WINDOWS):
        c = cs[:, :, g]
        prev = jnp.pad(c[:, : s - w], ((0, 0), (w, 0), (0, 0)))
        cnt = jnp.minimum(jnp.arange(1, s + 1), w).astype(jnp.float32)[None, :, None]
        means.append((c - prev) / cnt)
    pooled = (jnp.stack(means, axis=2) - vg).astype(v.dtype)
    mixed = jnp.einsum("bsgc,gcd->bsgd", pooled, pool_w)
    return mixed.reshape(b, s, D_POOL) * pool_scale

def hybrid_mixer(x, w_in, conv_a_w, conv_a_b, ln_a_g, ln_a_b, conv_b_w, pool_w, pool_scale, w_out):
    z = x @ w_in
    a_val, a_gate, b_gate, c_gate, b_val, pool_in = jnp.split(z, IN_SPLITS, axis=-1)
    u = a_val * jax.nn.sigmoid(a_gate)
    u = causal_depthwise_conv(u, conv_a_w) + conv_a_b
    y_a = jax.nn.silu(layer_norm(u, ln_a_g, ln_a_b))
    y_b = b_gate * causal_depthwise_conv(c_gate * b_val, conv_b_w)
    y_c = multiscale_pool(pool_in, pool_w, pool_scale)
    return jnp.concatenate([y_a, y_b, y_c], axis=-1) @ w_out

def moe_ffn(h, router_w, router_b, w_gate_up, b_gate_up, w_down, b_down):
    bsz, s, d = h.shape
    n = bsz * s
    hf = h.reshape(n, d)
    logits = (hf @ router_w + router_b).astype(jnp.float32)
    top_logits, top_idx = lax.top_k(logits, TOP_K)
    gates = jax.nn.softmax(top_logits, axis=-1)
    e_flat = top_idx.reshape(-1)
    order = jnp.argsort(e_flat)
    e_sorted = e_flat[order]
    tok_sorted = order // TOP_K
    gate_sorted = gates.reshape(-1)[order].astype(h.dtype)
    counts = jnp.bincount(e_flat, length=N_EXPERTS)
    starts = jnp.cumsum(counts) - counts
    padded = (counts + MOE_BLOCK - 1) // MOE_BLOCK * MOE_BLOCK
    pad_ends = jnp.cumsum(padded)
    pad_starts = pad_ends - padded
    dest = pad_starts[e_sorted] + (jnp.arange(n * TOP_K) - starts[e_sorted])
    n_blocks = -(-(n * TOP_K) // MOE_BLOCK) + N_EXPERTS
    n_rows = n_blocks * MOE_BLOCK
    buf = jnp.zeros((n_rows, d), h.dtype).at[dest].set(hf[tok_sorted])
    block_start = jnp.arange(n_blocks) * MOE_BLOCK
    block_expert = jnp.minimum(jnp.searchsorted(pad_ends, block_start, side="right"), N_EXPERTS - 1)

    def expert_block(args):
        xb, e = args
        gu = xb @ w_gate_up[e] + b_gate_up[e]
        gate, up = jnp.split(gu, 2, axis=-1)
        gate = jnp.minimum(gate, SWIGLU_LIMIT)
        up = jnp.clip(up, -SWIGLU_LIMIT, SWIGLU_LIMIT)
        act = (up + 1.0) * gate * jax.nn.sigmoid(SWIGLU_ALPHA * gate)
        return act @ w_down[e] + b_down[e]

    yb = lax.map(expert_block, (buf.reshape(n_blocks, MOE_BLOCK, d), block_expert))
    y_sorted = yb.reshape(n_rows, d)[dest] * gate_sorted[:, None]
    out = jnp.zeros((n, d), h.dtype).at[tok_sorted].add(y_sorted)
    return out.reshape(bsz, s, d)

def first_inputs(seed: int = 0) -> dict:
    key = jax.random.key(seed)
    ks = jax.random.split(key, 23)
    f32 = jnp.float32
    nrm = lambda k, shape, scale: jax.random.normal(k, shape, f32) * scale
    L = DEPTH
    return {
        "x": nrm(ks[0], (BATCH, SEQ, D_MODEL), 1.0),
        "p": nrm(ks[1], (DEPTH, BATCH, SEQ, PLE_DIM), 1.0),
        "w_in": nrm(ks[2], (L, D_MODEL, D_IN), D_MODEL ** -0.5),
        "conv_a_w": nrm(ks[3], (L, CONF_KERNEL, D_CONF), CONF_KERNEL ** -0.5),
        "conv_a_b": nrm(ks[4], (L, D_CONF), 0.02),
        "ln_a_g": 1.0 + nrm(ks[5], (L, D_CONF), 0.05),
        "ln_a_b": nrm(ks[6], (L, D_CONF), 0.02),
        "conv_b_w": nrm(ks[7], (L, SHORT_KERNEL, D_SHORT), SHORT_KERNEL ** -0.5),
        "pool_w": nrm(ks[8], (L, N_POOL_GROUPS, POOL_GROUP, POOL_GROUP), POOL_GROUP ** -0.5),
        "pool_scale": 1.0 + nrm(ks[9], (L, D_POOL), 0.1),
        "w_out": nrm(ks[10], (L, D_MODEL, D_MODEL), DEEPNORM_BETA * D_MODEL ** -0.5),
        "ln1_g": 1.0 + nrm(ks[11], (L, D_MODEL), 0.05),
        "ln1_b": nrm(ks[12], (L, D_MODEL), 0.02),
        "router_w": nrm(ks[13], (L, D_MODEL, N_EXPERTS), D_MODEL ** -0.5),
        "router_b": nrm(ks[14], (L, N_EXPERTS), 0.01),
        "w_gate_up": nrm(ks[15], (L, N_EXPERTS, D_MODEL, 2 * D_EXPERT), D_MODEL ** -0.5),
        "b_gate_up": nrm(ks[16], (L, N_EXPERTS, 2 * D_EXPERT), 0.02),
        "w_down": nrm(ks[17], (L, N_EXPERTS, D_EXPERT, D_MODEL), DEEPNORM_BETA * D_EXPERT ** -0.5),
        "b_down": nrm(ks[18], (L, N_EXPERTS, D_MODEL), 0.02),
        "ple_w_gate": nrm(ks[19], (L, D_MODEL, D_MODEL), D_MODEL ** -0.5),
        "ple_w_proj": nrm(ks[20], (L, PLE_DIM, D_MODEL), DEEPNORM_BETA * PLE_DIM ** -0.5),
        "ln2_g": 1.0 + nrm(ks[21], (L, D_MODEL), 0.05),
        "ln2_b": nrm(ks[22], (L, D_MODEL), 0.02),
    }

def first_block(x, p, w_in, conv_a_w, conv_a_b, ln_a_g, ln_a_b, conv_b_w, pool_w, pool_scale, w_out,
              ln1_g, ln1_b, router_w, router_b, w_gate_up, b_gate_up, w_down, b_down,
              ple_w_gate, ple_w_proj, ln2_g, ln2_b):
    for i in range(DEPTH):
        mix = hybrid_mixer(x, w_in[i], conv_a_w[i], conv_a_b[i], ln_a_g[i], ln_a_b[i], conv_b_w[i],
                           pool_w[i], pool_scale[i], w_out[i])
        h = layer_norm(DEEPNORM_ALPHA * x + mix, ln1_g[i], ln1_b[i])
        ffn = moe_ffn(h, router_w[i], router_b[i], w_gate_up[i], b_gate_up[i], w_down[i], b_down[i])
        ple = jax.nn.sigmoid(h @ ple_w_gate[i]) * (p[i] @ ple_w_proj[i])
        x = layer_norm(DEEPNORM_ALPHA * h + ffn + ple, ln2_g[i], ln2_b[i])
    return x


ATTN_WIDTH = D_MODEL // 2
ATTN_HEADS = 8
ATTN_HEAD_DIM = ATTN_WIDTH // ATTN_HEADS
DILATED_PAIRS = ((128, 1), (512, 4), (2048, 16))
ATTN_BLOCK = 128
ROPE_THETA = 10000.0
HGRN_WIDTH = D_MODEL - ATTN_WIDTH
HGRN_EXPAND = 128
HGRN_HEADS = HGRN_WIDTH // HGRN_EXPAND
HGRN_CHUNK = 16
MIX_WIDTH = ATTN_WIDTH + HGRN_WIDTH
IN_PROJ_WIDTH = 3 * ATTN_WIDTH + 4 * HGRN_WIDTH
FFN_HIDDEN = ((-(-8 * D_MODEL // 3) + 255) // 256) * 256
NORM_EPS = 1e-6


def rmsnorm(x, w):
    xf = x.astype(jnp.float32)
    y = xf * lax.rsqrt(jnp.mean(xf * xf, axis=-1, keepdims=True) + NORM_EPS)
    return (y * w.astype(jnp.float32)).astype(x.dtype)

def rotary(x):
    S, Dh = x.shape[1], x.shape[3]
    half = Dh // 2
    inv_freq = ROPE_THETA ** (-jnp.arange(half, dtype=jnp.float32) / half)
    ang = jnp.arange(S, dtype=jnp.float32)[:, None] * inv_freq[None, :]
    cos = jnp.cos(ang)[None, :, None, :]
    sin = jnp.sin(ang)[None, :, None, :]
    xf = x.astype(jnp.float32)
    x1, x2 = xf[..., :half], xf[..., half:]
    return jnp.concatenate([x1 * cos - x2 * sin, x2 * cos + x1 * sin], axis=-1)

def dilated_window_attention(q, k, v, window, dilation):
    B, S, H, Dh = q.shape
    L = S // dilation
    W = window // dilation
    n_blk = -(-L // ATTN_BLOCK)
    Lp = n_blk * ATTN_BLOCK

    def to_blocks(t):
        t = t.reshape(B, L, dilation, H, Dh).transpose(0, 2, 1, 3, 4)
        t = jnp.pad(t, ((0, 0), (0, 0), (0, Lp - L), (0, 0), (0, 0)))
        return t.reshape(B, dilation, n_blk, ATTN_BLOCK, H, Dh)

    def with_prev(t):
        prev = jnp.pad(t, ((0, 0), (0, 0), (1, 0), (0, 0), (0, 0), (0, 0)))[:, :, :-1]
        return jnp.concatenate([prev, t], axis=3)

    qb = to_blocks(q)
    kc = with_prev(to_blocks(k))
    vc = with_prev(to_blocks(v))
    scores = jnp.einsum('bdnqhe,bdnkhe->bdnhqk', qb, kc) * (Dh ** -0.5)
    qi = jnp.arange(ATTN_BLOCK)[:, None]
    kj = jnp.arange(2 * ATTN_BLOCK)[None, :]
    delta = ATTN_BLOCK + qi - kj
    blk = jnp.arange(n_blk)[:, None, None]
    valid = (delta >= 0) & (delta <= W) & ((blk > 0) | (kj >= ATTN_BLOCK))[...]
    scores = jnp.where(valid[None, None, :, None], scores, -jnp.inf)
    m = jnp.max(scores, axis=-1, keepdims=True)
    p = jnp.exp(scores - m)
    s = jnp.sum(p, axis=-1, keepdims=True)
    out = jnp.einsum('bdnhqk,bdnkhe->bdnqhe', p, vc) / s.transpose(0, 1, 2, 4, 3, 5)
    lse = (m + jnp.log(s))[..., 0].transpose(0, 1, 2, 4, 3)
    out = out.reshape(B, dilation, Lp, H, Dh)[:, :, :L].transpose(0, 2, 1, 3, 4).reshape(B, S, H, Dh)
    lse = lse.reshape(B, dilation, Lp, H)[:, :, :L].transpose(0, 2, 1, 3).reshape(B, S, H)
    return out, lse

def dilated_attention_group(q, k, v):
    B, S, _ = q.shape
    qh = rotary(q.reshape(B, S, ATTN_HEADS, ATTN_HEAD_DIM))
    kh = rotary(k.reshape(B, S, ATTN_HEADS, ATTN_HEAD_DIM))
    vh = v.reshape(B, S, ATTN_HEADS, ATTN_HEAD_DIM).astype(jnp.float32)
    outs, lses = [], []
    for window, dilation in DILATED_PAIRS:
        o, l = dilated_window_attention(qh, kh, vh, window, dilation)
        outs.append(o)
        lses.append(l)
    weights = jax.nn.softmax(jnp.stack(lses, axis=0), axis=0)
    y = jnp.sum(weights[..., None] * jnp.stack(outs, axis=0), axis=0)
    return y.reshape(B, S, ATTN_WIDTH)

def hgrn2_group(q, f_logit, i, g, lb, norm_w):
    B, S, _ = q.shape
    H, Dk, C = HGRN_HEADS, HGRN_EXPAND, HGRN_CHUNK
    N = S // C
    f = lb + (1.0 - lb) * jax.nn.sigmoid(f_logit.astype(jnp.float32))
    log_f = jnp.log(f)
    key = 1.0 - f
    qf = jax.nn.silu(q.astype(jnp.float32))

    def chunks(t):
        return t.reshape(B, N, C, H, Dk).transpose(0, 3, 1, 2, 4)

    qc, kc, vc, lfc = chunks(qf), chunks(key), chunks(i.astype(jnp.float32)), chunks(log_f)
    b = jnp.cumsum(lfc, axis=3)
    causal = jnp.tril(jnp.ones((C, C), dtype=bool))
    diff = b[:, :, :, :, None, :] - b[:, :, :, None, :, :]
    decay = jnp.exp(jnp.where(causal[:, :, None], diff, -jnp.inf))
    scores = jnp.einsum('bhntd,bhnsd,bhntsd->bhnts', qc, kc, decay)
    o_intra = jnp.einsum('bhnts,bhnsv->bhntv', scores, vc)

    b_last = b[:, :, :, -1:, :]
    q_inter = qc * jnp.exp(b)
    k_upd = kc * jnp.exp(b_last - b)
    chunk_decay = jnp.exp(b_last[:, :, :, 0, :])

    def step(state, xs):
        qn, kn, vn, dn = xs
        o = jnp.einsum('bhtd,bhdv->bhtv', qn, state)
        state = dn[..., None] * state + jnp.einsum('bhtd,bhtv->bhdv', kn, vn)
        return state, o

    xs = (jnp.moveaxis(q_inter, 2, 0), jnp.moveaxis(k_upd, 2, 0),
          jnp.moveaxis(vc, 2, 0), jnp.moveaxis(chunk_decay, 2, 0))
    state0 = jnp.zeros((B, H, Dk, Dk), dtype=jnp.float32)
    _, o_inter = lax.scan(step, state0, xs)
    o = o_intra + jnp.moveaxis(o_inter, 0, 2)
    o = o.transpose(0, 2, 3, 1, 4).reshape(B, S, H, Dk)
    o = o * lax.rsqrt(jnp.mean(o * o, axis=-1, keepdims=True) + NORM_EPS)
    o = o.reshape(B, S, HGRN_WIDTH) * norm_w.astype(jnp.float32)
    return o * jax.nn.silu(g.astype(jnp.float32))

def second_inputs(seed: int = 0) -> dict:
    key = jax.random.key(seed)
    ks = jax.random.split(key, 10)
    f32 = jnp.float32
    x = jax.random.normal(ks[0], (BATCH, SEQ, D_MODEL), f32)
    norm1_w = 1.0 + 0.02 * jax.random.normal(ks[1], (DEPTH, D_MODEL), f32)
    w_in = jax.random.normal(ks[2], (DEPTH, D_MODEL, IN_PROJ_WIDTH), f32) * D_MODEL ** -0.5
    lb_logits = 0.5 * jax.random.normal(ks[3], (DEPTH + 1, HGRN_WIDTH), f32)
    hgrn_norm_w = 1.0 + 0.02 * jax.random.normal(ks[4], (DEPTH, HGRN_WIDTH), f32)
    w_out = jax.random.normal(ks[5], (DEPTH, MIX_WIDTH, D_MODEL), f32) * MIX_WIDTH ** -0.5
    norm2_w = 1.0 + 0.02 * jax.random.normal(ks[6], (DEPTH, D_MODEL), f32)
    w_gate_up = jax.random.normal(ks[7], (DEPTH, D_MODEL, 2 * FFN_HIDDEN), f32) * D_MODEL ** -0.5
    w_down = jax.random.normal(ks[8], (DEPTH, FFN_HIDDEN, D_MODEL), f32) * FFN_HIDDEN ** -0.5
    final_norm_w = 1.0 + 0.02 * jax.random.normal(ks[9], (D_MODEL,), f32)
    return {"x": x, "norm1_w": norm1_w, "w_in": w_in, "lb_logits": lb_logits,
            "hgrn_norm_w": hgrn_norm_w, "w_out": w_out, "norm2_w": norm2_w,
            "w_gate_up": w_gate_up, "w_down": w_down, "final_norm_w": final_norm_w}

def second_block(x, norm1_w, w_in, lb_logits, hgrn_norm_w, w_out, norm2_w, w_gate_up, w_down, final_norm_w):
    lb_table = jnp.cumsum(jax.nn.softmax(lb_logits.astype(jnp.float32), axis=0), axis=0)
    h = x
    for l in range(DEPTH):
        u = rmsnorm(h, norm1_w[l])
        proj = jnp.einsum('bsd,de->bse', u, w_in[l])
        a = ATTN_WIDTH
        qa, ka, va = proj[..., :a], proj[..., a:2 * a], proj[..., 2 * a:3 * a]
        o = 3 * a
        w = HGRN_WIDTH
        qb, fb, ib, gb = (proj[..., o:o + w], proj[..., o + w:o + 2 * w],
                          proj[..., o + 2 * w:o + 3 * w], proj[..., o + 3 * w:o + 4 * w])
        ya = dilated_attention_group(qa, ka, va)
        yb = hgrn2_group(qb, fb, ib, gb, lb_table[l], hgrn_norm_w[l])
        mixed = jnp.concatenate([ya, yb], axis=-1).astype(h.dtype)
        h = h + jnp.einsum('bse,ed->bsd', mixed, w_out[l])
        u2 = rmsnorm(h, norm2_w[l])
        gu = jnp.einsum('bsd,df->bsf', u2, w_gate_up[l])
        gate, up = gu[..., :FFN_HIDDEN], gu[..., FFN_HIDDEN:]
        h = h + jnp.einsum('bsf,fd->bsd', jax.nn.silu(gate) * up, w_down[l])
    return rmsnorm(h, final_norm_w)


def setup_inputs(seed=0):
    out = dict(first_inputs(seed))
    for name, value in second_inputs(seed + 1).items():
        if name != "x":
            out[name + "_2"] = value
    return out


def reference(
    x, p, w_in, conv_a_w, conv_a_b, ln_a_g, ln_a_b, conv_b_w, pool_w, pool_scale, w_out, ln1_g,
    ln1_b, router_w, router_b, w_gate_up, b_gate_up, w_down, b_down, ple_w_gate, ple_w_proj,
    ln2_g, ln2_b, norm1_w_2, w_in_2, lb_logits_2, hgrn_norm_w_2, w_out_2, norm2_w_2,
    w_gate_up_2, w_down_2, final_norm_w_2,
):
    x = first_block(
        x, p, w_in, conv_a_w, conv_a_b, ln_a_g, ln_a_b, conv_b_w, pool_w, pool_scale, w_out,
        ln1_g, ln1_b, router_w, router_b, w_gate_up, b_gate_up, w_down, b_down, ple_w_gate,
        ple_w_proj, ln2_g, ln2_b,
    )
    return second_block(
        x, norm1_w_2, w_in_2, lb_logits_2, hgrn_norm_w_2, w_out_2, norm2_w_2, w_gate_up_2,
        w_down_2, final_norm_w_2,
    )


_drawn_inputs = setup_inputs


def setup_inputs(seed=0):
    import zlib

    import numpy as np

    out = dict(_drawn_inputs(seed))
    spreads = {}
    factors = {'conv_a_b': 2.698,
     'ln_a_b': 3.908,
     'router_b': 2.71,
     'b_gate_up': 7.932,
     'b_down': 5.238,
     'norm1_w_2': 4.296,
     'hgrn_norm_w_2': 6.846,
     'norm2_w_2': 13.47,
     'final_norm_w_2': 7.444}
    for name, (base, spread) in spreads.items():
        noise = np.random.default_rng([zlib.crc32(name.encode()), seed]).standard_normal(out[name].shape)
        drawn = base * np.exp(spread * noise) if base else spread * noise
        out[name] = __import__('jax').numpy.asarray(drawn.astype(out[name].dtype))
    for name, factor in factors.items():
        out[name] = (out[name] * factor).astype(out[name].dtype)
    return out
```

```python
from contextlib import ExitStack

import numpy as np

import concourse.bass as bass
from concourse import mybir

ALU = mybir.AluOpType
ACT = mybir.ActivationFunctionType
AX = mybir.AxisListType
F32 = mybir.dt.float32
I32 = mybir.dt.int32
U32 = mybir.dt.uint32

P = 128
S = 512
D = 1024
KT = D // P
TT = S // P
C_CONF = 384
NC_T = C_CONF // P
D_POOL = 256
CONV_A = 31
CONV_B = 3
POOL_PAD = 16
E = 32
TOPK = 4
ALPHA = float(2 ** 0.25)
LN_EPS = 1e-5
NORM_EPS = 1e-6
LIMIT = 7.0
SW_ALPHA = 1.702

CAP = 96
BLOCKS = (S * TOPK + E * (CAP - 1)) // CAP
LEAST_BLOCKS = -(-S * TOPK // CAP)
MAX_PER_EXPERT = -(-S // CAP)
META = 64
NB_META = 56
META_T = META - 1
NO_ROW = 2 * TOPK * S
META_LAST = META - 2
GU_CHUNKS = 4
DN_CHUNKS = 2
MOE_CHUNKS = GU_CHUNKS + DN_CHUNKS

HEADS = 8
DH = 64
SCALE = DH ** -0.5
HG_HEADS = 4
LEVELS = 9
TILE_LEVELS = 7
FFN = 2816
FFN_T = FFN // P
NEG = -1.0e30

RING = 6
CH = 4096
PRE = 10
RING2 = 3
POST = 26

PAR = {}
_at = 0
for _name, _n in (("conv_a_w", NC_T * CONV_A), ("conv_a_b", NC_T), ("ln_a_g", NC_T), ("ln_a_b", NC_T),
                  ("conv_b_w", NC_T * CONV_B), ("pool_scale", 2), ("ln1_g", KT), ("ln1_b", KT),
                  ("norm1", KT), ("norm2", KT), ("hg_norm", HG_HEADS), ("lb", 2 * HG_HEADS),
                  ("eps", 2)):
    PAR[_name] = _at
    _at += _n
N_PAR = _at


class Steps:

    def __init__(self, eng, sem, base=0):
        self.eng, self.sem, self.base, self.n = eng, sem, base, 0

    def __call__(self, ins):
        self.mark(ins)
        self.wait()

    def mark(self, ins):
        ins.then_inc(self.sem, 1)
        self.n += 1

    def wait(self):
        self.eng.wait_ge(self.sem, self.base + self.n)


def build(nc, a):
    ctx = ExitStack()
    with ctx:
        def sb(name, shape, dt=F32):
            return ctx.enter_context(nc.sbuf_tensor(name, shape, dt))

        def sem(name):
            return ctx.enter_context(nc.semaphore(name))

        ring = sb("ring", [P, RING * CH])
        room = sb("room", [P, 24576])
        rowvec = sb("rowvec", [P, 2 * D])
        par = sb("par", [P, N_PAR])
        cst = sb("cst", [P, 3 * P])
        poolw = sb("poolw", [P, 2, P])
        rw = sb("rw", [P, KT, E])
        rb = sb("rb", [P, E])
        eiota = sb("eiota", [P, E])
        pairs = sb("pairs", [P, TT * TOPK * 2], U32)
        blockid = sb("blockid", [1, META])
        meta = sb("meta", [1, META], I32)
        small = sb("small", [P, 128])
        bank = [ctx.enter_context(nc.psum_tensor(f"bank{i}", [P, 512], F32)) for i in range(8)]

        def v(at, n):
            return room[:, at:at + n]

        def slot(n):
            return ring[:, n * CH:(n + 1) * CH]

        def pcol(name, n=0):
            return par[:, PAR[name] + n:PAR[name] + n + 1]

        eps_ln, eps_rms = pcol("eps", 0), pcol("eps", 1)
        ident = cst[:, 0:P]
        ones = cst[:, P:2 * P]
        before = cst[:, 2 * P:3 * P]

        xT = v(0, KT * S).rearrange("p (k t) -> p k t", k=KT)
        z = v(4096, 17 * S).rearrange("p (j t) -> p j t", j=17)
        UP = 544
        upad = v(12800, NC_T * UP).rearrange("p (i t) -> p i t", i=NC_T)
        cpad = v(14432, NC_T * 516).rearrange("p (i t) -> p i t", i=NC_T)
        PP = S + POOL_PAD
        ppad = v(15980, 2 * PP).rearrange("p (i t) -> p i t", i=2)
        invcnt = v(17036, 2 * S).rearrange("p (i t) -> p i t", i=2)
        pwin = v(18060, 2 * PP).rearrange("p (i t) -> p i t", i=2)
        mu_a = v(19116, S)
        rs_a = v(19628, S)
        AV, AG, CG, BV, BG, PL = [0, 2, 4], [1, 3, 5], [6, 8, 10], [7, 9, 11], [12, 13, 14], [15, 16]
        mixT = [z[:, j, :] for j in AV + BG + PL]

        hn = v(20480, TT * D).rearrange("p (i d) -> p i d", i=TT)
        acc = v(16384, TT * D).rearrange("p (i d) -> p i d", i=TT)
        hT = v(0, KT * S).rearrange("p (k t) -> p k t", k=KT)
        pT = v(12800, 2 * S).rearrange("p (k t) -> p k t", k=2)
        sgate = v(13824, 2 * S).rearrange("p (a t) -> p a t", a=2)
        bgu = v(14848, E * 16)
        bdn = v(15360, D)
        GT = v(9216, S)
        oh = v(9728, TT * TOPK * E).rearrange("p (i k e) -> p i k e", i=TT, k=TOPK)
        ohw = v(10240, TT * TOPK * E).rearrange("p (i k e) -> p i k e", i=TT, k=TOPK)
        mask = v(10752, TT * E).rearrange("p (i e) -> p i e", i=TT)
        gmat = v(10880, TT * E).rearrange("p (i e) -> p i e", i=TT)
        pos = v(11008, TT * E).rearrange("p (i e) -> p i e", i=TT)
        logit = v(11136, TT * E).rearrange("p (i e) -> p i e", i=TT)
        cmp_be = v(4096, NB_META * E)
        plet = v(6656, S)
        xg = v(4096, D)
        xTb = v(5120, KT * CAP).rearrange("p (k s) -> p k s", k=KT)
        gu_sb = v(5888, 2 * 4 * CAP).rearrange("p (a n s) -> p a n s", a=2, n=4)
        sig_sb = v(6656, 2 * 2 * CAP).rearrange("p (a n s) -> p a n s", a=2, n=2)
        ug_sb = v(7040, 2 * 2 * CAP).rearrange("p (a n s) -> p a n s", a=2, n=2)
        actT = v(7424, KT * CAP).rearrange("p (k s) -> p k s", k=KT)
        y_sb = v(8192, D)
        yk = [t.rearrange("p (k d) -> p k d", k=TOPK) for t in (v(9216, CH), v(4096, CH), slot(4), slot(5))]
        idx_next = sb("idx_next", [P, 2], U32)
        idx_row = sb("idx_row", [P, 1], U32)
        empty = sb("empty", [P, BLOCKS + 1, 2], U32)
        bias_cur = sb("bias_cur", [P, 16])
        mv8 = sb("mv8", [P, TT, 8])
        mi8 = sb("mi8", [P, TT, 8], U32)
        mif = sb("mif", [P, TT, 8])
        gate = sb("gate", [P, TT, TOPK])
        gsum = sb("gsum", [P, TT])
        destf = sb("destf", [P, TT * TOPK])
        dest = sb("dest", [P, TT * TOPK], U32)
        cnt = sb("cnt", [P, 4, E])
        metaf = sb("metaf", [1, META])
        stats = sb("stats", [P, 2, 6])
        mva = sb("mva", [P, TT, 2])
        rstd = sb("rstd", [P, 8])
        att_s = sb("att_s", [P, 8])

        uT = hT
        qkT = v(4096, 8 * S).rearrange("p (m t) -> p m t", m=8)
        raw = v(8192, 2 * S).rearrange("p (a t) -> p a t", a=2)
        swp = v(9216, 2 * S).rearrange("p (a t) -> p a t", a=2)
        hQ = v(10240, HG_HEADS * S)
        hK = v(12288, HG_HEADS * S)
        hF = v(14336, HG_HEADS * S)
        h2 = acc
        tot = [hF, v(20480, 1024), v(21504, 512), v(22016, 256), v(22272, 128), v(22400, 64), v(22464, 32),
               v(22496, 16), v(22512, 8)]
        hG = v(22528, HG_HEADS * S).rearrange("p (h t) -> p h t", h=HG_HEADS)
        un = hn
        AT = ring[:, 4 * CH:6 * CH].rearrange("p (h j t) -> p h j t", h=HG_HEADS, j=TT)
        c2 = slot(3)
        ctab, madd, cosT, sinT = (c2[:, n * S:(n + 1) * S] for n in range(4))
        lmask = c2[:, 4 * S:4 * S + 8 * P].bitcast(I32).rearrange("p (l s) -> p l s", l=8)
        v_tok = v(10240, TT * S).rearrange("p (j c) -> p j c", j=TT)
        i_tok = v(12288, TT * S).rearrange("p (j c) -> p j c", j=TT)
        mixed = v(0, 8 * S).rearrange("p (m t) -> p m t", m=8)
        o_sb = v(20480, 2 * S).rearrange("p (a t) -> p a t", a=2)
        osq = v(21504, 2 * S).rearrange("p (a t) -> p a t", a=2)
        sc = v(14336, 2 * S).rearrange("p (a t) -> p a t", a=2)
        ex = v(15360, 2 * S).rearrange("p (a t) -> p a t", a=2)
        pTa = v(8192, TT * S).rearrange("p (j t) -> p j t", j=TT)
        un2 = ring[:, 4 * CH:5 * CH].rearrange("p (i d) -> p i d", i=TT)
        u2T = hT
        fact = v(4096, FFN_T * S).rearrange("p (f t) -> p f t", f=FFN_T)
        fsig = v(15360, 2 * S).rearrange("p (a t) -> p a t", a=2)
        outt = hn

        hn_dram = nc.dram_tensor("hn_rows", (S, D), F32).ap()
        y_dram = nc.dram_tensor("expert_rows", (TOPK * S, D), F32).ap()
        slot_dram = nc.dram_tensor("slot_rows", ((BLOCKS + 1) * CAP, 2), U32).ap()

        names = """xT_in consts_in xtok_in ln1_rows_in late_in table_zeroed hn_out scattered y_out z_ready z_evac
            pads_ready conv_ready sq_ready mean_ready var_ready std_ready ln_a_ready sgl_ready pool_in_ready
            pool_ready pool_out_ready mixT_ready mix_ready mix_evac v1_ready s1_ready hn_ready hT_done_a
            hT_done_v hnT_ready h_ready router_ready mask_ready pos_ready e_ready ex_ready meta_ready dest_ready
            gm_ready gT_ready GT_ready pleg_ready plep_ready sg_ready ple_evac bdn_ready bdn_done idx_in
            idx_kept rows_in bias_ready gu_ready gate_ready evac_done sig_done act_ready xt_ready xT_done
            down_ready y_copied yg_used ln2_rows_in fin_row_in c2_in v2_ready s2_ready x2_ready ss_ready
            un_ready unT_ready uT_done_a uT_done_v p_ready p_evac hsig_ready rot_done fK_ready lv_ready lv_upd
            lv_copied asum_ready p_evac_v vt_ready vt_evac o_ready o_evac osq_ready oms_ready ostd_ready
            hmix_ready sc_ready sc_done e2_ready pn_ready pt_ready pt_evac pv_ready pv_evac o2_ready h3_ready
            ss3_ready un3_ready unT3_ready u2T_done_a u2T_done_v f_ready fs_ready f_evac fd_used h4_ready
            ss4_ready out_ready out_written pool_waited dve_steps act_steps pool_steps moe_dve lb_ready
            lbe_ready""".split()
        s = {n: sem(n) for n in names}
        chunk_in = [sem(f"chunk_in{n}") for n in range(RING)]
        moe_in = [sem(f"moe_in{n}") for n in range(MOE_CHUNKS)]
        post_in = [sem(f"post_in{n}") for n in range(RING2)]
        yk_in = [sem(f"yk_in{n}") for n in range(TT)]
        swap_in = [sem(f"swap_in{n}") for n in range(2)]

        pre_used = ([("z_ready", 4), ("z_ready", 8), ("z_ready", 12), ("z_ready", 16), ("z_ready", 17),
                     ("mix_ready", 7), ("mix_ready", 8), ("pleg_ready", 7), ("pleg_ready", 8), ("plep_ready", 8)])
        post_used = ([("p_ready", 4 * (c + 1)) for c in range(5)] + [("vt_ready", 4), ("vt_ready", 8)]
                     + [("o2_ready", 7), ("o2_ready", 8)] + [("f_ready", 4 * (c + 1)) for c in range(11)]
                     + [("fd_used", c + 1) for c in range(6)])
        assert len(pre_used) == PRE and len(post_used) == POST

        def chunk_cols(n):
            return {4: KT * P, 9: 2 * D}.get(n, CH)

        def post_cols(n):
            return 2 * D if n == POST - 1 else CH

        def chunk(eng, n):
            eng.wait_ge(chunk_in[n % RING], 16 * (n // RING + 1))
            return slot(n % RING)

        def chunk2(eng, n):
            eng.wait_ge(post_in[n % RING2], 16 * (n // RING2 + 1))
            return slot(n % RING2)

        block = ctx.enter_context(nc.Block())

        @block.sync
        def _(sp):
            for k in range(KT):
                sp.dma_start(xT[:, k, :], a["xT"][:, k * S:(k + 1) * S]).then_inc(s["xT_in"], 16)
                if k == 0:
                    sp.dma_start(slot(0), a["wd"][0]).then_inc(chunk_in[0], 16)
            for n in range(1, PRE):
                if n >= RING:
                    sp.wait_ge(s[pre_used[n - RING][0]], pre_used[n - RING][1])
                sp.dma_start(slot(n % RING)[:, 0:chunk_cols(n)], a["wd"][n, :, 0:chunk_cols(n)])\
                  .then_inc(chunk_in[n % RING], 16)

            sp.wait_ge(s["meta_ready"], 3)
            T = sp.value_load(meta[0:1, META_T:META_T + 1], min_val=LEAST_BLOCKS, max_val=BLOCKS)

            last = sp.value_load(meta[0:1, META_LAST:META_LAST + 1], min_val=LEAST_BLOCKS - 1, max_val=BLOCKS - 1)

            def block_loads(b, first):
                expert = sp.value_load(meta[0:1, bass.ts(b, 1)], min_val=0, max_val=E - 1)
                for c in range(MOE_CHUNKS):
                    if first:
                        before_it = max(n for n in range(PRE) if n % RING == c)
                        sp.wait_ge(s[pre_used[before_it][0]], pre_used[before_it][1])
                    elif c < GU_CHUNKS:
                        sp.wait_ge(s["gu_ready"], (b - 1) * GU_CHUNKS + (c + 1))
                    else:
                        sp.wait_ge(s["down_ready"], (b - 1) * DN_CHUNKS + (c - GU_CHUNKS + 1))
                    sp.dma_start(slot(c), a["wmoe"][bass.ts(expert, 1), c].rearrange("o p n -> (o p) n"))\
                      .then_inc(moe_in[c], 16)

            block_loads(0, True)
            with sp.Fori(1, BLOCKS) as b:
                with sp.If(b < T):
                    block_loads(b, False)

            for n in range(POST):
                if n < RING2:
                    sp.wait_ge(s["gu_ready"], last * GU_CHUNKS + (n + 1))
                else:
                    sp.wait_ge(s[post_used[n - RING2][0]], post_used[n - RING2][1])
                sp.dma_start(slot(n % RING2)[:, 0:post_cols(n)], a["wp"][n, :, 0:post_cols(n)])\
                  .then_inc(post_in[n % RING2], 16)
                if n == 0:
                    sp.wait_ge(s["gu_ready"], T * GU_CHUNKS)
                    sp.dma_start(c2[:, 0:4 * S], a["c2"]).then_inc(s["c2_in"], 16)
                    sp.dma_start(lmask, a["lmask"].rearrange("p (l s) -> p l s", l=8)).then_inc(s["c2_in"], 16)
                if n == 2:
                    sp.wait_ge(s["y_out"], T * 16)
                    for i in range(TT):
                        sp.dma_start(yk[i], y_dram.rearrange("(k i p) d -> i p k d", k=TOPK, p=P)[i]).then_inc(yk_in[i], 16)
                    sp.wait_ge(s["h_ready"], 2 * TT)
                    sp.dma_start(rowvec[:, 0:D], a["rows"][2:3, :].broadcast_to([P, D])).then_inc(s["ln2_rows_in"], 16)
                    sp.dma_start(rowvec[:, D:2 * D], a["rows"][3:4, :].broadcast_to([P, D])).then_inc(s["ln2_rows_in"], 16)
                if n == 9:
                    sp.wait_ge(s["x2_ready"], 2 * TT)
                    sp.dma_start(rowvec[:, 0:D], a["rows"][4:5, :].broadcast_to([P, D])).then_inc(s["fin_row_in"], 16)

            for i in range(TT):
                sp.wait_ge(s["out_ready"], i + 1)
                sp.dma_start(a["out"][i * P:(i + 1) * P, :], outt[:, i, :]).then_inc(s["out_written"], 16)
            sp.wait_ge(s["out_written"], 16 * TT)

        @block.gpsimd
        def _(pool):
            step = Steps(pool, s["pool_steps"])
            step.mark(pool.memset(upad[:, :, 0:CONV_A - 1], 0.0))
            step.mark(pool.memset(cpad[:, :, 0:CONV_B - 1], 0.0))
            step.mark(pool.memset(ppad[:, :, 0:POOL_PAD], 0.0))
            pool.memset(pwin[:, :, 0:POOL_PAD], 0.0).then_inc(s["pads_ready"], 1)
            step.mark(pool.memset(empty[:, :, 0:1], NO_ROW))
            step(pool.memset(empty[:, :, 1:2], 0))
            pool.dma_start(slot_dram.rearrange("(p n) o -> p (n o)", p=CAP),
                           empty[0:CAP, :, :].rearrange("p n o -> p (n o)"))\
                .then_inc(s["table_zeroed"], 16)
            for i in range(TT):
                pool.wait_ge(s["hn_ready"], i + 1)
                pool.dma_start(hn_dram[i * P:(i + 1) * P, :], hn[:, i, :]).then_inc(s["hn_out"], 16)
            pool.wait_ge(s["ln1_rows_in"], 32)
            for i in range(TT):
                pool.tensor_tensor(acc[:, i, :], hn[:, i, :], rowvec[:, 0:D], ALU.mult).then_inc(s["h_ready"], 1)
                pool.wait_ge(s["h_ready"], 2 * i + 1)
                pool.tensor_tensor(acc[:, i, :], acc[:, i, :], rowvec[:, D:2 * D], ALU.add).then_inc(s["h_ready"], 1)

            pool.wait_ge(s["table_zeroed"], 16)
            pool.wait_ge(s["dest_ready"], 1)
            for i in range(TT):
                for k in range(TOPK):
                    c = i * TOPK + k
                    pool.indirect_dma_start(slot_dram, bass.IndirectOffsetOnAxis(ap=dest[:, c:c + 1], axis=0),
                                            pairs[:, 2 * c:2 * c + 2], None).then_inc(s["scattered"], 16)
            pool.wait_ge(s["scattered"], 16 * TT * TOPK)
            pool.wait_ge(s["hn_out"], 16 * TT)
            pool.wait_ge(s["meta_ready"], 3)
            pool.wait_ge(s["late_in"], 48)
            T = pool.value_load(meta[0:1, META_T:META_T + 1], min_val=LEAST_BLOCKS, max_val=BLOCKS)

            def wait_counted(name, value):
                pool.wait_ge(s[name], value)
                pool.sem_inc(s["pool_waited"], 1)

            def prepare(b, first):
                expert = pool.value_load(meta[0:1, bass.ts(b, 1)], min_val=0, max_val=E - 1)
                if not first:
                    wait_counted("rows_in", b * 16)
                    wait_counted("idx_kept", b)
                pool.dma_start(idx_next[0:CAP, :], slot_dram[bass.ds(b * CAP, CAP), :]).then_inc(s["idx_in"], 16)
                wait_counted("idx_in", b * 16 + 16)
                if not first:
                    wait_counted("xt_ready", b)
                pool.indirect_dma_start(xg[0:CAP, :], None, hn_dram,
                                        bass.IndirectOffsetOnAxis(ap=idx_next[0:CAP, 1:2], axis=0))\
                    .then_inc(s["rows_in"], 16)
                if not first:
                    wait_counted("evac_done", b * GU_CHUNKS)
                pool.tensor_copy(bias_cur[:, :], bgu[:, bass.ts(expert, 16)]).then_inc(s["bias_ready"], 1)

            def rows_out(b):
                wait_counted("y_copied", b * DN_CHUNKS + DN_CHUNKS)
                wait_counted("idx_kept", b + 1)
                pool.indirect_dma_start(y_dram, bass.IndirectOffsetOnAxis(ap=idx_row[0:CAP, :], axis=0),
                                        y_sb[0:CAP, :], None, bounds_check=TOPK * S - 1, oob_is_err=False)\
                    .then_inc(s["y_out"], 16)

            prepare(0, True)
            pool.tensor_copy(idx_row[0:CAP, :], idx_next[0:CAP, 0:1]).then_inc(s["idx_kept"], 1)
            with pool.Fori(0, BLOCKS) as b:
                with pool.If(b < T):
                    prepare(b + 1, False)
                    rows_out(b)
                    wait_counted("y_out", b * 16 + 16)
                    pool.tensor_copy(idx_row[0:CAP, :], idx_next[0:CAP, 0:1]).then_inc(s["idx_kept"], 1)

        @block.scalar
        def _(act):
            step = Steps(act, s["act_steps"])
            act.dma_start(par[:, :], a["par"]).then_inc(s["consts_in"], 16)
            act.dma_start(cst[:, :], a["cst"]).then_inc(s["consts_in"], 16)
            act.dma_start(invcnt, a["invcnt"].rearrange("p (i t) -> p i t", i=2)).then_inc(s["consts_in"], 16)
            act.dma_start(poolw[:, :, :], a["poolw"].rearrange("p (i t) -> p i t", i=2)).then_inc(s["consts_in"], 16)
            act.dma_start(rw[:, :, :], a["rw"].rearrange("p (k e) -> p k e", k=KT)).then_inc(s["consts_in"], 16)
            act.dma_start(rb[:, :], a["rb"].broadcast_to([P, E])).then_inc(s["consts_in"], 16)
            act.dma_start(eiota[:, :], a["eiota"].broadcast_to([P, E])).then_inc(s["consts_in"], 16)
            act.dma_start(pairs[:, :].bitcast(I32), a["pairs"]).then_inc(s["consts_in"], 16)
            act.dma_start(blockid[:, :], a["blockid"]).then_inc(s["consts_in"], 16)
            act.dma_start(hn, a["xtok"].rearrange("p (i d) -> p i d", i=TT)).then_inc(s["xtok_in"], 16)
            for r in range(2):
                act.dma_start(rowvec[:, r * D:(r + 1) * D], a["rows"][r:r + 1, :].broadcast_to([P, D]))\
                   .then_inc(s["ln1_rows_in"], 16)

            for j in range(17):
                dst = ppad[:, j - PL[0], POOL_PAD:PP] if j in PL else z[:, j, :]
                if j == PL[0]:
                    act.wait_ge(s["pads_ready"], 1)
                if j == 14:
                    for i in range(NC_T):
                        act.wait_ge(s["mean_ready"], i + 1)
                        act.activation(z[:, AG[i], :], z[:, AV[i], :], ACT.Square).then_inc(s["sq_ready"], 1)
                act.wait_ge(s["z_ready"], j + 1)
                act.activation(dst, bank[j % 4][:, :], ACT.Sigmoid if j in AG else ACT.Copy).then_inc(s["z_evac"], 1)

            act.wait_ge(s["var_ready"], 1)
            act.activation(rs_a, bank[5][:, :], ACT.Sqrt, bias=eps_ln, scale=1.0 / C_CONF).then_inc(s["std_ready"], 1)
            for i in range(NC_T):
                act.wait_ge(s["ln_a_ready"], i + 1)
                act.activation(z[:, AG[i], :], z[:, AV[i], :], ACT.Sigmoid).then_inc(s["sgl_ready"], 1)

            for i in range(2):
                act.wait_ge(s["pool_out_ready"], i + 1)
                act.activation(z[:, PL[i], :], bank[6 + i][:, :], ACT.Copy, scale=pcol("pool_scale", i))\
                   .then_inc(s["pool_ready"], 1)

            for i in range(TT):
                act.wait_ge(s["v1_ready"], i + 1)
                act.activation(rstd[:, i:i + 1], mva[:, i, 1:2], ACT.Sqrt, bias=eps_ln).then_inc(s["s1_ready"], 1)

            act.wait_ge(s["mix_ready"], 2 * TT)
            act.dma_start(pT, a["pT"].rearrange("p (k t) -> p k t", k=2)).then_inc(s["late_in"], 16)
            act.dma_start(bgu, a["bgu"]).then_inc(s["late_in"], 16)
            act.dma_start(bdn[0:E, :], a["bdn"]).then_inc(s["late_in"], 16)

            for k in range(0, KT, 2):
                act.wait_ge(s["hnT_ready"], k + 1)
                act.activation(hT[:, k, :], bank[k][:, :], ACT.Identity, bias=pcol("ln1_b", k), scale=pcol("ln1_g", k))\
                   .then_inc(s["hT_done_a"], 1)

            act.wait_ge(s["e_ready"], 1)
            act.activation(gate[:, :, :], gate[:, :, :], ACT.Exp).then_inc(s["ex_ready"], 1)

            def ple_gate(g):
                act.wait_ge(s["pleg_ready"], g + 1)
                if g >= 2:
                    act.wait_ge(s["ple_evac"], g - 1)
                act.activation(sgate[:, g % 2, :], bank[1 + g % 2][:, :], ACT.Sigmoid).then_inc(s["sg_ready"], 1)

            for g in range(2 * TT):
                ple_gate(g)
                if g == 4:
                    act.wait_ge(s["gT_ready"], 1)
                    act.activation(GT[0:E, :], bank[6][0:E, :], ACT.Copy).then_inc(s["GT_ready"], 1)

            act.wait_ge(s["meta_ready"], 3)
            T = act.value_load(meta[0:1, META_T:META_T + 1], min_val=LEAST_BLOCKS, max_val=BLOCKS)

            def gathered(b):
                act.wait_ge(s["xt_ready"], b + 1)
                for k in range(KT):
                    ins = act.activation(xTb[:, k, :], bank[4 + k // 4][:, (k % 4) * CAP:(k % 4 + 1) * CAP],
                                         ACT.Identity, bias=pcol("ln1_b", k), scale=pcol("ln1_g", k))
                ins.then_inc(s["xT_done"], 1)

            def block_act(b, first):
                for c in range(GU_CHUNKS):
                    act.wait_ge(s["gate_ready"], b * GU_CHUNKS + (c + 1))
                    act.activation(sig_sb[:, c % 2, :, :], gu_sb[:, c % 2, 0:2, :], ACT.Sigmoid, scale=SW_ALPHA)\
                       .then_inc(s["sig_done"], 1)
                gathered(b + 1)
                if not first:
                    act.wait_ge(s["y_out"], b * 16)
                for n in range(DN_CHUNKS):
                    act.wait_ge(s["down_ready"], b * DN_CHUNKS + (n + 1))
                    act.activation(y_sb[0:CAP, n * 512:(n + 1) * 512], bank[6 + n][0:CAP, :], ACT.Copy)\
                       .then_inc(s["y_copied"], 1)

            gathered(0)
            block_act(0, True)
            with act.Fori(1, BLOCKS) as b:
                with act.If(b < T):
                    block_act(b, False)

            act.wait_ge(s["bias_ready"], T + 1)
            for i in range(TT):
                act.wait_ge(s["v2_ready"], i + 1)
                act.activation(rstd[:, i:i + 1], mva[:, i, 1:2], ACT.Sqrt, bias=eps_ln).then_inc(s["s2_ready"], 1)
                act.wait_ge(s["x2_ready"], 2 * i + 2)
                act.activation(un[:, i, :], h2[:, i, :], ACT.Square, accum_out=rstd[:, 4 + i:5 + i]).then_inc(s["ss_ready"], 1)
                act.wait_ge(s["ss_ready"], 2 * i + 1)
                act.activation(rstd[:, 4 + i:5 + i], rstd[:, 4 + i:5 + i], ACT.Sqrt, bias=eps_rms, scale=1.0 / D)\
                   .then_inc(s["ss_ready"], 1)
            for k in range(0, KT, 2):
                act.wait_ge(s["unT_ready"], k + 1)
                act.activation(uT[:, k, :], bank[k][:, :], ACT.Copy, scale=pcol("norm1", k)).then_inc(s["uT_done_a"], 1)

            act.wait_ge(s["lb_ready"], 1)
            act.activation(small[:, 0:2 * HG_HEADS], small[:, 0:2 * HG_HEADS], ACT.Exp).then_inc(s["lbe_ready"], 1)

            for j in range(20):
                act.wait_ge(s["p_ready"], j + 1)
                if j < 4:
                    act.activation(hQ[:, j * S:(j + 1) * S], bank[j % 2][:, :], ACT.Sigmoid).then_inc(s["hsig_ready"], 1)
                elif j < 8:
                    act.activation(hF[:, (j - 4) * S:(j - 3) * S], bank[j % 2][:, :], ACT.Sigmoid).then_inc(s["hsig_ready"], 1)
                elif j < 12:
                    act.activation(hG[:, j - 8, :], bank[j % 2][:, :], ACT.Sigmoid).then_inc(s["hsig_ready"], 1)
                else:
                    m = j - 12
                    if m >= 2:
                        act.wait_ge(s["rot_done"], m - 1)
                    act.activation(raw[:, m % 2, :], bank[j % 2][:, :], ACT.Copy).then_inc(s["p_evac"], 1)
                    act.wait_ge(s["p_evac"], m + 1)
                    for q in range(4):
                        act.dma_start(swp[q * 32:(q + 1) * 32, m % 2, :], raw[(q ^ 1) * 32:(q ^ 1) * 32 + 32, m % 2, :])\
                           .then_inc(swap_in[m % 2], 16)
            for g in range(8):
                act.wait_ge(s["vt_ready"], g + 1)
                if g < 4:
                    dst = v_tok[:, g, :]
                else:
                    dst = i_tok[:, g - 4, :]
                if g == 0:
                    act.wait_ge(s["lv_ready"], LEVELS + 1)
                act.activation(dst, bank[g % 2][:, :], ACT.Copy).then_inc(s["vt_evac"], 1)

            for h in range(HG_HEADS):
                act.wait_ge(s["o_ready"], h + 1)
                if h >= 2:
                    act.wait_ge(s["hmix_ready"], h - 1)
                act.activation(o_sb[:, h % 2, :], bank[2 + h % 2][:, :], ACT.Copy).then_inc(s["o_evac"], 1)
                act.activation(osq[:, h % 2, :], bank[2 + h % 2][:, :], ACT.Square).then_inc(s["osq_ready"], 1)
                act.wait_ge(s["oms_ready"], h + 1)
                act.activation(osq[:, h % 2, :], bank[4 + h % 2][:, :], ACT.Sqrt, bias=eps_rms, scale=1.0 / P)\
                   .then_inc(s["ostd_ready"], 1)

            def probs_out(h):
                act.wait_ge(s["pt_ready"], TT * (h + 1))
                if h >= 1:
                    act.wait_ge(s["pv_ready"], h)
                for j in range(TT):
                    ins = act.activation(pTa[:, j, j * P:S], bank[2 + j][:, j * P:S], ACT.Copy)
                ins.then_inc(s["pt_evac"], 1)

            def head_out(h):
                act.wait_ge(s["pv_ready"], h + 1)
                lo = (h % 2) * DH
                act.activation(mixed[lo:lo + DH, h // 2, :], bank[6 + h % 2][lo:lo + DH, :], ACT.Copy)\
                   .then_inc(s["pv_evac"], 1)

            for u in range(HEADS * TT):
                h, i = divmod(u, TT)
                act.wait_ge(s["sc_done"], u + 1)
                if u >= 2:
                    act.wait_ge(s["pt_ready"], u - 1)
                w = (i + 1) * P
                act.activation(ex[:, u % 2, 0:w], sc[:, u % 2, 0:w], ACT.Exp, bias=att_s[:, 4 + u % 2:5 + u % 2],
                               scale=SCALE).then_inc(s["e2_ready"], 1)
                if i == 0 and h >= 1:
                    probs_out(h - 1)
                if i == 1 and h >= 1:
                    head_out(h - 1)
            probs_out(HEADS - 1)
            head_out(HEADS - 1)

            for i in range(TT):
                act.wait_ge(s["h3_ready"], 2 * i + 2)
                act.activation(un2[:, i, :], h2[:, i, :], ACT.Square, accum_out=rstd[:, i:i + 1]).then_inc(s["ss3_ready"], 1)
                act.wait_ge(s["ss3_ready"], 2 * i + 1)
                act.activation(rstd[:, i:i + 1], rstd[:, i:i + 1], ACT.Sqrt, bias=eps_rms, scale=1.0 / D)\
                   .then_inc(s["ss3_ready"], 1)
            for k in range(0, KT, 2):
                act.wait_ge(s["unT3_ready"], k + 1)
                act.activation(u2T[:, k, :], bank[k][:, :], ACT.Copy, scale=pcol("norm2", k)).then_inc(s["u2T_done_a"], 1)

            for f in range(FFN_T):
                act.wait_ge(s["f_ready"], 2 * f + 1)
                if f >= 2:
                    act.wait_ge(s["f_evac"], f - 1)
                act.activation(fsig[:, f % 2, :], bank[2 * (f % 2)][:, :], ACT.Sigmoid).then_inc(s["fs_ready"], 1)

            for i in range(TT):
                act.wait_ge(s["h4_ready"], 2 * i + 2)
                act.activation(outt[:, i, :], h2[:, i, :], ACT.Square, accum_out=rstd[:, 4 + i:5 + i])\
                   .then_inc(s["ss4_ready"], 1)
                act.wait_ge(s["ss4_ready"], 2 * i + 1)
                act.activation(rstd[:, 4 + i:5 + i], rstd[:, 4 + i:5 + i], ACT.Sqrt, bias=eps_rms, scale=1.0 / D)\
                   .then_inc(s["ss4_ready"], 1)

        @block.tensor
        def _(pe):
            def accumulate(out, pairs):
                n = len(pairs)
                for k, (lhsT, rhs) in enumerate(pairs):
                    ins = pe.matmul(out, lhsT, rhs, start=(k == 0), stop=(k == n - 1))
                return ins

            pe.wait_ge(s["xT_in"], 16 * KT)

            def z_tile(j):
                w = chunk(pe, j // 4)
                n = 4 if j < 16 else 1
                w = w[:, 0:KT * n * P].rearrange("p (k c) -> p k c", k=KT)
                if j >= 4:
                    pe.wait_ge(s["z_evac"], j - 3)
                c = (j % 4) * P if j < 16 else 0
                accumulate(bank[j % 4][:, :], [(w[:, k, c:c + P], xT[:, k, :]) for k in range(KT)])\
                    .then_inc(s["z_ready"], 1)

            for j in range(17):
                z_tile(j)
                if j == 0:
                    pe.wait_ge(s["consts_in"], 16 * 9)
                if j == 12:
                    pe.wait_ge(s["conv_ready"], NC_T)
                    accumulate(bank[4][:, :], [(ones, z[:, t, :]) for t in AV]).then_inc(s["asum_ready"], 1)
                if j == 14:
                    pe.wait_ge(s["sq_ready"], NC_T)
                    accumulate(bank[5][:, :], [(ones, z[:, t, :]) for t in AG]).then_inc(s["var_ready"], 1)
            for i in range(2):
                pe.wait_ge(s["pool_in_ready"], i + 1)
                accumulate(bank[6 + i][:, :], [(poolw[:, i, :], z[:, PL[i], :])]).then_inc(s["pool_out_ready"], 1)

            pe.wait_ge(s["z_evac"], 17)
            pe.wait_ge(s["mixT_ready"], NC_T)
            pe.wait_ge(s["pool_ready"], 2)
            for g in range(2 * TT):
                i, n = divmod(g, 2)
                w = chunk(pe, 5 + n).rearrange("p (k c) -> p k c", k=KT)
                if g >= 4:
                    pe.wait_ge(s["mix_evac"], g - 3)
                accumulate(bank[g % 4][:, :], [(mixT[k][:, i * P:(i + 1) * P], w[:, k, :]) for k in range(KT)])\
                    .then_inc(s["mix_ready"], 1)

            pe.wait_ge(s["mix_evac"], 2 * TT)
            for i in range(TT):
                pe.wait_ge(s["hn_ready"], i + 1)
                for k in range(KT):
                    ins = pe.transpose(bank[k][:, i * P:(i + 1) * P], hn[:, i, k * P:(k + 1) * P], ident)
                    if i == TT - 1:
                        ins.then_inc(s["hnT_ready"], 1)

            pe.wait_ge(s["hT_done_a"], KT // 2)
            pe.wait_ge(s["hT_done_v"], KT // 2)
            for i in range(TT):
                ins = accumulate(bank[0][:, i * E:(i + 1) * E],
                                 [(hT[:, k, i * P:(i + 1) * P], rw[:, k, :]) for k in range(KT)])
            ins.then_inc(s["router_ready"], 1)

            def ple(g):
                i, n = divmod(g, 2)
                w = chunk(pe, 7 + n).rearrange("p (k c) -> p k c", k=KT)
                if g >= 2:
                    pe.wait_ge(s["ple_evac"], g - 1)
                accumulate(bank[1 + g % 2][:, :], [(hT[:, k, i * P:(i + 1) * P], w[:, k, :]) for k in range(KT)])\
                    .then_inc(s["pleg_ready"], 1)
                w = chunk(pe, 9)[:, 0:2 * D].rearrange("p (k c) -> p k c", k=2)
                if g == 0:
                    pe.wait_ge(s["late_in"], 48)
                accumulate(bank[3 + g % 2][:, :],
                           [(pT[:, k, i * P:(i + 1) * P], w[:, k, n * 512:(n + 1) * 512]) for k in range(2)])\
                    .then_inc(s["plep_ready"], 1)

            ple(0)
            ple(1)
            pe.wait_ge(s["mask_ready"], 1)
            for i in range(TT):
                accumulate(bank[5][:, i * E:(i + 1) * E],
                           [(ones, mask[:, j, :]) for j in range(i)] + [(before, mask[:, i, :])])
            accumulate(bank[5][:, TT * E:(TT + 1) * E], [(ones, mask[:, j, :]) for j in range(TT)])\
                .then_inc(s["pos_ready"], 1)
            ple(2)
            ple(3)
            pe.wait_ge(s["gm_ready"], 1)
            for i in range(TT):
                ins = pe.transpose(bank[6][0:E, i * P:(i + 1) * P], gmat[:, i, :], ident)
            ins.then_inc(s["gT_ready"], 1)
            for g in range(4, 2 * TT):
                ple(g)
            pe.wait_ge(s["GT_ready"], 1)
            for g in range(2 * TT):
                i, n = divmod(g, 2)
                if g >= 2:
                    pe.wait_ge(s["bdn_done"], g - 1)
                accumulate(bank[7 * (g % 2)][:, :], [(GT[0:E, i * P:(i + 1) * P], bdn[0:E, n * 512:(n + 1) * 512])])\
                    .then_inc(s["bdn_ready"], 1)

            pe.wait_ge(s["meta_ready"], 3)
            T = pe.value_load(meta[0:1, META_T:META_T + 1], min_val=LEAST_BLOCKS, max_val=BLOCKS)
            pe.wait_ge(s["ple_evac"], 2 * TT)
            pe.wait_ge(s["bdn_done"], 2 * TT)

            def gathered(b):
                pe.wait_ge(s["rows_in"], b * 16 + 16)
                for k in range(KT):
                    ins = pe.transpose(bank[4 + k // 4][:, (k % 4) * CAP:(k % 4 + 1) * CAP],
                                       xg[0:CAP, k * P:(k + 1) * P], ident[0:CAP, 0:CAP])
                ins.then_inc(s["xt_ready"], 1)

            def block_pe(b, first):
                pe.wait_ge(s["xT_done"], b + 1)
                for c in range(GU_CHUNKS):
                    pe.wait_ge(moe_in[c], b * 16 + 16)
                    if not first:
                        pe.wait_ge(s["evac_done"], (b - 1) * GU_CHUNKS + (c + 1))
                    w = slot(c).rearrange("p (k c) -> p k c", k=KT)
                    for n in range(4):
                        ins = accumulate(bank[c][:, n * CAP:(n + 1) * CAP],
                                         [(w[:, k, n * P:(n + 1) * P], xTb[:, k, :]) for k in range(KT)])
                    ins.then_inc(s["gu_ready"], 1)
                gathered(b + 1)
                pe.wait_ge(s["act_ready"], b * GU_CHUNKS + GU_CHUNKS)
                for n in range(DN_CHUNKS):
                    pe.wait_ge(moe_in[GU_CHUNKS + n], b * 16 + 16)
                    if not first:
                        pe.wait_ge(s["y_copied"], (b - 1) * DN_CHUNKS + (n + 1))
                    w = slot(GU_CHUNKS + n).rearrange("p (k c) -> p k c", k=KT)
                    accumulate(bank[6 + n][0:CAP, :], [(actT[:, k, :], w[:, k, :]) for k in range(KT)])\
                        .then_inc(s["down_ready"], 1)

            gathered(0)
            block_pe(0, True)
            with pe.Fori(1, BLOCKS) as b:
                with pe.If(b < T):
                    block_pe(b, False)

            pe.wait_ge(s["xT_done"], T + 1)
            pe.wait_ge(s["evac_done"], T * GU_CHUNKS)
            pe.wait_ge(s["y_copied"], T * DN_CHUNKS)
            for i in range(TT):
                pe.wait_ge(s["un_ready"], i + 1)
                for k in range(KT):
                    ins = pe.transpose(bank[k][:, i * P:(i + 1) * P], un[:, i, k * P:(k + 1) * P], ident)
                    if i == TT - 1:
                        ins.then_inc(s["unT_ready"], 1)
            pe.wait_ge(s["uT_done_a"], KT // 2)
            pe.wait_ge(s["uT_done_v"], KT // 2)

            def p_tile(j):
                w = chunk2(pe, j // 4).rearrange("p (k c) -> p k c", k=KT)
                if 2 <= j < 6:
                    pe.wait_ge(s["p_evac_v"], j - 1)
                elif 6 <= j < 10:
                    pe.wait_ge(s["hsig_ready"], j - 1)
                elif 10 <= j < 14:
                    pe.wait_ge(s["p_evac_v"], j - 5)
                elif j >= 14:
                    pe.wait_ge(s["p_evac"], j - 13)
                c = (j % 4) * P
                accumulate(bank[j % 2][:, :], [(w[:, k, c:c + P], uT[:, k, :]) for k in range(KT)])\
                    .then_inc(s["p_ready"], 1)

            def level(n):
                if n == 0:
                    pe.wait_ge(s["fK_ready"], 1)
                else:
                    pe.wait_ge(s["lv_upd"], n)
                    pe.wait_ge(s["lv_copied"], n)
                for h in range(HG_HEADS):
                    q0 = h * S
                    if n <= TILE_LEVELS:
                        for j in range(TT):
                            at = q0 + j * P
                            ins = pe.matmul(bank[2 + h][:, j * P:(j + 1) * P], hK[:, at:at + P], hQ[:, at:at + P],
                                            start=True, stop=True)
                    elif n == TILE_LEVELS + 1:
                        for j in range(2):
                            at = q0 + 2 * j * P
                            ins = pe.matmul(bank[2 + h][:, j * P:(j + 1) * P], hK[:, at:at + P],
                                            hQ[:, at + P:at + 2 * P], start=True, stop=True)
                    else:
                        for j in range(2):
                            ins = pe.matmul(bank[2 + h][:, 2 * j * P:2 * (j + 1) * P],
                                            hK[:, q0 + j * P:q0 + (j + 1) * P], hQ[:, q0 + 2 * P:q0 + 4 * P],
                                            start=True, stop=True)
                ins.then_inc(s["lv_ready"], 1)

            for j in range(8):
                p_tile(j)
            for n in range(LEVELS + 1):
                level(n)
                p_tile(8 + n)
            p_tile(18)
            p_tile(19)
            for g in range(8):
                w = chunk2(pe, 5 + g // 4).rearrange("p (k c) -> p k c", k=KT)
                if g < 2:
                    pe.wait_ge(s["p_evac"], 7 + g)
                else:
                    pe.wait_ge(s["vt_evac"], g - 1)
                i = g % 4
                accumulate(bank[g % 2][:, :], [(uT[:, k, i * P:(i + 1) * P], w[:, k, :]) for k in range(KT)])\
                    .then_inc(s["vt_ready"], 1)

            pe.wait_ge(s["lv_copied"], LEVELS + 1)
            pe.wait_ge(s["vt_evac"], 8)

            def hgrn_out(h):
                if h >= 2:
                    pe.wait_ge(s["osq_ready"], h - 1)
                for j in range(TT):
                    ins = pe.matmul(bank[2 + h % 2][:, j * P:S], i_tok[:, j, h * P:(h + 1) * P], AT[:, h, j, j * P:S],
                                    start=(j == 0), stop=(j == TT - 1), skip_group_check=True)
                ins.then_inc(s["o_ready"], 1)

            def hgrn_ms(h):
                pe.wait_ge(s["osq_ready"], h + 1)
                if h >= 2:
                    pe.wait_ge(s["ostd_ready"], h - 1)
                accumulate(bank[4 + h % 2][:, :], [(ones, osq[:, h % 2, :])]).then_inc(s["oms_ready"], 1)

            hgrn_out(0)
            for h in range(HG_HEADS):
                if h + 1 < HG_HEADS:
                    hgrn_out(h + 1)
                hgrn_ms(h)

            pe.wait_ge(s["rot_done"], 8)
            pe.wait_ge(s["ostd_ready"], HG_HEADS)

            def scores(u):
                h, i = divmod(u, TT)
                lo = (h % 2) * DH
                m = h // 2
                if u >= 2:
                    pe.wait_ge(s["sc_done"], u - 1)
                pe.matmul(bank[u % 2][:, 0:(i + 1) * P], qkT[lo:lo + DH, m, i * P:(i + 1) * P],
                          qkT[lo:lo + DH, 4 + m, 0:(i + 1) * P], start=True, stop=True).then_inc(s["sc_ready"], 1)

            def probs_T(u):
                h, i = divmod(u, TT)
                pe.wait_ge(s["pn_ready"], u + 1)
                if i == 0 and h >= 1:
                    pe.wait_ge(s["pt_evac"], h)
                for j in range(i + 1):
                    ins = pe.transpose(bank[2 + j][:, i * P:(i + 1) * P], ex[:, u % 2, j * P:(j + 1) * P], ident)
                ins.then_inc(s["pt_ready"], 1)

            def head_values(h):
                lo = (h % 2) * DH
                pe.wait_ge(s["pt_evac"], h + 1)
                if h >= 2:
                    pe.wait_ge(s["pv_evac"], h - 1)
                for j in range(TT):
                    ins = pe.matmul(bank[6 + h % 2][lo:lo + DH, j * P:S], v_tok[:, j, h * DH:(h + 1) * DH],
                                    pTa[:, j, j * P:S], start=(j == 0), stop=(j == TT - 1), skip_group_check=True)
                ins.then_inc(s["pv_ready"], 1)

            scores(0)
            scores(1)
            for u in range(HEADS * TT):
                probs_T(u)
                if u + 2 < HEADS * TT:
                    scores(u + 2)
                if u % TT == TT - 1:
                    head_values(u // TT)

            pe.wait_ge(s["pv_evac"], HEADS)
            pe.wait_ge(s["hmix_ready"], HG_HEADS)
            pe.wait_ge(s["sc_done"], HEADS * TT)
            for g in range(2 * TT):
                i, n = divmod(g, 2)
                w = chunk2(pe, 7 + n).rearrange("p (k c) -> p k c", k=KT)
                if g >= 4:
                    pe.wait_ge(s["h3_ready"], g - 3)
                accumulate(bank[g % 4][:, :], [(mixed[:, k, i * P:(i + 1) * P], w[:, k, :]) for k in range(KT)])\
                    .then_inc(s["o2_ready"], 1)

            pe.wait_ge(s["h3_ready"], 2 * TT)
            for i in range(TT):
                pe.wait_ge(s["un3_ready"], i + 1)
                for k in range(KT):
                    ins = pe.transpose(bank[k][:, i * P:(i + 1) * P], un2[:, i, k * P:(k + 1) * P], ident)
                    if i == TT - 1:
                        ins.then_inc(s["unT3_ready"], 1)
            pe.wait_ge(s["u2T_done_a"], KT // 2)
            pe.wait_ge(s["u2T_done_v"], KT // 2)
            for f in range(FFN_T):
                w = chunk2(pe, 9 + f // 2).rearrange("p (k c) -> p k c", k=KT)
                if f >= 2:
                    pe.wait_ge(s["f_evac"], f - 1)
                for n in range(2):
                    c = (2 * n + f % 2) * P
                    accumulate(bank[2 * (f % 2) + n][:, :], [(w[:, k, c:c + P], u2T[:, k, :]) for k in range(KT)])\
                        .then_inc(s["f_ready"], 1)
            pe.wait_ge(s["f_evac"], FFN_T)
            for c in range(6):
                rows = 4 if c < 5 else FFN_T - 20
                w = chunk2(pe, 20 + c)[:, 0:rows * D].rearrange("p (k c) -> p k c", k=rows)
                for r in range(rows):
                    k = 4 * c + r
                    for i in range(TT):
                        for n in range(2):
                            ins = pe.matmul(bank[2 * i + n][:, :], fact[:, k, i * P:(i + 1) * P],
                                            w[:, r, n * 512:(n + 1) * 512], start=(k == 0), stop=(k == FFN_T - 1))
                ins.then_inc(s["fd_used"], 1)

        @block.vector
        def _(dve):
            step = Steps(dve, s["dve_steps"])

            def shifted_sum(out, buf, lo, shift, hi=P):
                return dve.tensor_tensor(out[lo:hi], buf[lo:hi, POOL_PAD:PP], buf[lo:hi, POOL_PAD - shift:PP - shift],
                                         ALU.add)

            dve.wait_ge(s["consts_in"], 16 * 9)
            dve.wait_ge(s["pads_ready"], 1)
            for i in range(NC_T):
                dve.wait_ge(s["z_evac"], 2 * i + 2)
                step(dve.tensor_tensor(upad[:, i, CONV_A - 1:CONV_A - 1 + S], z[:, AV[i], :], z[:, AG[i], :], ALU.mult))
                o = z[:, AV[i], :]
                for k in range(CONV_A):
                    w = pcol("conv_a_w", i * CONV_A + k)
                    if k == 0:
                        step(dve.tensor_scalar(o, upad[:, i, 0:S], w, None, ALU.mult))
                    else:
                        step(dve.scalar_tensor_tensor(o, upad[:, i, k:k + S], w, o, ALU.mult, ALU.add))
                dve.tensor_scalar(o, o, pcol("conv_a_b", i), None, ALU.add).then_inc(s["conv_ready"], 1)

            def short(i):
                dve.wait_ge(s["z_evac"], 8 + 2 * i)
                step(dve.tensor_tensor(cpad[:, i, CONV_B - 1:CONV_B - 1 + S], z[:, CG[i], :], z[:, BV[i], :], ALU.mult))
                o = z[:, CG[i], :]
                for k in range(CONV_B):
                    w = pcol("conv_b_w", i * CONV_B + k)
                    if k == 0:
                        step(dve.tensor_scalar(o, cpad[:, i, 0:S], w, None, ALU.mult))
                    else:
                        step(dve.scalar_tensor_tensor(o, cpad[:, i, k:k + S], w, o, ALU.mult, ALU.add))

            for i in range(NC_T):
                short(i)
            dve.wait_ge(s["asum_ready"], 1)
            step(dve.tensor_scalar(mu_a, bank[4][:, :], 1.0 / C_CONF, None, ALU.mult))
            for i in range(NC_T):
                dve.tensor_tensor(z[:, AV[i], :], z[:, AV[i], :], mu_a, ALU.subtract).then_inc(s["mean_ready"], 1)
            dve.wait_ge(s["std_ready"], 1)
            step(dve.reciprocal(rs_a, rs_a))
            for i in range(NC_T):
                step(dve.tensor_tensor(z[:, AV[i], :], z[:, AV[i], :], rs_a, ALU.mult))
                dve.tensor_scalar(z[:, AV[i], :], z[:, AV[i], :], pcol("ln_a_g", i), pcol("ln_a_b", i), ALU.mult, ALU.add)\
                   .then_inc(s["ln_a_ready"], 1)
            for i in range(NC_T):
                dve.wait_ge(s["z_evac"], BG[i] + 1)
                step.mark(dve.tensor_tensor(z[:, BG[i], :], z[:, BG[i], :], z[:, CG[i], :], ALU.mult))

            for i in range(2):
                win, src, dst = pwin[:, i, :], ppad[:, i, :], z[:, PL[i], :]
                dve.wait_ge(s["z_evac"], PL[i] + 1)
                step(shifted_sum(win[:, POOL_PAD:PP], src, 0, 1))
                if i == 1:
                    four = upad[:, 0, :]
                    step(shifted_sum(four[:, POOL_PAD:PP], win, 0, 2))
                    step(shifted_sum(win[:, POOL_PAD:PP], four, 0, 4))
                step(shifted_sum(dst, win, P // 2, 2 if i == 0 else 8))
                step.mark(dve.tensor_tensor(dst[0:P // 2], win[0:P // 2, POOL_PAD:PP], invcnt[0:P // 2, i, :], ALU.mult))
                step(dve.tensor_tensor(dst[P // 2:P], dst[P // 2:P], invcnt[P // 2:P, i, :], ALU.mult))
                dve.tensor_tensor(dst, dst, src[:, POOL_PAD:PP], ALU.subtract).then_inc(s["pool_in_ready"], 1)
            for i in range(NC_T):
                dve.wait_ge(s["sgl_ready"], i + 1)
                dve.tensor_tensor(z[:, AV[i], :], z[:, AV[i], :], z[:, AG[i], :], ALU.mult).then_inc(s["mixT_ready"], 1)

            dve.wait_ge(s["xtok_in"], 16)

            def row_stats(i, src, ready):
                for q in range(2):
                    step.mark(dve.bn_stats(stats[:, q, :], src[:, q * 512:(q + 1) * 512]))
                step.wait()
                dve.bn_aggr(mva[:, i, :], stats[:, :, :].rearrange("p a b -> p (a b)")).then_inc(ready, 1)

            for i in range(TT):
                for n in range(2):
                    g = 2 * i + n
                    dve.wait_ge(s["mix_ready"], g + 1)
                    part = hn[:, i, n * 512:(n + 1) * 512]
                    dve.scalar_tensor_tensor(part, part, ALPHA, bank[g % 4][:, :], ALU.mult, ALU.add)\
                       .then_inc(s["mix_evac"], 1)
                dve.wait_ge(s["mix_evac"], 2 * i + 2)
                row_stats(i, hn[:, i, :], s["v1_ready"])
                dve.wait_ge(s["s1_ready"], i + 1)
                step(dve.reciprocal(rstd[:, i:i + 1], rstd[:, i:i + 1]))
                dve.tensor_scalar(hn[:, i, :], hn[:, i, :], mva[:, i, 0:1], rstd[:, i:i + 1], ALU.subtract, ALU.mult)\
                   .then_inc(s["hn_ready"], 1)
            for k in range(1, KT, 2):
                dve.wait_ge(s["hnT_ready"], k + 1)
                dve.tensor_scalar(hT[:, k, :], bank[k][:, :], pcol("ln1_g", k), pcol("ln1_b", k), ALU.mult, ALU.add)\
                   .then_inc(s["hT_done_v"], 1)

            dve.wait_ge(s["router_ready"], 1)
            step(dve.tensor_tensor(logit, bank[0][:, 0:TT * E].rearrange("p (i e) -> p i e", i=TT),
                                   rb[:, :].unsqueeze(1).broadcast_to([P, TT, E]), ALU.add))
            for i in range(TT):
                step(dve.max(mv8[:, i, :], logit[:, i, :]))
                step(dve.max_index(mi8[:, i, :], mv8[:, i, :], logit[:, i, :]))
            step(dve.tensor_copy(mif[:, :, :], mi8[:, :, :]))
            step(dve.tensor_tensor(oh, eiota[:, :].unsqueeze(1).unsqueeze(1).broadcast_to([P, TT, TOPK, E]),
                                   mif[:, :, 0:TOPK].unsqueeze(3).broadcast_to([P, TT, TOPK, E]), ALU.is_equal))
            dve.tensor_reduce(mask, oh.rearrange("p i k e -> p i e k"), AX.X, ALU.add).then_inc(s["mask_ready"], 1)
            dve.tensor_tensor(gate[:, :, :], mv8[:, :, 0:TOPK], mv8[:, :, 0:1].broadcast_to([P, TT, TOPK]), ALU.subtract)\
               .then_inc(s["e_ready"], 1)
            dve.wait_ge(s["ex_ready"], 1)
            step(dve.tensor_reduce(gsum[:, :], gate[:, :, :], AX.X, ALU.add))
            step(dve.reciprocal(gsum[:, :], gsum[:, :]))
            step(dve.tensor_tensor(gate[:, :, :], gate[:, :, :], gsum[:, :].unsqueeze(2).broadcast_to([P, TT, TOPK]),
                                   ALU.mult))
            step(dve.tensor_tensor(ohw, oh, gate[:, :, :].unsqueeze(3).broadcast_to([P, TT, TOPK, E]), ALU.mult))
            dve.tensor_reduce(gmat, ohw.rearrange("p i k e -> p i e k"), AX.X, ALU.add).then_inc(s["gm_ready"], 1)

            dve.wait_ge(s["pos_ready"], 1)
            count, nblk, end, first_slot = (cnt[:, n, :] for n in range(4))
            step(dve.tensor_copy(count, bank[5][:, TT * E:(TT + 1) * E]))
            step(dve.tensor_scalar(nblk, count, 0.0, None, ALU.is_gt))
            for m in range(1, MAX_PER_EXPERT):
                step(dve.scalar_tensor_tensor(nblk, count, float(m * CAP), nblk, ALU.is_gt, ALU.add))
            step(dve.tensor_tensor_scan(end, ones[:, 0:E], nblk, 0.0, ALU.mult, ALU.add))
            step(dve.tensor_tensor(first_slot, end, nblk, ALU.subtract))
            step(dve.tensor_scalar(first_slot, first_slot, float(CAP), None, ALU.mult))
            step(dve.tensor_tensor(pos, bank[5][:, 0:TT * E].rearrange("p (i e) -> p i e", i=TT),
                                   first_slot.unsqueeze(1).broadcast_to([P, TT, E]), ALU.add))
            dve.wait_ge(s["gm_ready"], 1)
            step(dve.tensor_tensor(ohw, oh, pos.unsqueeze(2).broadcast_to([P, TT, TOPK, E]), ALU.mult))
            step(dve.tensor_reduce(destf[:, :].rearrange("p (i k) -> p i k", i=TT), ohw, AX.X, ALU.add))
            dve.tensor_copy(dest[:, :], destf[:, :]).then_inc(s["dest_ready"], 1)
            be = cmp_be[0:1, :].rearrange("p (b e) -> p b e", e=E)
            step(dve.tensor_tensor(be, end[0:1, :].unsqueeze(1).broadcast_to([1, NB_META, E]),
                                   blockid[0:1, 0:NB_META].unsqueeze(2).broadcast_to([1, NB_META, E]), ALU.is_le))
            step(dve.tensor_reduce(metaf[0:1, 0:NB_META], be, AX.X, ALU.add))
            step(dve.tensor_scalar(metaf[0:1, 0:NB_META], metaf[0:1, 0:NB_META], float(E - 1), None, ALU.min))
            dve.tensor_copy(meta[0:1, 0:NB_META], metaf[0:1, 0:NB_META]).then_inc(s["meta_ready"], 1)
            step(dve.tensor_scalar(metaf[0:1, META_LAST:META_LAST + 1], end[0:1, E - 1:E], -1.0, None, ALU.add))
            dve.tensor_copy(meta[0:1, META_LAST:META_LAST + 1], metaf[0:1, META_LAST:META_LAST + 1])\
               .then_inc(s["meta_ready"], 1)
            dve.tensor_copy(meta[0:1, META_T:META], end[0:1, E - 1:E]).then_inc(s["meta_ready"], 1)

            for g in range(2 * TT):
                i, n = divmod(g, 2)
                part = acc[:, i, n * 512:(n + 1) * 512]
                dve.wait_ge(s["sg_ready"], g + 1)
                dve.wait_ge(s["plep_ready"], g + 1)
                dve.tensor_tensor(plet, sgate[:, g % 2, :], bank[3 + g % 2][:, :], ALU.mult).then_inc(s["ple_evac"], 1)
                dve.wait_ge(s["ple_evac"], g + 1)
                dve.wait_ge(s["h_ready"], 2 * i + 2)
                step(dve.scalar_tensor_tensor(part, part, ALPHA, plet, ALU.mult, ALU.add))
            for g in range(2 * TT):
                i, n = divmod(g, 2)
                part = acc[:, i, n * 512:(n + 1) * 512]
                dve.wait_ge(s["bdn_ready"], g + 1)
                dve.tensor_tensor(part, part, bank[7 * (g % 2)][:, :], ALU.add).then_inc(s["bdn_done"], 1)

            dve.wait_ge(s["meta_ready"], 3)
            T = dve.value_load(meta[0:1, META_T:META_T + 1], min_val=LEAST_BLOCKS, max_val=BLOCKS)
            per_block = 2 * GU_CHUNKS

            def block_dve(b):
                own = Steps(dve, s["moe_dve"], b * per_block)
                dve.wait_ge(s["bias_ready"], b + 1)
                for c in range(GU_CHUNKS):
                    at = c % 2
                    dve.wait_ge(s["gu_ready"], b * GU_CHUNKS + (c + 1))
                    for n in range(4):
                        col = (n // 2) * KT + 2 * c + n % 2
                        ins = dve.tensor_scalar(gu_sb[:, at, n, :], bank[c][:, n * CAP:(n + 1) * CAP],
                                                bias_cur[:, col:col + 1], LIMIT, ALU.add, ALU.min)
                        if n == 1:
                            ins.then_inc(s["gate_ready"], 1)
                    ins.then_inc(s["evac_done"], 1)
                    dve.wait_ge(s["evac_done"], b * GU_CHUNKS + (c + 1))
                    own(dve.tensor_scalar(gu_sb[:, at, 2:4, :], gu_sb[:, at, 2:4, :], -LIMIT, 1.0, ALU.max, ALU.add))
                    own(dve.tensor_tensor(ug_sb[:, at, :, :], gu_sb[:, at, 2:4, :], gu_sb[:, at, 0:2, :], ALU.mult))
                    dve.wait_ge(s["sig_done"], b * GU_CHUNKS + (c + 1))
                    dve.tensor_tensor(actT[:, 2 * c:2 * c + 2, :], ug_sb[:, at, :, :], sig_sb[:, at, :, :], ALU.mult)\
                       .then_inc(s["act_ready"], 1)
                assert own.n == per_block

            block_dve(0)
            with dve.Fori(1, BLOCKS) as b:
                with dve.If(b < T):
                    block_dve(b)

            for c in range(TT * TOPK):
                i, k = divmod(c, TOPK)
                dve.wait_ge(yk_in[i], 16)
                if c > 0:
                    dve.wait_ge(s["yg_used"], c)
                dve.scalar_tensor_tensor(acc[:, i, :], yk[i][:, k, :], gate[:, i, k:k + 1], acc[:, i, :], ALU.mult, ALU.add)\
                   .then_inc(s["yg_used"], 1)

            for i in range(TT):
                dve.wait_ge(s["yg_used"], TOPK * (i + 1))
                row_stats(i, acc[:, i, :], s["v2_ready"])
                if i == 0:
                    dve.wait_ge(s["ln2_rows_in"], 32)
                dve.wait_ge(s["v2_ready"], i + 1)
                dve.scalar_tensor_tensor(acc[:, i, :], acc[:, i, :], mva[:, i, 0:1], rowvec[:, 0:D], ALU.subtract, ALU.mult)\
                   .then_inc(s["x2_ready"], 1)
                dve.wait_ge(s["s2_ready"], i + 1)
                step(dve.reciprocal(rstd[:, i:i + 1], rstd[:, i:i + 1]))
                dve.wait_ge(s["x2_ready"], 2 * i + 1)
                dve.scalar_tensor_tensor(h2[:, i, :], acc[:, i, :], rstd[:, i:i + 1], rowvec[:, D:2 * D], ALU.mult, ALU.add)\
                   .then_inc(s["x2_ready"], 1)
                dve.wait_ge(s["ss_ready"], 2 * i + 2)
                step(dve.reciprocal(rstd[:, 4 + i:5 + i], rstd[:, 4 + i:5 + i]))
                dve.tensor_scalar(un[:, i, :], h2[:, i, :], rstd[:, 4 + i:5 + i], None, ALU.mult).then_inc(s["un_ready"], 1)
            for k in range(1, KT, 2):
                dve.wait_ge(s["unT_ready"], k + 1)
                dve.tensor_scalar(uT[:, k, :], bank[k][:, :], pcol("norm1", k), None, ALU.mult).then_inc(s["uT_done_v"], 1)

            H4 = HG_HEADS
            l0, l1 = par[:, PAR["lb"]:PAR["lb"] + H4], par[:, PAR["lb"] + H4:PAR["lb"] + 2 * H4]
            e0, e1, top, lb, lb1 = (small[:, n * H4:(n + 1) * H4] for n in range(5))
            step(dve.tensor_tensor(top, l0, l1, ALU.max))
            step(dve.tensor_tensor(e0, l0, top, ALU.subtract))
            dve.tensor_tensor(e1, l1, top, ALU.subtract).then_inc(s["lb_ready"], 1)
            dve.wait_ge(s["lbe_ready"], 1)
            step(dve.tensor_tensor(top, e0, e1, ALU.add))
            step(dve.reciprocal(top, top))
            step(dve.tensor_tensor(lb, e0, top, ALU.mult))
            step(dve.tensor_tensor(lb1, e1, top, ALU.mult))

            for j in range(4):
                part = hQ[:, j * S:(j + 1) * S]
                dve.wait_ge(s["hsig_ready"], j + 1)
                dve.tensor_tensor(part, part, bank[j % 2][:, :], ALU.mult).then_inc(s["p_evac_v"], 1)
            step.mark(dve.memset(AT, 0.0))
            for j in range(4):
                part = hF[:, j * S:(j + 1) * S]
                dve.wait_ge(s["hsig_ready"], 5 + j)
                step(dve.tensor_scalar(part, part, lb1[:, j:j + 1], lb[:, j:j + 1], ALU.mult, ALU.add))
                ins = dve.tensor_scalar(hK[:, j * S:(j + 1) * S], part, -1.0, 1.0, ALU.mult, ALU.add)
            ins.then_inc(s["fK_ready"], 1)

            def rotate(m):
                dve.wait_ge(s["p_evac"], m + 1)
                if m == 0:
                    dve.wait_ge(s["c2_in"], 32)
                step.mark(dve.tensor_tensor(qkT[:, m, :], raw[:, m % 2, :], cosT, ALU.mult))
                dve.wait_ge(swap_in[m % 2], 64 * (m // 2 + 1))
                step(dve.tensor_tensor(swp[:, m % 2, :], swp[:, m % 2, :], sinT, ALU.mult))
                dve.tensor_tensor(qkT[:, m, :], qkT[:, m, :], swp[:, m % 2, :], ALU.add).then_inc(s["rot_done"], 1)

            for n in range(LEVELS + 1):
                dve.wait_ge(s["lv_ready"], n + 1)
                if n == 0:
                    dve.wait_ge(s["fK_ready"], 1)
                    dve.tensor_tensor(hQ, hQ, hF, ALU.mult).then_inc(s["lv_upd"], 1)
                    dve.wait_ge(s["c2_in"], 32)
                elif n < LEVELS:
                    L = 1 << (n - 1)
                    qv = hQ.rearrange("p (n a l) -> p n a l", a=2, l=L)
                    kv = hK.rearrange("p (n a l) -> p n a l", a=2, l=L)
                    tv = tot[n - 1].rearrange("p (n a) -> p n a", a=2)
                    N = HG_HEADS * S // (2 * L)
                    dve.wait_ge(s["lv_upd"], n)
                    step.mark(dve.tensor_tensor(tot[n], tv[:, :, 0], tv[:, :, 1], ALU.mult))
                    step.mark(dve.tensor_tensor(qv[:, :, 1, :], qv[:, :, 1, :],
                                                tv[:, :, 0:1].broadcast_to([P, N, L]), ALU.mult))
                    dve.tensor_tensor(kv[:, :, 0, :], kv[:, :, 0, :], tv[:, :, 1:2].broadcast_to([P, N, L]), ALU.mult)\
                       .then_inc(s["lv_upd"], 1)
                    step.wait()
                for h in range(HG_HEADS):
                    src = bank[2 + h]
                    if n <= TILE_LEVELS:
                        diag = AT[:, h, :, :].rearrange("p j t -> p (j t)")
                        for j in range(TT):
                            at = j * (S + P)
                            ins = dve.copy_predicated(diag[:, at:at + P], lmask[:, n, :], src[:, j * P:(j + 1) * P])
                    elif n == TILE_LEVELS + 1:
                        for j in range(2):
                            ins = dve.tensor_copy(AT[:, h, 2 * j, (2 * j + 1) * P:(2 * j + 2) * P],
                                                  src[:, j * P:(j + 1) * P])
                    else:
                        ins = dve.tensor_copy(AT[:, h, 0:2, 2 * P:4 * P], src[:, :].rearrange("p (j t) -> p j t", j=2))
                ins.then_inc(s["lv_copied"], 1)
                if n < 4:
                    dve.wait_ge(s["hsig_ready"], 9 + n)
                    dve.tensor_tensor(hG[:, n, :], hG[:, n, :], bank[n % 2][:, :], ALU.mult).then_inc(s["p_evac_v"], 1)
                if n >= 5:
                    rotate(n - 5)
            for m in range(5, 8):
                rotate(m)

            for h in range(HG_HEADS):
                dve.wait_ge(s["ostd_ready"], h + 1)
                step(dve.reciprocal(osq[:, h % 2, :], osq[:, h % 2, :]))
                step(dve.tensor_tensor(o_sb[:, h % 2, :], o_sb[:, h % 2, :], osq[:, h % 2, :], ALU.mult))
                dve.scalar_tensor_tensor(mixed[:, 4 + h, :], o_sb[:, h % 2, :], pcol("hg_norm", h), hG[:, h, :],
                                         ALU.mult, ALU.mult).then_inc(s["hmix_ready"], 1)

            def masked(u):
                i = u % TT
                w = (i + 1) * P
                a2 = u % 2
                dve.wait_ge(s["sc_ready"], u + 1)
                step(dve.tensor_tensor_reduce(sc[:, a2, 0:w], bank[a2][:, 0:w], madd[:, S - w:S], 1.0, NEG * 4,
                                              ALU.add, ALU.max, att_s[:, a2:a2 + 1]))
                dve.tensor_scalar(att_s[:, 4 + a2:5 + a2], att_s[:, a2:a2 + 1], -SCALE, None, ALU.mult)\
                   .then_inc(s["sc_done"], 1)

            def weighted(u):
                i = u % TT
                w = (i + 1) * P
                a2 = u % 2
                dve.wait_ge(s["e2_ready"], u + 1)
                step(dve.tensor_tensor_reduce(ex[:, a2, 0:w], ex[:, a2, 0:w], ctab[:, S - w:S], 1.0, 0.0,
                                              ALU.mult, ALU.add, att_s[:, 2 + a2:3 + a2]))
                step(dve.reciprocal(att_s[:, 2 + a2:3 + a2], att_s[:, 2 + a2:3 + a2]))
                dve.tensor_scalar(ex[:, a2, 0:w], ex[:, a2, 0:w], att_s[:, 2 + a2:3 + a2], None, ALU.mult)\
                   .then_inc(s["pn_ready"], 1)

            masked(0)
            for u in range(HEADS * TT):
                if u + 1 < HEADS * TT:
                    masked(u + 1)
                weighted(u)

            for i in range(TT):
                for n in range(2):
                    g = 2 * i + n
                    dve.wait_ge(s["o2_ready"], g + 1)
                    part = h2[:, i, n * 512:(n + 1) * 512]
                    dve.tensor_tensor(part, part, bank[g % 4][:, :], ALU.add).then_inc(s["h3_ready"], 1)
                dve.wait_ge(s["ss3_ready"], 2 * i + 2)
                step(dve.reciprocal(rstd[:, i:i + 1], rstd[:, i:i + 1]))
                dve.tensor_scalar(un2[:, i, :], h2[:, i, :], rstd[:, i:i + 1], None, ALU.mult).then_inc(s["un3_ready"], 1)
            for k in range(1, KT, 2):
                dve.wait_ge(s["unT3_ready"], k + 1)
                dve.tensor_scalar(u2T[:, k, :], bank[k][:, :], pcol("norm2", k), None, ALU.mult).then_inc(s["u2T_done_v"], 1)

            for f in range(FFN_T):
                dve.wait_ge(s["fs_ready"], f + 1)
                step(dve.tensor_tensor(fsig[:, f % 2, :], fsig[:, f % 2, :], bank[2 * (f % 2)][:, :], ALU.mult))
                dve.wait_ge(s["f_ready"], 2 * f + 2)
                dve.tensor_tensor(fact[:, f, :], fsig[:, f % 2, :], bank[2 * (f % 2) + 1][:, :], ALU.mult)\
                   .then_inc(s["f_evac"], 1)

            dve.wait_ge(s["fd_used"], 6)
            dve.wait_ge(s["fin_row_in"], 16)
            for i in range(TT):
                for n in range(2):
                    part = h2[:, i, n * 512:(n + 1) * 512]
                    dve.tensor_tensor(part, part, bank[2 * i + n][:, :], ALU.add).then_inc(s["h4_ready"], 1)
            for i in range(TT):
                dve.wait_ge(s["ss4_ready"], 2 * i + 2)
                step(dve.reciprocal(rstd[:, 4 + i:5 + i], rstd[:, 4 + i:5 + i]))
                dve.scalar_tensor_tensor(outt[:, i, :], h2[:, i, :], rstd[:, 4 + i:5 + i], rowvec[:, 0:D], ALU.mult, ALU.mult)\
                   .then_inc(s["out_ready"], 1)



def constants():
    f = np.float32
    p = np.arange(P)
    c = {}
    c["cst"] = np.concatenate([np.eye(P), np.ones((P, P)), p[:, None] < p[None, :]], axis=1).astype(f)
    t = np.arange(S)
    windows = np.repeat([[2, 4], [8, 16]], P // 2, axis=1).reshape(2, P)
    c["invcnt"] = (1.0 / np.minimum(t[None, None, :] + 1, windows.T[:, :, None])).astype(f).reshape(P, 2 * S)
    c["eiota"] = np.arange(E, dtype=f)[None, :]
    token = (p[:, None, None] + P * np.arange(TT)[None, :, None]) + np.zeros((1, 1, TOPK), int)
    c["pairs"] = np.stack([token + S * np.arange(TOPK), token], axis=-1).reshape(P, -1).astype(np.int32)
    c["blockid"] = np.arange(META, dtype=f)[None, :]
    delta = p[:, None] + (TT - 1) * P - t[None, :]
    count = np.zeros((P, S))
    for window, dilation in ((128, 1), (512, 4), (2048, 16)):
        count += (delta >= 0) & (delta <= window) & (delta % dilation == 0)
    half = DH // 2
    inv_freq = (f(10000.0) ** (-np.arange(half, dtype=f) / f(half))).astype(f)
    ang = (t.astype(f)[None, :] * inv_freq[p % half][:, None]).astype(f).astype(np.float64)
    sign = np.where(p % DH < half, -1.0, 1.0)[:, None]
    c["c2"] = np.concatenate([count, np.where(count > 0, 0.0, NEG), np.cos(ang), sign * np.sin(ang)], axis=1).astype(f)
    levels = [np.eye(P)]
    for n in range(TILE_LEVELS):
        L = 1 << n
        levels.append((p[:, None] // (2 * L) == p[None, :] // (2 * L)) & (p[:, None] // L % 2 == 0) & (p[None, :] // L % 2 == 1))
    c["lmask"] = np.concatenate(levels, axis=1).astype(np.int32)
    return c


def kernel(**inputs):
    import concourse.bacc as _bacc
    from concourse.bass_utils import run_bass_kernel_spmd as _run

    x = {k: np.asarray(val) for k, val in inputs.items()}

    def cols(w, tiles):
        w = w.reshape(w.shape[0] // P, P, -1, P)[:, :, tiles, :]
        return w.transpose(1, 0, 2, 3).reshape(P, -1)

    def per_channel(w):
        n = w.shape[0]
        return w.reshape(n, -1, P).transpose(2, 1, 0).reshape(P, -1)

    def pack(chunks):
        out = np.zeros((len(chunks), P, CH), np.float32)
        for n, c in enumerate(chunks):
            out[n, :, 0:c.shape[1]] = c
        return out

    w_in = x["w_in"][0]
    order = [0, 3, 1, 4, 2, 5, 9, 12, 10, 13, 11, 14, 6, 7, 8, 15, 16]
    w_out = x["w_out"][0]
    pg, pp = x["ple_w_gate"][0], x["ple_w_proj"][0]
    arrays = {}
    arrays["wd"] = pack([cols(w_in, order[4 * n:4 * n + 4]) for n in range(5)]
                        + [cols(w_out, list(range(4 * n, 4 * n + 4))) for n in range(2)]
                        + [cols(pg, list(range(4 * n, 4 * n + 4))) for n in range(2)]
                        + [cols(pp, list(range(8)))])
    gu = x["w_gate_up"][0].reshape(E, KT, P, 2, GU_CHUNKS, 2, P)
    gu = gu.transpose(0, 4, 2, 1, 3, 5, 6).reshape(E, GU_CHUNKS, P, CH)
    dn = x["w_down"][0].reshape(E, KT, P, DN_CHUNKS, 512).transpose(0, 3, 2, 1, 4).reshape(E, DN_CHUNKS, P, CH)
    arrays["wmoe"] = np.concatenate([gu, dn], axis=1)
    w2 = x["w_in_2_2"][0] if "w_in_2_2" in x else x["w_in_2"][0]
    g2 = x["w_gate_up_2"][0]
    d2 = x["w_down_2"][0].reshape(FFN_T, P, D).transpose(1, 0, 2)
    arrays["wp"] = pack([cols(w2, list(range(a, a + 4))) for a in (12, 16, 24, 0, 4, 8, 20)]
                        + [cols(x["w_out_2"][0], list(range(4 * n, 4 * n + 4))) for n in range(2)]
                        + [cols(g2, [2 * n, 2 * n + 1, FFN_T + 2 * n, FFN_T + 2 * n + 1]) for n in range(FFN_T // 2)]
                        + [d2[:, 4 * n:4 * n + 4].reshape(P, -1) for n in range(6)])
    c = constants()
    arrays["par"] = np.concatenate(
        [per_channel(x["conv_a_w"][0]), per_channel(x["conv_a_b"]), per_channel(x["ln_a_g"]), per_channel(x["ln_a_b"]),
         per_channel(x["conv_b_w"][0]), per_channel(x["pool_scale"]), per_channel(x["ln1_g"]), per_channel(x["ln1_b"]),
         per_channel(x["norm1_w_2"]), per_channel(x["norm2_w_2"]), per_channel(x["hgrn_norm_w_2"]),
         per_channel(x["lb_logits_2"][0:1]), per_channel(x["lb_logits_2"][1:2]),
         np.tile(np.array([[LN_EPS, NORM_EPS]], np.float32), (P, 1))], axis=1)
    poolw = np.zeros((2, P, P), np.float32)
    for g in range(4):
        lo = (g % 2) * 64
        poolw[g // 2, lo:lo + 64, lo:lo + 64] = x["pool_w"][0, g]
    arrays["poolw"] = poolw.transpose(1, 0, 2).reshape(P, 2 * P)
    arrays["rw"] = x["router_w"][0].reshape(KT, P, E).transpose(1, 0, 2).reshape(P, KT * E)
    arrays["rb"] = x["router_b"]
    arrays["rows"] = np.concatenate([x["ln1_g"], x["ln1_b"], x["ln2_g"], x["ln2_b"], x["final_norm_w_2"][None]], axis=0)
    arrays["xT"] = x["x"][0].reshape(S, KT, P).transpose(2, 1, 0).reshape(P, KT * S)
    arrays["xtok"] = x["x"][0].reshape(TT, P, D).transpose(1, 0, 2).reshape(P, TT * D)
    arrays["pT"] = x["p"][0, 0].reshape(S, 2, P).transpose(2, 1, 0).reshape(P, 2 * S)
    arrays["bgu"] = x["b_gate_up"][0].reshape(E, 16, P).transpose(2, 0, 1).reshape(P, E * 16)
    arrays["bdn"] = x["b_down"][0]
    arrays.update(c)

    nc = _bacc.Bacc("TRN2", target_bir_lowering=False, num_devices=1)
    handles = {}
    arrays = {f"in_{k}": np.ascontiguousarray(val) for k, val in arrays.items()}
    for k, val in arrays.items():
        handles[k[3:]] = nc.dram_tensor(k, val.shape, mybir.dt.from_np(val.dtype), kind="ExternalInput").ap()
    handles["out"] = nc.dram_tensor("out_0", (S, D), F32, kind="ExternalOutput").ap()
    build(nc, handles)
    r = _run(nc, [arrays], core_ids=[0])
    return r.results[0]["out_0"].reshape(1, S, D)
```

```python
from contextlib import ExitStack

import numpy as np

import concourse.bass as bass
from concourse import mybir

ALU = mybir.AluOpType
ACT = mybir.ActivationFunctionType
AX = mybir.AxisListType
F32 = mybir.dt.float32
F32R = mybir.dt.float32r
I32 = mybir.dt.int32
U32 = mybir.dt.uint32

P = 128
S = 512
D = 1024
KT = D // P
TT = S // P
C_CONF = 384
NC_T = C_CONF // P
D_POOL = 256
CONV_A = 31
CONV_B = 3
POOL_PAD = 16
E = 32
TOPK = 4
ALPHA = float(2 ** 0.25)
LN_EPS = 1e-5
NORM_EPS = 1e-6
LIMIT = 7.0
SW_ALPHA = 1.702

CAP = 96
BLOCKS = (S * TOPK + E * (CAP - 1)) // CAP
LEAST_BLOCKS = -(-S * TOPK // CAP)
MAX_PER_EXPERT = -(-S // CAP)
META = 64
NB_META = 56
META_T = META - 1
NO_ROW = 2 * TOPK * S
META_LAST = META - 2
GU_CHUNKS = 4
HALVES = 3 * GU_CHUNKS
RAW = 6
PAIRS = 4

HEADS = 8
DH = 64
SCALE = DH ** -0.5
HG_HEADS = 4
LEVELS = 9
TILE_LEVELS = 7
FFN = 2816
FFN_T = FFN // P
NEG = -1.0e30

RING = 6
CH = 4096
HW = CH // 2
PRE = 10
PRE_SLOT = [0, 1, 2, 3, 4, 5, 3, 4, 5, 3]
RING2 = 3
POST = 26

PAR = {}
_at = 0
for _name, _n in (("conv_a_w", NC_T * CONV_A), ("conv_a_b", NC_T), ("ln_a_g", NC_T), ("ln_a_b", NC_T),
                  ("conv_b_w", NC_T * CONV_B), ("pool_scale", 2), ("ln1_g", KT), ("ln1_b", KT),
                  ("norm1", KT), ("norm2", KT), ("hg_norm", HG_HEADS), ("lb", 2 * HG_HEADS),
                  ("eps", 2), ("expert", 1)):
    PAR[_name] = _at
    _at += _n
N_PAR = _at


class Steps:

    def __init__(self, eng, sem, base=0):
        self.eng, self.sem, self.base, self.n = eng, sem, base, 0

    def __call__(self, ins):
        self.mark(ins)
        self.wait()

    def mark(self, ins):
        ins.then_inc(self.sem, 1)
        self.n += 1

    def wait(self):
        self.eng.wait_ge(self.sem, self.base + self.n)


def build(nc, a):
    ctx = ExitStack()
    with ctx:
        def sb(name, shape, dt=F32):
            return ctx.enter_context(nc.sbuf_tensor(name, shape, dt))

        def sem(name):
            return ctx.enter_context(nc.semaphore(name))

        with nc.sbuf_tensor("ring_r", [P, RING * CH], F32R) as ring_r, nc.sbuf_tensor("room_r", [P, 24576], F32R) as room_r:
            pass
        ring = sb("ring", [P, RING * CH])
        room = sb("room", [P, 24576])
        rowvec = sb("rowvec", [P, 2 * D])
        par = sb("par", [P, N_PAR])
        cst = sb("cst", [P, 3 * P])
        poolw = sb("poolw", [P, 2, P])
        rw = sb("rw", [P, KT, E])
        rb = sb("rb", [P, E])
        eiota = sb("eiota", [P, E])
        pairs = sb("pairs", [P, TT * TOPK * 2], U32)
        blockid = sb("blockid", [P, META])
        meta = sb("meta", [1, META], I32)
        small = sb("small", [P, 128])
        bank = [ctx.enter_context(nc.psum_tensor(f"bank{i}", [P, 512], F32)) for i in range(8)]

        def v(at, n):
            return room[:, at:at + n]

        def vr(at, n):
            return room_r[:, at:at + n]

        def slot(n):
            return ring[:, n * CH:(n + 1) * CH]

        def pcol(name, n=0):
            return par[:, PAR[name] + n:PAR[name] + n + 1]

        eps_ln, eps_rms = pcol("eps", 0), pcol("eps", 1)
        ident = cst[:, 0:P]
        ones = cst[:, P:2 * P]
        before = cst[:, 2 * P:3 * P]

        xT = v(0, KT * S).rearrange("p (k t) -> p k t", k=KT)
        z = v(4096, 17 * S).rearrange("p (j t) -> p j t", j=17)
        UP = 544
        upad = v(12800, NC_T * UP).rearrange("p (i t) -> p i t", i=NC_T)
        cpad = v(14432, NC_T * 516).rearrange("p (i t) -> p i t", i=NC_T)
        PP = S + POOL_PAD
        ppad = v(15980, 2 * PP).rearrange("p (i t) -> p i t", i=2)
        invcnt = v(17036, 2 * S).rearrange("p (i t) -> p i t", i=2)
        pwin = v(18060, 2 * PP).rearrange("p (i t) -> p i t", i=2)
        mu_a = v(19116, S)
        rs_a = v(19628, S)
        AV, AG, CG, BV, BG, PL = [0, 2, 4], [1, 3, 5], [6, 8, 10], [7, 9, 11], [12, 13, 14], [15, 16]
        mixT = [z[:, j, :] for j in AV + BG + PL]

        hn = v(20480, TT * D).rearrange("p (i d) -> p i d", i=TT)
        acc = v(16384, TT * D).rearrange("p (i d) -> p i d", i=TT)
        hT = v(0, KT * S).rearrange("p (k t) -> p k t", k=KT)
        pT = v(15360, 2 * S).rearrange("p (k t) -> p k t", k=2)
        sgate = v(14336, 2 * S).rearrange("p (a t) -> p a t", a=2)
        bdn = v(11264, D)
        GT = v(9216, S)
        oh = v(9728, TT * TOPK * E).rearrange("p (i k e) -> p i k e", i=TT, k=TOPK)
        ohw = v(10240, TT * TOPK * E).rearrange("p (i k e) -> p i k e", i=TT, k=TOPK)
        mask = v(10752, TT * E).rearrange("p (i e) -> p i e", i=TT)
        gmat = v(10880, TT * E).rearrange("p (i e) -> p i e", i=TT)
        pos = v(11008, TT * E).rearrange("p (i e) -> p i e", i=TT)
        logit = v(11136, TT * E).rearrange("p (i e) -> p i e", i=TT)
        cmp_be = v(4096, NB_META * E)
        plet = v(6656, S)
        braw = v(20480, 4 * 512)
        bias_tab = vr(12288, 4 * 512)
        sel_cur = vr(7680, CAP)
        sel_all = v(7808, NB_META)
        xg = v(4096, D)
        xT_hi = vr(0, KT * P).rearrange("p (k s) -> p k s", k=KT)
        xT_lo = vr(1024, KT * P).rearrange("p (k s) -> p k s", k=KT)
        gu_sb = v(5120, 2 * 512).rearrange("p (a c) -> p a c", a=2)
        sig_sb = v(6144, 2 * 256).rearrange("p (a c) -> p a c", a=2)
        ug_sb = v(6656, 2 * 256).rearrange("p (a c) -> p a c", a=2)
        act_sb = v(7168, 2 * 256).rearrange("p (a c) -> p a c", a=2)
        actT_hi = vr(2048, KT * P).rearrange("p (k s) -> p k s", k=KT)
        actT_lo = vr(3072, KT * P).rearrange("p (k s) -> p k s", k=KT)
        y_sb = v(8192, D)
        raw_w = [ring[:, n * HW:(n + 1) * HW] for n in range(RAW)]
        pair = [ring_r[:, n * CH:(n + 1) * CH] for n in (3, 4, 5)] + [vr(20480, CH)]
        w_hi = [q[:, 0:HW] for q in pair]
        w_lo = [q[:, HW:CH] for q in pair]
        yk = [t.rearrange("p (k d) -> p k d", k=TOPK) for t in (v(9216, CH), v(4096, CH), slot(4), slot(5))]
        idx_tok = sb("idx_tok", [P, 1], U32)
        idx_row = sb("idx_row", [P, 1], U32)
        places = sb("places", [P, BLOCKS + 1, 2], U32)
        mv8 = sb("mv8", [P, TT, 8])
        mi8 = sb("mi8", [P, TT, 8], U32)
        mif = sb("mif", [P, TT, 8])
        gate = sb("gate", [P, TT, TOPK])
        gsum = sb("gsum", [P, TT])
        destf = sb("destf", [P, TT * TOPK])
        dest = sb("dest", [P, TT * TOPK], U32)
        cnt = sb("cnt", [P, 4, E])
        metaf = sb("metaf", [P, META])
        stats = sb("stats", [P, 2, 6])
        mva = sb("mva", [P, TT, 2])
        rstd = sb("rstd", [P, 8])
        att_s = sb("att_s", [P, 8])

        uT = hT
        qkT = v(4096, 8 * S).rearrange("p (m t) -> p m t", m=8)
        raw = v(8192, 2 * S).rearrange("p (a t) -> p a t", a=2)
        swp = v(9216, 2 * S).rearrange("p (a t) -> p a t", a=2)
        hQ = v(10240, HG_HEADS * S)
        hK = v(12288, HG_HEADS * S)
        hF = v(14336, HG_HEADS * S)
        h2 = acc
        tot = [hF, v(20480, 1024), v(21504, 512), v(22016, 256), v(22272, 128), v(22400, 64), v(22464, 32),
               v(22496, 16), v(22512, 8)]
        hG = v(22528, HG_HEADS * S).rearrange("p (h t) -> p h t", h=HG_HEADS)
        un = hn
        AT = ring[:, 4 * CH:6 * CH].rearrange("p (h j t) -> p h j t", h=HG_HEADS, j=TT)
        c2 = slot(3)
        ctab, madd, cosT, sinT = (c2[:, n * S:(n + 1) * S] for n in range(4))
        lmask = c2[:, 4 * S:4 * S + 8 * P].bitcast(I32).rearrange("p (l s) -> p l s", l=8)
        v_tok = v(10240, TT * S).rearrange("p (j c) -> p j c", j=TT)
        i_tok = v(12288, TT * S).rearrange("p (j c) -> p j c", j=TT)
        mixed = v(0, 8 * S).rearrange("p (m t) -> p m t", m=8)
        o_sb = v(20480, 2 * S).rearrange("p (a t) -> p a t", a=2)
        osq = v(21504, 2 * S).rearrange("p (a t) -> p a t", a=2)
        sc = v(14336, 2 * S).rearrange("p (a t) -> p a t", a=2)
        ex = v(15360, 2 * S).rearrange("p (a t) -> p a t", a=2)
        pTa = v(8192, TT * S).rearrange("p (j t) -> p j t", j=TT)
        un2 = ring[:, 4 * CH:5 * CH].rearrange("p (i d) -> p i d", i=TT)
        u2T = hT
        fact = v(4096, FFN_T * S).rearrange("p (f t) -> p f t", f=FFN_T)
        fsig = v(15360, 2 * S).rearrange("p (a t) -> p a t", a=2)
        outt = hn

        h_dram = nc.dram_tensor("h_rows", (S, D), F32).ap()
        y_dram = nc.dram_tensor("expert_rows", (TOPK * S, D), F32).ap()
        slot_dram = nc.dram_tensor("slot_rows", ((BLOCKS + 1) * CAP, 2), U32).ap()

        names = """xT_in consts_in xtok_in ln1_rows_in late_in table_zeroed h_out scattered y_out z_ready z_evac
            pads_ready conv_ready sq_ready mean_ready var_ready std_ready ln_a_ready sgl_ready pool_in_ready
            pool_ready pool_out_ready mixT_ready mix_ready mix_evac v1_ready s1_ready hn_ready hT_done_a
            hT_done_v hnT_ready h_ready router_ready mask_ready pos_ready e_ready ex_ready meta_ready dest_ready
            gm_ready gT_ready GT_ready pleg_ready plep_ready sg_ready ple_evac bdn_ready bdn_done idx_in
            idx_kept tok_kept rows_in bias_in bias_hi bias_split sel_ready hi_done lo_dve lo_pool half_used evac_done
            sig_done act_ready xt_ready x_hi x_lo turned act_hi act_lo y_copied yg_used ln2_rows_in fin_row_in c2_in v2_ready s2_ready x2_ready ss_ready
            un_ready unT_ready uT_done_a uT_done_v p_ready p_evac hsig_ready rot_done fK_ready lv_ready lv_upd
            lv_copied asum_ready p_evac_v vt_ready vt_evac o_ready o_evac osq_ready oms_ready ostd_ready
            hmix_ready sc_ready sc_done e2_ready pn_ready pt_ready pt_evac pv_ready pv_evac o2_ready h3_ready
            ss3_ready un3_ready unT3_ready u2T_done_a u2T_done_v f_ready fs_ready f_evac fd_used h4_ready
            ss4_ready out_ready out_written pool_waited dve_steps act_steps pool_steps moe_dve lb_ready
            lbe_ready""".split()
        s = {n: sem(n) for n in names}
        chunk_in = [sem(f"chunk_in{n}") for n in range(RING)]
        raw_in = [sem(f"raw_in{n}") for n in range(RAW)]
        post_in = [sem(f"post_in{n}") for n in range(RING2)]
        yk_in = [sem(f"yk_in{n}") for n in range(TT)]
        swap_in = [sem(f"swap_in{n}") for n in range(2)]

        pre_used = ([("z_ready", 4), ("z_ready", 8), ("z_ready", 12), ("z_ready", 16), ("z_ready", 17),
                     ("mix_ready", 7), ("mix_ready", 8), ("pleg_ready", 7), ("pleg_ready", 8), ("plep_ready", 8)])
        post_used = ([("p_ready", 4 * (c + 1)) for c in range(5)] + [("vt_ready", 4), ("vt_ready", 8)]
                     + [("o2_ready", 7), ("o2_ready", 8)] + [("f_ready", 4 * (c + 1)) for c in range(11)]
                     + [("fd_used", c + 1) for c in range(6)])
        assert len(pre_used) == PRE and len(post_used) == POST

        def chunk_cols(n):
            return {4: KT * P, 9: 2 * D}.get(n, CH)

        def post_cols(n):
            return 2 * D if n == POST - 1 else CH

        def chunk(eng, n):
            q = PRE_SLOT[n]
            eng.wait_ge(chunk_in[q], 16 * PRE_SLOT[0:n + 1].count(q))
            return slot(q)

        def split_by_pool(i):
            return i % 4 == 3

        def split_count(b, i):
            if split_by_pool(i):
                return s["lo_pool"], b * (HALVES // 4) + (i // 4 + 1)
            return s["lo_dve"], b * (HALVES - HALVES // 4) + (i - i // 4 + 1)

        def chunk2(eng, n):
            eng.wait_ge(post_in[n % RING2], 16 * (n // RING2 + 1))
            return slot(n % RING2)

        block = ctx.enter_context(nc.Block())

        @block.sync
        def _(sp):
            for k in range(KT):
                sp.dma_start(xT[:, k, :], a["xT"][:, k * S:(k + 1) * S]).then_inc(s["xT_in"], 16)
                if k == 0:
                    sp.dma_start(slot(0), a["wd"][0]).then_inc(chunk_in[0], 16)
            for n in range(1, PRE):
                q = PRE_SLOT[n]
                if q in PRE_SLOT[0:n]:
                    name, count = pre_used[max(m for m in range(n) if PRE_SLOT[m] == q)]
                    sp.wait_ge(s[name], count)
                sp.dma_start(slot(q)[:, 0:chunk_cols(n)], a["wd"][n, :, 0:chunk_cols(n)]).then_inc(chunk_in[q], 16)

            sp.wait_ge(s["meta_ready"], 3)
            T = sp.value_load(meta[0:1, META_T:META_T + 1], min_val=LEAST_BLOCKS, max_val=BLOCKS)

            last = sp.value_load(meta[0:1, META_LAST:META_LAST + 1], min_val=LEAST_BLOCKS - 1, max_val=BLOCKS - 1)

            def block_loads(b, first):
                expert = sp.value_load(meta[0:1, bass.ts(b, 1)], min_val=0, max_val=E - 1)
                for i in range(HALVES):
                    if i >= RAW:
                        sp.wait_ge(*split_count(b, i - RAW))
                    elif not first:
                        sp.wait_ge(*split_count(b - 1, i + HALVES - RAW))
                    sp.dma_start(raw_w[i % RAW], a["wmoe"][bass.ts(expert, 1), i].rearrange("o p n -> (o p) n"))\
                      .then_inc(raw_in[i % RAW], 16)

            block_loads(0, True)
            with sp.Fori(1, BLOCKS) as b:
                with sp.If(b < T):
                    block_loads(b, False)

            for n in range(POST):
                if n < RING2:
                    sp.wait_ge(s["half_used"], last * HALVES + (RAW + 2 * n + 2))
                else:
                    sp.wait_ge(s[post_used[n - RING2][0]], post_used[n - RING2][1])
                sp.dma_start(slot(n % RING2)[:, 0:post_cols(n)], a["wp"][n, :, 0:post_cols(n)])\
                  .then_inc(post_in[n % RING2], 16)
                if n == 0:
                    sp.wait_ge(s["half_used"], T * HALVES)
                    sp.dma_start(c2[:, 0:4 * S], a["c2"]).then_inc(s["c2_in"], 16)
                    sp.dma_start(lmask, a["lmask"].rearrange("p (l s) -> p l s", l=8)).then_inc(s["c2_in"], 16)
                if n == 2:
                    sp.wait_ge(s["y_out"], T * 16)
                    for i in range(TT):
                        sp.dma_start(yk[i], y_dram.rearrange("(k i p) d -> i p k d", k=TOPK, p=P)[i]).then_inc(yk_in[i], 16)
                    sp.wait_ge(s["h_ready"], 2 * TT)
                    sp.dma_start(rowvec[:, 0:D], a["rows"][2:3, :].broadcast_to([P, D])).then_inc(s["ln2_rows_in"], 16)
                    sp.dma_start(rowvec[:, D:2 * D], a["rows"][3:4, :].broadcast_to([P, D])).then_inc(s["ln2_rows_in"], 16)
                if n == 9:
                    sp.wait_ge(s["x2_ready"], 2 * TT)
                    sp.dma_start(rowvec[:, 0:D], a["rows"][4:5, :].broadcast_to([P, D])).then_inc(s["fin_row_in"], 16)

            for i in range(TT):
                sp.wait_ge(s["out_ready"], i + 1)
                sp.dma_start(a["out"][i * P:(i + 1) * P, :], outt[:, i, :]).then_inc(s["out_written"], 16)
            sp.wait_ge(s["out_written"], 16 * TT)

        @block.gpsimd
        def _(pool):
            step = Steps(pool, s["pool_steps"])
            places_row = places[0:CAP, :, :].rearrange("p n o -> p (n o)")
            step.mark(pool.memset(upad[:, :, 0:CONV_A - 1], 0.0))
            step.mark(pool.memset(cpad[:, :, 0:CONV_B - 1], 0.0))
            step.mark(pool.memset(ppad[:, :, 0:POOL_PAD], 0.0))
            pool.memset(pwin[:, :, 0:POOL_PAD], 0.0).then_inc(s["pads_ready"], 1)
            step.mark(pool.memset(places[:, :, 0:1], NO_ROW))
            step(pool.memset(places[:, :, 1:2], 0))
            pool.dma_start(slot_dram.rearrange("(p n) o -> p (n o)", p=CAP), places_row).then_inc(s["table_zeroed"], 16)
            pool.wait_ge(s["ln1_rows_in"], 32)
            for i in range(TT):
                pool.wait_ge(s["hn_ready"], i + 1)
                pool.tensor_tensor(acc[:, i, :], hn[:, i, :], rowvec[:, 0:D], ALU.mult).then_inc(s["h_ready"], 1)
                pool.wait_ge(s["h_ready"], 2 * i + 1)
                pool.tensor_tensor(acc[:, i, :], acc[:, i, :], rowvec[:, D:2 * D], ALU.add).then_inc(s["h_ready"], 1)
                pool.wait_ge(s["h_ready"], 2 * i + 2)
                pool.dma_start(h_dram[i * P:(i + 1) * P, :], acc[:, i, :]).then_inc(s["h_out"], 16)
            pool.wait_ge(s["hnT_ready"], KT)
            pool.dma_start(braw, a["bgu"]).then_inc(s["bias_in"], 16)

            pool.wait_ge(s["table_zeroed"], 16)
            pool.wait_ge(s["dest_ready"], 1)
            for i in range(TT):
                for k in range(TOPK):
                    c = i * TOPK + k
                    pool.indirect_dma_start(slot_dram, bass.IndirectOffsetOnAxis(ap=dest[:, c:c + 1], axis=0),
                                            pairs[:, 2 * c:2 * c + 2], None).then_inc(s["scattered"], 16)
            pool.wait_ge(s["scattered"], 16 * TT * TOPK)
            pool.dma_start(places_row, slot_dram.rearrange("(p n) o -> p (n o)", p=CAP)).then_inc(s["idx_in"], 16)
            pool.wait_ge(s["idx_in"], 16)
            pool.wait_ge(s["h_out"], 16 * TT)
            pool.wait_ge(s["meta_ready"], 3)
            T = pool.value_load(meta[0:1, META_T:META_T + 1], min_val=LEAST_BLOCKS, max_val=BLOCKS)

            def wait_counted(name, value):
                pool.wait_ge(s[name], value)
                pool.sem_inc(s["pool_waited"], 1)

            def gather(b):
                pool.tensor_copy(idx_tok[0:CAP, :], places[0:CAP, bass.ds(b, 1), 1]).then_inc(s["tok_kept"], 1)
                wait_counted("tok_kept", b + 1)
                pool.indirect_dma_start(xg[0:CAP, :], None, h_dram,
                                        bass.IndirectOffsetOnAxis(ap=idx_tok[0:CAP, :], axis=0))\
                    .then_inc(s["rows_in"], 16)

            def select(b):
                pool.tensor_copy(sel_cur, sel_all[:, bass.ds(b, 1)].broadcast_to([P, CAP])).then_inc(s["sel_ready"], 1)

            def split_lo(b, i):
                wait_counted("hi_done", b * HALVES + (i + 1))
                pool.tensor_tensor(w_lo[i % PAIRS], raw_w[i % RAW], w_hi[i % PAIRS].bitcast(F32), ALU.subtract)\
                    .then_inc(s["lo_pool"], 1)

            def rows_out(b):
                wait_counted("y_copied", b * 2 + 2)
                wait_counted("idx_kept", b + 1)
                pool.indirect_dma_start(y_dram, bass.IndirectOffsetOnAxis(ap=idx_row[0:CAP, :], axis=0),
                                        y_sb[0:CAP, :], None, bounds_check=TOPK * S - 1, oob_is_err=False)\
                    .then_inc(s["y_out"], 16)

            def block_pool(b, first):
                if not first:
                    rows_out(b - 1)
                split_lo(b, 3)
                wait_counted("rows_in", b * 16 + 16)
                wait_counted("xt_ready", b + 1)
                gather(b + 1)
                split_lo(b, 7)
                if not first:
                    wait_counted("y_out", b * 16)
                pool.tensor_copy(idx_row[0:CAP, :], places[0:CAP, bass.ds(b, 1), 0]).then_inc(s["idx_kept"], 1)
                wait_counted("half_used", b * HALVES + 2 * GU_CHUNKS)
                select(b + 1)
                split_lo(b, 11)

            gather(0)
            select(0)
            block_pool(0, True)
            with pool.Fori(1, BLOCKS) as b:
                with pool.If(b < T):
                    block_pool(b, False)
            last = pool.value_load(meta[0:1, META_LAST:META_LAST + 1], min_val=LEAST_BLOCKS - 1, max_val=BLOCKS - 1)
            rows_out(last)

        @block.scalar
        def _(act):
            step = Steps(act, s["act_steps"])
            act.dma_start(par[:, :], a["par"]).then_inc(s["consts_in"], 16)
            act.dma_start(cst[:, :], a["cst"]).then_inc(s["consts_in"], 16)
            act.dma_start(invcnt, a["invcnt"].rearrange("p (i t) -> p i t", i=2)).then_inc(s["consts_in"], 16)
            act.dma_start(poolw[:, :, :], a["poolw"].rearrange("p (i t) -> p i t", i=2)).then_inc(s["consts_in"], 16)
            act.dma_start(rw[:, :, :], a["rw"].rearrange("p (k e) -> p k e", k=KT)).then_inc(s["consts_in"], 16)
            act.dma_start(rb[:, :], a["rb"].broadcast_to([P, E])).then_inc(s["consts_in"], 16)
            act.dma_start(eiota[:, :], a["eiota"].broadcast_to([P, E])).then_inc(s["consts_in"], 16)
            act.dma_start(pairs[:, :].bitcast(I32), a["pairs"]).then_inc(s["consts_in"], 16)
            act.dma_start(blockid[:, :], a["blockid"].broadcast_to([P, META])).then_inc(s["consts_in"], 16)
            act.dma_start(hn, a["xtok"].rearrange("p (i d) -> p i d", i=TT)).then_inc(s["xtok_in"], 16)
            for r in range(2):
                act.dma_start(rowvec[:, r * D:(r + 1) * D], a["rows"][r:r + 1, :].broadcast_to([P, D]))\
                   .then_inc(s["ln1_rows_in"], 16)

            for j in range(17):
                dst = ppad[:, j - PL[0], POOL_PAD:PP] if j in PL else z[:, j, :]
                if j == PL[0]:
                    act.wait_ge(s["pads_ready"], 1)
                if j == 14:
                    for i in range(NC_T):
                        act.wait_ge(s["mean_ready"], i + 1)
                        act.activation(z[:, AG[i], :], z[:, AV[i], :], ACT.Square).then_inc(s["sq_ready"], 1)
                act.wait_ge(s["z_ready"], j + 1)
                act.activation(dst, bank[j % 4][:, :], ACT.Sigmoid if j in AG else ACT.Copy).then_inc(s["z_evac"], 1)

            act.wait_ge(s["var_ready"], 1)
            act.activation(rs_a, bank[5][:, :], ACT.Sqrt, bias=eps_ln, scale=1.0 / C_CONF).then_inc(s["std_ready"], 1)
            for i in range(NC_T):
                act.wait_ge(s["ln_a_ready"], i + 1)
                act.activation(z[:, AG[i], :], z[:, AV[i], :], ACT.Sigmoid).then_inc(s["sgl_ready"], 1)

            for i in range(2):
                act.wait_ge(s["pool_out_ready"], i + 1)
                act.activation(z[:, PL[i], :], bank[6 + i][:, :], ACT.Copy, scale=pcol("pool_scale", i))\
                   .then_inc(s["pool_ready"], 1)

            for i in range(TT):
                act.wait_ge(s["v1_ready"], i + 1)
                act.activation(rstd[:, i:i + 1], mva[:, i, 1:2], ACT.Sqrt, bias=eps_ln).then_inc(s["s1_ready"], 1)

            act.wait_ge(s["mix_ready"], 2 * TT)
            act.dma_start(pT, a["pT"].rearrange("p (k t) -> p k t", k=2)).then_inc(s["late_in"], 16)
            act.dma_start(bdn[0:E, :], a["bdn"]).then_inc(s["late_in"], 16)

            for k in range(0, KT, 2):
                act.wait_ge(s["hnT_ready"], k + 1)
                act.activation(hT[:, k, :], bank[k][:, :], ACT.Identity, bias=pcol("ln1_b", k), scale=pcol("ln1_g", k))\
                   .then_inc(s["hT_done_a"], 1)

            act.wait_ge(s["e_ready"], 1)
            act.activation(gate[:, :, :], gate[:, :, :], ACT.Exp).then_inc(s["ex_ready"], 1)

            def ple_gate(g):
                act.wait_ge(s["pleg_ready"], g + 1)
                if g >= 2:
                    act.wait_ge(s["ple_evac"], g - 1)
                act.activation(sgate[:, g % 2, :], bank[1 + g % 2][:, :], ACT.Sigmoid).then_inc(s["sg_ready"], 1)

            for g in range(2 * TT):
                ple_gate(g)
                if g == 4:
                    act.wait_ge(s["gT_ready"], 1)
                    act.activation(GT[0:E, :], bank[6][0:E, :], ACT.Copy).then_inc(s["GT_ready"], 1)
                if g == 5:
                    act.wait_ge(s["bias_in"], 16)
                    act.activation(bias_tab, braw, ACT.Copy).then_inc(s["bias_hi"], 1)

            act.wait_ge(s["meta_ready"], 3)
            T = act.value_load(meta[0:1, META_T:META_T + 1], min_val=LEAST_BLOCKS, max_val=BLOCKS)

            last = act.value_load(meta[0:1, META_LAST:META_LAST + 1], min_val=LEAST_BLOCKS - 1, max_val=BLOCKS - 1)

            def split_hi(b, i, first=False):
                act.wait_ge(raw_in[i % RAW], b * (16 * HALVES // RAW) + 16 * (i // RAW + 1))
                if not first or i >= PAIRS:
                    act.wait_ge(s["half_used"], b * HALVES + (i - PAIRS + 1))
                act.activation(w_hi[i % PAIRS], raw_w[i % RAW], ACT.Copy).then_inc(s["hi_done"], 1)

            def gathered_hi(b):
                act.wait_ge(s["xt_ready"], b + 1)
                for q in range(2):
                    ins = act.activation(xT_hi[:, 4 * q:4 * q + 4, 0:CAP],
                                         bank[4 + q][:, 0:4 * CAP].rearrange("p (k s) -> p k s", k=4), ACT.Copy)
                ins.then_inc(s["x_hi"], 1)

            def sigmoids(b, c):
                act.wait_ge(s["evac_done"], b * GU_CHUNKS + (c + 1))
                act.activation(sig_sb[0:CAP, c % 2, :], gu_sb[0:CAP, c % 2, 0:256], ACT.Sigmoid, scale=SW_ALPHA)\
                   .then_inc(s["sig_done"], 1)

            def turned_hi(b, c):
                act.wait_ge(s["turned"], b * GU_CHUNKS + (c + 1))
                act.activation(actT_hi[:, 2 * c:2 * c + 2, 0:CAP],
                               bank[2 + c % 2][:, 0:2 * CAP].rearrange("p (k s) -> p k s", k=2), ACT.Copy)\
                   .then_inc(s["act_hi"], 1)

            def outputs(b):
                act.wait_ge(s["half_used"], b * HALVES + HALVES)
                act.wait_ge(s["idx_kept"], b + 1)
                for n in range(2):
                    act.activation(y_sb[0:CAP, n * 512:(n + 1) * 512], bank[6 + n][0:CAP, :], ACT.Copy)\
                       .then_inc(s["y_copied"], 1)

            def first_part(b, first=False):
                for i in range(9):
                    split_hi(b, i + 3, first)
                    if i >= 2 and i % 2 == 0:
                        sigmoids(b, i // 2 - 1)
                    if i >= 4 and i % 2 == 0:
                        turned_hi(b, i // 2 - 2)
                gathered_hi(b + 1)

            act.wait_ge(s["plep_ready"], 2 * TT)
            for i in range(3):
                split_hi(0, i, True)
            gathered_hi(0)
            act.wait_ge(s["bias_split"], 1)
            first_part(0, True)
            with act.Fori(1, BLOCKS) as b:
                with act.If(b < T):
                    split_hi(b, 0)
                    turned_hi(b - 1, GU_CHUNKS - 1)
                    split_hi(b, 1)
                    split_hi(b, 2)
                    outputs(b - 1)
                    first_part(b)
            turned_hi(last, GU_CHUNKS - 1)
            outputs(last)

            for i in range(TT):
                act.wait_ge(s["v2_ready"], i + 1)
                act.activation(rstd[:, i:i + 1], mva[:, i, 1:2], ACT.Sqrt, bias=eps_ln).then_inc(s["s2_ready"], 1)
                act.wait_ge(s["x2_ready"], 2 * i + 2)
                act.activation(un[:, i, :], h2[:, i, :], ACT.Square, accum_out=rstd[:, 4 + i:5 + i]).then_inc(s["ss_ready"], 1)
                act.wait_ge(s["ss_ready"], 2 * i + 1)
                act.activation(rstd[:, 4 + i:5 + i], rstd[:, 4 + i:5 + i], ACT.Sqrt, bias=eps_rms, scale=1.0 / D)\
                   .then_inc(s["ss_ready"], 1)
            for k in range(0, KT, 2):
                act.wait_ge(s["unT_ready"], k + 1)
                act.activation(uT[:, k, :], bank[k][:, :], ACT.Copy, scale=pcol("norm1", k)).then_inc(s["uT_done_a"], 1)

            act.wait_ge(s["lb_ready"], 1)
            act.activation(small[:, 0:2 * HG_HEADS], small[:, 0:2 * HG_HEADS], ACT.Exp).then_inc(s["lbe_ready"], 1)

            for j in range(20):
                act.wait_ge(s["p_ready"], j + 1)
                if j < 4:
                    act.activation(hQ[:, j * S:(j + 1) * S], bank[j % 2][:, :], ACT.Sigmoid).then_inc(s["hsig_ready"], 1)
                elif j < 8:
                    act.activation(hF[:, (j - 4) * S:(j - 3) * S], bank[j % 2][:, :], ACT.Sigmoid).then_inc(s["hsig_ready"], 1)
                elif j < 12:
                    act.activation(hG[:, j - 8, :], bank[j % 2][:, :], ACT.Sigmoid).then_inc(s["hsig_ready"], 1)
                else:
                    m = j - 12
                    if m >= 2:
                        act.wait_ge(s["rot_done"], m - 1)
                    act.activation(raw[:, m % 2, :], bank[j % 2][:, :], ACT.Copy).then_inc(s["p_evac"], 1)
                    act.wait_ge(s["p_evac"], m + 1)
                    for q in range(4):
                        act.dma_start(swp[q * 32:(q + 1) * 32, m % 2, :], raw[(q ^ 1) * 32:(q ^ 1) * 32 + 32, m % 2, :])\
                           .then_inc(swap_in[m % 2], 16)
            for g in range(8):
                act.wait_ge(s["vt_ready"], g + 1)
                if g < 4:
                    dst = v_tok[:, g, :]
                else:
                    dst = i_tok[:, g - 4, :]
                if g == 0:
                    act.wait_ge(s["lv_ready"], LEVELS + 1)
                act.activation(dst, bank[g % 2][:, :], ACT.Copy).then_inc(s["vt_evac"], 1)

            for h in range(HG_HEADS):
                act.wait_ge(s["o_ready"], h + 1)
                if h >= 2:
                    act.wait_ge(s["hmix_ready"], h - 1)
                act.activation(o_sb[:, h % 2, :], bank[2 + h % 2][:, :], ACT.Copy).then_inc(s["o_evac"], 1)
                act.activation(osq[:, h % 2, :], bank[2 + h % 2][:, :], ACT.Square).then_inc(s["osq_ready"], 1)
                act.wait_ge(s["oms_ready"], h + 1)
                act.activation(osq[:, h % 2, :], bank[4 + h % 2][:, :], ACT.Sqrt, bias=eps_rms, scale=1.0 / P)\
                   .then_inc(s["ostd_ready"], 1)

            def probs_out(h):
                act.wait_ge(s["pt_ready"], TT * (h + 1))
                if h >= 1:
                    act.wait_ge(s["pv_ready"], h)
                for j in range(TT):
                    ins = act.activation(pTa[:, j, j * P:S], bank[2 + j][:, j * P:S], ACT.Copy)
                ins.then_inc(s["pt_evac"], 1)

            def head_out(h):
                act.wait_ge(s["pv_ready"], h + 1)
                lo = (h % 2) * DH
                act.activation(mixed[lo:lo + DH, h // 2, :], bank[6 + h % 2][lo:lo + DH, :], ACT.Copy)\
                   .then_inc(s["pv_evac"], 1)

            for u in range(HEADS * TT):
                h, i = divmod(u, TT)
                act.wait_ge(s["sc_done"], u + 1)
                if u >= 2:
                    act.wait_ge(s["pt_ready"], u - 1)
                w = (i + 1) * P
                act.activation(ex[:, u % 2, 0:w], sc[:, u % 2, 0:w], ACT.Exp, bias=att_s[:, 4 + u % 2:5 + u % 2],
                               scale=SCALE).then_inc(s["e2_ready"], 1)
                if i == 0 and h >= 1:
                    probs_out(h - 1)
                if i == 1 and h >= 1:
                    head_out(h - 1)
            probs_out(HEADS - 1)
            head_out(HEADS - 1)

            for i in range(TT):
                act.wait_ge(s["h3_ready"], 2 * i + 2)
                act.activation(un2[:, i, :], h2[:, i, :], ACT.Square, accum_out=rstd[:, i:i + 1]).then_inc(s["ss3_ready"], 1)
                act.wait_ge(s["ss3_ready"], 2 * i + 1)
                act.activation(rstd[:, i:i + 1], rstd[:, i:i + 1], ACT.Sqrt, bias=eps_rms, scale=1.0 / D)\
                   .then_inc(s["ss3_ready"], 1)
            for k in range(0, KT, 2):
                act.wait_ge(s["unT3_ready"], k + 1)
                act.activation(u2T[:, k, :], bank[k][:, :], ACT.Copy, scale=pcol("norm2", k)).then_inc(s["u2T_done_a"], 1)

            for f in range(FFN_T):
                act.wait_ge(s["f_ready"], 2 * f + 1)
                if f >= 2:
                    act.wait_ge(s["f_evac"], f - 1)
                act.activation(fsig[:, f % 2, :], bank[2 * (f % 2)][:, :], ACT.Sigmoid).then_inc(s["fs_ready"], 1)

            for i in range(TT):
                act.wait_ge(s["h4_ready"], 2 * i + 2)
                act.activation(outt[:, i, :], h2[:, i, :], ACT.Square, accum_out=rstd[:, 4 + i:5 + i])\
                   .then_inc(s["ss4_ready"], 1)
                act.wait_ge(s["ss4_ready"], 2 * i + 1)
                act.activation(rstd[:, 4 + i:5 + i], rstd[:, 4 + i:5 + i], ACT.Sqrt, bias=eps_rms, scale=1.0 / D)\
                   .then_inc(s["ss4_ready"], 1)

        @block.tensor
        def _(pe):
            def accumulate(out, pairs):
                n = len(pairs)
                for k, (lhsT, rhs) in enumerate(pairs):
                    ins = pe.matmul(out, lhsT, rhs, start=(k == 0), stop=(k == n - 1))
                return ins

            pe.wait_ge(s["xT_in"], 16 * KT)

            def z_tile(j):
                w = chunk(pe, j // 4)
                n = 4 if j < 16 else 1
                w = w[:, 0:KT * n * P].rearrange("p (k c) -> p k c", k=KT)
                if j >= 4:
                    pe.wait_ge(s["z_evac"], j - 3)
                c = (j % 4) * P if j < 16 else 0
                accumulate(bank[j % 4][:, :], [(w[:, k, c:c + P], xT[:, k, :]) for k in range(KT)])\
                    .then_inc(s["z_ready"], 1)

            for j in range(17):
                z_tile(j)
                if j == 0:
                    pe.wait_ge(s["consts_in"], 16 * 9)
                if j == 12:
                    pe.wait_ge(s["conv_ready"], NC_T)
                    accumulate(bank[4][:, :], [(ones, z[:, t, :]) for t in AV]).then_inc(s["asum_ready"], 1)
                if j == 14:
                    pe.wait_ge(s["sq_ready"], NC_T)
                    accumulate(bank[5][:, :], [(ones, z[:, t, :]) for t in AG]).then_inc(s["var_ready"], 1)
            for i in range(2):
                pe.wait_ge(s["pool_in_ready"], i + 1)
                accumulate(bank[6 + i][:, :], [(poolw[:, i, :], z[:, PL[i], :])]).then_inc(s["pool_out_ready"], 1)

            pe.wait_ge(s["z_evac"], 17)
            pe.wait_ge(s["mixT_ready"], NC_T)
            pe.wait_ge(s["pool_ready"], 2)
            for g in range(2 * TT):
                i, n = divmod(g, 2)
                w = chunk(pe, 5 + n).rearrange("p (k c) -> p k c", k=KT)
                if g >= 4:
                    pe.wait_ge(s["mix_evac"], g - 3)
                accumulate(bank[g % 4][:, :], [(mixT[k][:, i * P:(i + 1) * P], w[:, k, :]) for k in range(KT)])\
                    .then_inc(s["mix_ready"], 1)

            pe.wait_ge(s["mix_evac"], 2 * TT)
            for i in range(TT):
                pe.wait_ge(s["hn_ready"], i + 1)
                for k in range(KT):
                    ins = pe.transpose(bank[k][:, i * P:(i + 1) * P], hn[:, i, k * P:(k + 1) * P], ident)
                    if i == TT - 1:
                        ins.then_inc(s["hnT_ready"], 1)

            pe.wait_ge(s["hT_done_a"], KT // 2)
            pe.wait_ge(s["hT_done_v"], KT // 2)
            for i in range(TT):
                ins = accumulate(bank[0][:, i * E:(i + 1) * E],
                                 [(hT[:, k, i * P:(i + 1) * P], rw[:, k, :]) for k in range(KT)])
            ins.then_inc(s["router_ready"], 1)

            def ple(g):
                i, n = divmod(g, 2)
                w = chunk(pe, 7 + n).rearrange("p (k c) -> p k c", k=KT)
                if g >= 2:
                    pe.wait_ge(s["ple_evac"], g - 1)
                accumulate(bank[1 + g % 2][:, :], [(hT[:, k, i * P:(i + 1) * P], w[:, k, :]) for k in range(KT)])\
                    .then_inc(s["pleg_ready"], 1)
                w = chunk(pe, 9)[:, 0:2 * D].rearrange("p (k c) -> p k c", k=2)
                if g == 0:
                    pe.wait_ge(s["late_in"], 32)
                accumulate(bank[3 + g % 2][:, :],
                           [(pT[:, k, i * P:(i + 1) * P], w[:, k, n * 512:(n + 1) * 512]) for k in range(2)])\
                    .then_inc(s["plep_ready"], 1)

            ple(0)
            ple(1)
            pe.wait_ge(s["mask_ready"], 1)
            for i in range(TT):
                accumulate(bank[5][:, i * E:(i + 1) * E],
                           [(ones, mask[:, j, :]) for j in range(i)] + [(before, mask[:, i, :])])
            accumulate(bank[5][:, TT * E:(TT + 1) * E], [(ones, mask[:, j, :]) for j in range(TT)])\
                .then_inc(s["pos_ready"], 1)
            ple(2)
            ple(3)
            pe.wait_ge(s["gm_ready"], 1)
            for i in range(TT):
                ins = pe.transpose(bank[6][0:E, i * P:(i + 1) * P], gmat[:, i, :], ident)
            ins.then_inc(s["gT_ready"], 1)
            for g in range(4, 2 * TT):
                ple(g)
            pe.wait_ge(s["GT_ready"], 1)
            for g in range(2 * TT):
                i, n = divmod(g, 2)
                if g >= 2:
                    pe.wait_ge(s["bdn_done"], g - 1)
                accumulate(bank[7 * (g % 2)][:, :], [(GT[0:E, i * P:(i + 1) * P], bdn[0:E, n * 512:(n + 1) * 512])])\
                    .then_inc(s["bdn_ready"], 1)

            pe.wait_ge(s["meta_ready"], 3)
            T = pe.value_load(meta[0:1, META_T:META_T + 1], min_val=LEAST_BLOCKS, max_val=BLOCKS)
            pe.wait_ge(s["ple_evac"], 2 * TT)
            pe.wait_ge(s["bdn_done"], 2 * TT)

            pe.wait_ge(s["bias_split"], 1)

            def gathered(b):
                pe.wait_ge(s["rows_in"], b * 16 + 16)
                for k in range(KT):
                    ins = pe.transpose(bank[4 + k // 4][:, (k % 4) * CAP:(k % 4 + 1) * CAP],
                                       xg[0:CAP, k * P:(k + 1) * P], ident[0:CAP, 0:CAP])
                ins.then_inc(s["xt_ready"], 1)

            def product(out, x_hi, x_lo, w_hi, w_lo, start, stop):
                pe.matmul(out, x_hi, w_hi, start=start, stop=False, skip_group_check=True)
                pe.matmul(out, x_hi, w_lo, start=False, stop=False, skip_group_check=True)
                return pe.matmul(out, x_lo, w_hi, start=False, stop=stop, skip_group_check=True)

            def turn(b, c):
                pe.wait_ge(s["act_ready"], b * GU_CHUNKS + (c + 1))
                if c >= 2:
                    pe.wait_ge(s["act_lo"], b * GU_CHUNKS + (c - 1))
                for r in range(2):
                    ins = pe.transpose(bank[2 + c % 2][:, r * CAP:(r + 1) * CAP],
                                       act_sb[0:CAP, c % 2, r * P:(r + 1) * P], ident[0:CAP, 0:CAP])
                ins.then_inc(s["turned"], 1)

            def block_pe(b, first):
                pe.wait_ge(s["x_lo"], b + 1)
                pe.wait_ge(s["sel_ready"], b + 1)
                for i in range(2 * GU_CHUNKS):
                    c = i // 2
                    out = bank[c % 2][0:CAP, :]
                    if i % 2 == 0:
                        if not first or c >= 2:
                            pe.wait_ge(s["evac_done"], b * GU_CHUNKS + (c - 1))
                        pe.matmul(out, sel_cur, bias_tab[:, c * 512:(c + 1) * 512], start=True, stop=False,
                                  skip_group_check=True)
                    pe.wait_ge(*split_count(b, i))
                    hi, lo = (w[i % PAIRS].rearrange("p (k c) -> p k c", k=4) for w in (w_hi, w_lo))
                    for q in range(4):
                        k = 4 * (i % 2) + q
                        ins = product(out, xT_hi[:, k, 0:CAP], xT_lo[:, k, 0:CAP], hi[:, q, :], lo[:, q, :],
                                      False, k == KT - 1)
                    ins.then_inc(s["half_used"], 1)
                    if i % 2 == 1 and c >= 1:
                        turn(b, c - 1)
                gathered(b + 1)
                for d in range(GU_CHUNKS):
                    i = 2 * GU_CHUNKS + d
                    if d == 0 and not first:
                        pe.wait_ge(s["y_copied"], b * 2)
                    pe.wait_ge(s["act_lo"], b * GU_CHUNKS + (d + 1))
                    pe.wait_ge(*split_count(b, i))
                    hi, lo = (w[i % PAIRS].rearrange("p (r c) -> p r c", r=2) for w in (w_hi, w_lo))
                    for r in range(2):
                        k = 2 * d + r
                        for n in range(2):
                            ins = product(bank[6 + n][0:CAP, :], actT_hi[:, k, 0:CAP], actT_lo[:, k, 0:CAP],
                                          hi[:, r, n * 512:(n + 1) * 512], lo[:, r, n * 512:(n + 1) * 512],
                                          k == 0, k == KT - 1)
                    ins.then_inc(s["half_used"], 1)
                    if d == 1:
                        turn(b, GU_CHUNKS - 1)

            gathered(0)
            block_pe(0, True)
            with pe.Fori(1, BLOCKS) as b:
                with pe.If(b < T):
                    block_pe(b, False)

            pe.wait_ge(s["x_lo"], T + 1)
            pe.wait_ge(s["act_lo"], T * GU_CHUNKS)
            pe.wait_ge(s["y_copied"], T * 2)
            for i in range(TT):
                pe.wait_ge(s["un_ready"], i + 1)
                for k in range(KT):
                    ins = pe.transpose(bank[k][:, i * P:(i + 1) * P], un[:, i, k * P:(k + 1) * P], ident)
                    if i == TT - 1:
                        ins.then_inc(s["unT_ready"], 1)
            pe.wait_ge(s["uT_done_a"], KT // 2)
            pe.wait_ge(s["uT_done_v"], KT // 2)

            def p_tile(j):
                w = chunk2(pe, j // 4).rearrange("p (k c) -> p k c", k=KT)
                if 2 <= j < 6:
                    pe.wait_ge(s["p_evac_v"], j - 1)
                elif 6 <= j < 10:
                    pe.wait_ge(s["hsig_ready"], j - 1)
                elif 10 <= j < 14:
                    pe.wait_ge(s["p_evac_v"], j - 5)
                elif j >= 14:
                    pe.wait_ge(s["p_evac"], j - 13)
                c = (j % 4) * P
                accumulate(bank[j % 2][:, :], [(w[:, k, c:c + P], uT[:, k, :]) for k in range(KT)])\
                    .then_inc(s["p_ready"], 1)

            def level(n):
                if n == 0:
                    pe.wait_ge(s["fK_ready"], 1)
                else:
                    pe.wait_ge(s["lv_upd"], n)
                    pe.wait_ge(s["lv_copied"], n)
                for h in range(HG_HEADS):
                    q0 = h * S
                    if n <= TILE_LEVELS:
                        for j in range(TT):
                            at = q0 + j * P
                            ins = pe.matmul(bank[2 + h][:, j * P:(j + 1) * P], hK[:, at:at + P], hQ[:, at:at + P],
                                            start=True, stop=True)
                    elif n == TILE_LEVELS + 1:
                        for j in range(2):
                            at = q0 + 2 * j * P
                            ins = pe.matmul(bank[2 + h][:, j * P:(j + 1) * P], hK[:, at:at + P],
                                            hQ[:, at + P:at + 2 * P], start=True, stop=True)
                    else:
                        for j in range(2):
                            ins = pe.matmul(bank[2 + h][:, 2 * j * P:2 * (j + 1) * P],
                                            hK[:, q0 + j * P:q0 + (j + 1) * P], hQ[:, q0 + 2 * P:q0 + 4 * P],
                                            start=True, stop=True)
                ins.then_inc(s["lv_ready"], 1)

            for j in range(8):
                p_tile(j)
            for n in range(LEVELS + 1):
                level(n)
                p_tile(8 + n)
            p_tile(18)
            p_tile(19)
            for g in range(8):
                w = chunk2(pe, 5 + g // 4).rearrange("p (k c) -> p k c", k=KT)
                if g < 2:
                    pe.wait_ge(s["p_evac"], 7 + g)
                else:
                    pe.wait_ge(s["vt_evac"], g - 1)
                i = g % 4
                accumulate(bank[g % 2][:, :], [(uT[:, k, i * P:(i + 1) * P], w[:, k, :]) for k in range(KT)])\
                    .then_inc(s["vt_ready"], 1)

            pe.wait_ge(s["lv_copied"], LEVELS + 1)
            pe.wait_ge(s["vt_evac"], 8)

            def hgrn_out(h):
                if h >= 2:
                    pe.wait_ge(s["osq_ready"], h - 1)
                for j in range(TT):
                    ins = pe.matmul(bank[2 + h % 2][:, j * P:S], i_tok[:, j, h * P:(h + 1) * P], AT[:, h, j, j * P:S],
                                    start=(j == 0), stop=(j == TT - 1), skip_group_check=True)
                ins.then_inc(s["o_ready"], 1)

            def hgrn_ms(h):
                pe.wait_ge(s["osq_ready"], h + 1)
                if h >= 2:
                    pe.wait_ge(s["ostd_ready"], h - 1)
                accumulate(bank[4 + h % 2][:, :], [(ones, osq[:, h % 2, :])]).then_inc(s["oms_ready"], 1)

            hgrn_out(0)
            for h in range(HG_HEADS):
                if h + 1 < HG_HEADS:
                    hgrn_out(h + 1)
                hgrn_ms(h)

            pe.wait_ge(s["rot_done"], 8)
            pe.wait_ge(s["ostd_ready"], HG_HEADS)

            def scores(u):
                h, i = divmod(u, TT)
                lo = (h % 2) * DH
                m = h // 2
                if u >= 2:
                    pe.wait_ge(s["sc_done"], u - 1)
                pe.matmul(bank[u % 2][:, 0:(i + 1) * P], qkT[lo:lo + DH, m, i * P:(i + 1) * P],
                          qkT[lo:lo + DH, 4 + m, 0:(i + 1) * P], start=True, stop=True).then_inc(s["sc_ready"], 1)

            def probs_T(u):
                h, i = divmod(u, TT)
                pe.wait_ge(s["pn_ready"], u + 1)
                if i == 0 and h >= 1:
                    pe.wait_ge(s["pt_evac"], h)
                for j in range(i + 1):
                    ins = pe.transpose(bank[2 + j][:, i * P:(i + 1) * P], ex[:, u % 2, j * P:(j + 1) * P], ident)
                ins.then_inc(s["pt_ready"], 1)

            def head_values(h):
                lo = (h % 2) * DH
                pe.wait_ge(s["pt_evac"], h + 1)
                if h >= 2:
                    pe.wait_ge(s["pv_evac"], h - 1)
                for j in range(TT):
                    ins = pe.matmul(bank[6 + h % 2][lo:lo + DH, j * P:S], v_tok[:, j, h * DH:(h + 1) * DH],
                                    pTa[:, j, j * P:S], start=(j == 0), stop=(j == TT - 1), skip_group_check=True)
                ins.then_inc(s["pv_ready"], 1)

            scores(0)
            scores(1)
            for u in range(HEADS * TT):
                probs_T(u)
                if u + 2 < HEADS * TT:
                    scores(u + 2)
                if u % TT == TT - 1:
                    head_values(u // TT)

            pe.wait_ge(s["pv_evac"], HEADS)
            pe.wait_ge(s["hmix_ready"], HG_HEADS)
            pe.wait_ge(s["sc_done"], HEADS * TT)
            for g in range(2 * TT):
                i, n = divmod(g, 2)
                w = chunk2(pe, 7 + n).rearrange("p (k c) -> p k c", k=KT)
                if g >= 4:
                    pe.wait_ge(s["h3_ready"], g - 3)
                accumulate(bank[g % 4][:, :], [(mixed[:, k, i * P:(i + 1) * P], w[:, k, :]) for k in range(KT)])\
                    .then_inc(s["o2_ready"], 1)

            pe.wait_ge(s["h3_ready"], 2 * TT)
            for i in range(TT):
                pe.wait_ge(s["un3_ready"], i + 1)
                for k in range(KT):
                    ins = pe.transpose(bank[k][:, i * P:(i + 1) * P], un2[:, i, k * P:(k + 1) * P], ident)
                    if i == TT - 1:
                        ins.then_inc(s["unT3_ready"], 1)
            pe.wait_ge(s["u2T_done_a"], KT // 2)
            pe.wait_ge(s["u2T_done_v"], KT // 2)
            for f in range(FFN_T):
                w = chunk2(pe, 9 + f // 2).rearrange("p (k c) -> p k c", k=KT)
                if f >= 2:
                    pe.wait_ge(s["f_evac"], f - 1)
                for n in range(2):
                    c = (2 * n + f % 2) * P
                    accumulate(bank[2 * (f % 2) + n][:, :], [(w[:, k, c:c + P], u2T[:, k, :]) for k in range(KT)])\
                        .then_inc(s["f_ready"], 1)
            pe.wait_ge(s["f_evac"], FFN_T)
            for c in range(6):
                rows = 4 if c < 5 else FFN_T - 20
                w = chunk2(pe, 20 + c)[:, 0:rows * D].rearrange("p (k c) -> p k c", k=rows)
                for r in range(rows):
                    k = 4 * c + r
                    for i in range(TT):
                        for n in range(2):
                            ins = pe.matmul(bank[2 * i + n][:, :], fact[:, k, i * P:(i + 1) * P],
                                            w[:, r, n * 512:(n + 1) * 512], start=(k == 0), stop=(k == FFN_T - 1))
                ins.then_inc(s["fd_used"], 1)

        @block.vector
        def _(dve):
            step = Steps(dve, s["dve_steps"])

            def shifted_sum(out, buf, lo, shift, hi=P):
                return dve.tensor_tensor(out[lo:hi], buf[lo:hi, POOL_PAD:PP], buf[lo:hi, POOL_PAD - shift:PP - shift],
                                         ALU.add)

            dve.wait_ge(s["consts_in"], 16 * 9)
            dve.wait_ge(s["pads_ready"], 1)
            for i in range(NC_T):
                dve.wait_ge(s["z_evac"], 2 * i + 2)
                step(dve.tensor_tensor(upad[:, i, CONV_A - 1:CONV_A - 1 + S], z[:, AV[i], :], z[:, AG[i], :], ALU.mult))
                o = z[:, AV[i], :]
                for k in range(CONV_A):
                    w = pcol("conv_a_w", i * CONV_A + k)
                    if k == 0:
                        step(dve.tensor_scalar(o, upad[:, i, 0:S], w, None, ALU.mult))
                    else:
                        step(dve.scalar_tensor_tensor(o, upad[:, i, k:k + S], w, o, ALU.mult, ALU.add))
                dve.tensor_scalar(o, o, pcol("conv_a_b", i), None, ALU.add).then_inc(s["conv_ready"], 1)

            def short(i):
                dve.wait_ge(s["z_evac"], 8 + 2 * i)
                step(dve.tensor_tensor(cpad[:, i, CONV_B - 1:CONV_B - 1 + S], z[:, CG[i], :], z[:, BV[i], :], ALU.mult))
                o = z[:, CG[i], :]
                for k in range(CONV_B):
                    w = pcol("conv_b_w", i * CONV_B + k)
                    if k == 0:
                        step(dve.tensor_scalar(o, cpad[:, i, 0:S], w, None, ALU.mult))
                    else:
                        step(dve.scalar_tensor_tensor(o, cpad[:, i, k:k + S], w, o, ALU.mult, ALU.add))

            for i in range(NC_T):
                short(i)
            dve.wait_ge(s["asum_ready"], 1)
            step(dve.tensor_scalar(mu_a, bank[4][:, :], 1.0 / C_CONF, None, ALU.mult))
            for i in range(NC_T):
                dve.tensor_tensor(z[:, AV[i], :], z[:, AV[i], :], mu_a, ALU.subtract).then_inc(s["mean_ready"], 1)
            dve.wait_ge(s["std_ready"], 1)
            step(dve.reciprocal(rs_a, rs_a))
            for i in range(NC_T):
                step(dve.tensor_tensor(z[:, AV[i], :], z[:, AV[i], :], rs_a, ALU.mult))
                dve.tensor_scalar(z[:, AV[i], :], z[:, AV[i], :], pcol("ln_a_g", i), pcol("ln_a_b", i), ALU.mult, ALU.add)\
                   .then_inc(s["ln_a_ready"], 1)
            for i in range(NC_T):
                dve.wait_ge(s["z_evac"], BG[i] + 1)
                step.mark(dve.tensor_tensor(z[:, BG[i], :], z[:, BG[i], :], z[:, CG[i], :], ALU.mult))

            for i in range(2):
                win, src, dst = pwin[:, i, :], ppad[:, i, :], z[:, PL[i], :]
                dve.wait_ge(s["z_evac"], PL[i] + 1)
                step(shifted_sum(win[:, POOL_PAD:PP], src, 0, 1))
                if i == 1:
                    four = upad[:, 0, :]
                    step(shifted_sum(four[:, POOL_PAD:PP], win, 0, 2))
                    step(shifted_sum(win[:, POOL_PAD:PP], four, 0, 4))
                step(shifted_sum(dst, win, P // 2, 2 if i == 0 else 8))
                step.mark(dve.tensor_tensor(dst[0:P // 2], win[0:P // 2, POOL_PAD:PP], invcnt[0:P // 2, i, :], ALU.mult))
                step(dve.tensor_tensor(dst[P // 2:P], dst[P // 2:P], invcnt[P // 2:P, i, :], ALU.mult))
                dve.tensor_tensor(dst, dst, src[:, POOL_PAD:PP], ALU.subtract).then_inc(s["pool_in_ready"], 1)
            for i in range(NC_T):
                dve.wait_ge(s["sgl_ready"], i + 1)
                dve.tensor_tensor(z[:, AV[i], :], z[:, AV[i], :], z[:, AG[i], :], ALU.mult).then_inc(s["mixT_ready"], 1)

            dve.wait_ge(s["xtok_in"], 16)

            def row_stats(i, src, ready):
                for q in range(2):
                    step.mark(dve.bn_stats(stats[:, q, :], src[:, q * 512:(q + 1) * 512]))
                step.wait()
                dve.bn_aggr(mva[:, i, :], stats[:, :, :].rearrange("p a b -> p (a b)")).then_inc(ready, 1)

            for i in range(TT):
                for n in range(2):
                    g = 2 * i + n
                    dve.wait_ge(s["mix_ready"], g + 1)
                    part = hn[:, i, n * 512:(n + 1) * 512]
                    dve.scalar_tensor_tensor(part, part, ALPHA, bank[g % 4][:, :], ALU.mult, ALU.add)\
                       .then_inc(s["mix_evac"], 1)
                dve.wait_ge(s["mix_evac"], 2 * i + 2)
                row_stats(i, hn[:, i, :], s["v1_ready"])
                dve.wait_ge(s["s1_ready"], i + 1)
                step(dve.reciprocal(rstd[:, i:i + 1], rstd[:, i:i + 1]))
                dve.tensor_scalar(hn[:, i, :], hn[:, i, :], mva[:, i, 0:1], rstd[:, i:i + 1], ALU.subtract, ALU.mult)\
                   .then_inc(s["hn_ready"], 1)
            for k in range(1, KT, 2):
                dve.wait_ge(s["hnT_ready"], k + 1)
                dve.tensor_scalar(hT[:, k, :], bank[k][:, :], pcol("ln1_g", k), pcol("ln1_b", k), ALU.mult, ALU.add)\
                   .then_inc(s["hT_done_v"], 1)

            dve.wait_ge(s["router_ready"], 1)
            step(dve.tensor_tensor(logit, bank[0][:, 0:TT * E].rearrange("p (i e) -> p i e", i=TT),
                                   rb[:, :].unsqueeze(1).broadcast_to([P, TT, E]), ALU.add))
            for i in range(TT):
                step(dve.max(mv8[:, i, :], logit[:, i, :]))
                step(dve.max_index(mi8[:, i, :], mv8[:, i, :], logit[:, i, :]))
            step(dve.tensor_copy(mif[:, :, :], mi8[:, :, :]))
            step(dve.tensor_tensor(oh, eiota[:, :].unsqueeze(1).unsqueeze(1).broadcast_to([P, TT, TOPK, E]),
                                   mif[:, :, 0:TOPK].unsqueeze(3).broadcast_to([P, TT, TOPK, E]), ALU.is_equal))
            dve.tensor_reduce(mask, oh.rearrange("p i k e -> p i e k"), AX.X, ALU.add).then_inc(s["mask_ready"], 1)
            dve.tensor_tensor(gate[:, :, :], mv8[:, :, 0:TOPK], mv8[:, :, 0:1].broadcast_to([P, TT, TOPK]), ALU.subtract)\
               .then_inc(s["e_ready"], 1)
            dve.wait_ge(s["ex_ready"], 1)
            step(dve.tensor_reduce(gsum[:, :], gate[:, :, :], AX.X, ALU.add))
            step(dve.reciprocal(gsum[:, :], gsum[:, :]))
            step(dve.tensor_tensor(gate[:, :, :], gate[:, :, :], gsum[:, :].unsqueeze(2).broadcast_to([P, TT, TOPK]),
                                   ALU.mult))
            step(dve.tensor_tensor(ohw, oh, gate[:, :, :].unsqueeze(3).broadcast_to([P, TT, TOPK, E]), ALU.mult))
            dve.tensor_reduce(gmat, ohw.rearrange("p i k e -> p i e k"), AX.X, ALU.add).then_inc(s["gm_ready"], 1)

            dve.wait_ge(s["pos_ready"], 1)
            count, nblk, end, first_slot = (cnt[:, n, :] for n in range(4))
            step(dve.tensor_copy(count, bank[5][:, TT * E:(TT + 1) * E]))
            step(dve.tensor_scalar(nblk, count, 0.0, None, ALU.is_gt))
            for m in range(1, MAX_PER_EXPERT):
                step(dve.scalar_tensor_tensor(nblk, count, float(m * CAP), nblk, ALU.is_gt, ALU.add))
            step(dve.tensor_tensor_scan(end, ones[:, 0:E], nblk, 0.0, ALU.mult, ALU.add))
            step(dve.tensor_tensor(first_slot, end, nblk, ALU.subtract))
            step(dve.tensor_scalar(first_slot, first_slot, float(CAP), None, ALU.mult))
            step(dve.tensor_tensor(pos, bank[5][:, 0:TT * E].rearrange("p (i e) -> p i e", i=TT),
                                   first_slot.unsqueeze(1).broadcast_to([P, TT, E]), ALU.add))
            dve.wait_ge(s["gm_ready"], 1)
            step(dve.tensor_tensor(ohw, oh, pos.unsqueeze(2).broadcast_to([P, TT, TOPK, E]), ALU.mult))
            step(dve.tensor_reduce(destf[:, :].rearrange("p (i k) -> p i k", i=TT), ohw, AX.X, ALU.add))
            whole = small[:, 0:TT * TOPK]
            step(dve.tensor_scalar(whole, destf[:, :], 1.0 / CAP, 0.5 / CAP - 0.5, ALU.mult, ALU.add))
            step(dve.tensor_scalar(whole, whole, 12582912.0, None, ALU.add))
            step(dve.tensor_scalar(whole, whole, 12582912.0, None, ALU.subtract))
            step(dve.tensor_scalar(whole, whole, float(1 - CAP * (BLOCKS + 1)), None, ALU.mult))
            step(dve.scalar_tensor_tensor(destf[:, :], destf[:, :], float(BLOCKS + 1), whole, ALU.mult, ALU.add))
            dve.tensor_copy(dest[:, :], destf[:, :]).then_inc(s["dest_ready"], 1)
            be = cmp_be.rearrange("p (b e) -> p b e", e=E)
            step(dve.tensor_tensor(be, end.unsqueeze(1).broadcast_to([P, NB_META, E]),
                                   blockid[:, 0:NB_META].unsqueeze(2).broadcast_to([P, NB_META, E]), ALU.is_le))
            step(dve.tensor_reduce(metaf[:, 0:NB_META], be, AX.X, ALU.add))
            step(dve.tensor_scalar(metaf[:, 0:NB_META], metaf[:, 0:NB_META], float(E - 1), None, ALU.min))
            step(dve.tensor_scalar(sel_all, metaf[:, 0:NB_META], pcol("expert"), None, ALU.is_equal))
            dve.tensor_copy(meta[0:1, 0:NB_META], metaf[0:1, 0:NB_META]).then_inc(s["meta_ready"], 1)
            step(dve.tensor_scalar(metaf[0:1, META_LAST:META_LAST + 1], end[0:1, E - 1:E], -1.0, None, ALU.add))
            dve.tensor_copy(meta[0:1, META_LAST:META_LAST + 1], metaf[0:1, META_LAST:META_LAST + 1])\
               .then_inc(s["meta_ready"], 1)
            dve.tensor_copy(meta[0:1, META_T:META], end[0:1, E - 1:E]).then_inc(s["meta_ready"], 1)

            dve.wait_ge(s["h_out"], 16 * TT)
            for g in range(2 * TT):
                i, n = divmod(g, 2)
                part = acc[:, i, n * 512:(n + 1) * 512]
                dve.wait_ge(s["sg_ready"], g + 1)
                dve.wait_ge(s["plep_ready"], g + 1)
                dve.tensor_tensor(plet, sgate[:, g % 2, :], bank[3 + g % 2][:, :], ALU.mult).then_inc(s["ple_evac"], 1)
                dve.wait_ge(s["ple_evac"], g + 1)
                dve.wait_ge(s["h_ready"], 2 * i + 2)
                step(dve.scalar_tensor_tensor(part, part, ALPHA, plet, ALU.mult, ALU.add))
            for g in range(2 * TT):
                i, n = divmod(g, 2)
                part = acc[:, i, n * 512:(n + 1) * 512]
                dve.wait_ge(s["bdn_ready"], g + 1)
                dve.tensor_tensor(part, part, bank[7 * (g % 2)][:, :], ALU.add).then_inc(s["bdn_done"], 1)

            dve.wait_ge(s["bias_hi"], 1)
            dve.tensor_tensor(bias_tab[E:2 * E, :], braw[E:2 * E, :], bias_tab[E:2 * E, :].bitcast(F32), ALU.subtract)\
               .then_inc(s["bias_split"], 1)

            dve.wait_ge(s["meta_ready"], 3)
            T = dve.value_load(meta[0:1, META_T:META_T + 1], min_val=LEAST_BLOCKS, max_val=BLOCKS)
            last = dve.value_load(meta[0:1, META_LAST:META_LAST + 1], min_val=LEAST_BLOCKS - 1, max_val=BLOCKS - 1)

            def split_lo(b, i):
                if not split_by_pool(i):
                    dve.wait_ge(s["hi_done"], b * HALVES + (i + 1))
                    dve.tensor_tensor(w_lo[i % PAIRS], raw_w[i % RAW], w_hi[i % PAIRS].bitcast(F32), ALU.subtract)\
                       .then_inc(s["lo_dve"], 1)

            def gathered_lo(b):
                dve.wait_ge(s["x_hi"], b + 1)
                for q in range(2):
                    ins = dve.tensor_tensor(xT_lo[:, 4 * q:4 * q + 4, 0:CAP],
                                            bank[4 + q][:, 0:4 * CAP].rearrange("p (k s) -> p k s", k=4),
                                            xT_hi[:, 4 * q:4 * q + 4, 0:CAP].bitcast(F32), ALU.subtract)
                ins.then_inc(s["x_lo"], 1)

            def turned_lo(b, c):
                dve.wait_ge(s["act_hi"], b * GU_CHUNKS + (c + 1))
                dve.tensor_tensor(actT_lo[:, 2 * c:2 * c + 2, 0:CAP],
                                  bank[2 + c % 2][:, 0:2 * CAP].rearrange("p (k s) -> p k s", k=2),
                                  actT_hi[:, 2 * c:2 * c + 2, 0:CAP].bitcast(F32), ALU.subtract)\
                   .then_inc(s["act_lo"], 1)

            def gates(b, c):
                own = Steps(dve, s["moe_dve"], b * (2 * GU_CHUNKS) + 2 * c)
                gu, ug = gu_sb[0:CAP, c % 2, :], ug_sb[0:CAP, c % 2, :]
                dve.wait_ge(s["half_used"], b * HALVES + (2 * c + 2))
                dve.tensor_scalar(gu, bank[c % 2][0:CAP, :], LIMIT, None, ALU.min).then_inc(s["evac_done"], 1)
                dve.wait_ge(s["evac_done"], b * GU_CHUNKS + (c + 1))
                own(dve.tensor_scalar(ug, gu[:, 256:512], -LIMIT, 1.0, ALU.max, ALU.add))
                own.mark(dve.tensor_tensor(ug, ug, gu[:, 0:256], ALU.mult))

            def activations(b, c):
                dve.wait_ge(s["moe_dve"], b * (2 * GU_CHUNKS) + 2 * c + 2)
                dve.wait_ge(s["sig_done"], b * GU_CHUNKS + (c + 1))
                dve.tensor_tensor(act_sb[0:CAP, c % 2, :], ug_sb[0:CAP, c % 2, :], sig_sb[0:CAP, c % 2, :], ALU.mult)\
                   .then_inc(s["act_ready"], 1)

            def first_part(b):
                for i in range(9):
                    if i >= 2 and i % 2 == 0:
                        gates(b, i // 2 - 1)
                    split_lo(b, i + 3)
                    if i >= 2 and i % 2 == 0:
                        activations(b, i // 2 - 1)
                    if i >= 4 and i % 2 == 0:
                        turned_lo(b, i // 2 - 2)
                gathered_lo(b + 1)

            for i in range(3):
                split_lo(0, i)
            gathered_lo(0)
            first_part(0)
            with dve.Fori(1, BLOCKS) as b:
                with dve.If(b < T):
                    split_lo(b, 0)
                    turned_lo(b - 1, GU_CHUNKS - 1)
                    split_lo(b, 1)
                    split_lo(b, 2)
                    first_part(b)
            turned_lo(last, GU_CHUNKS - 1)

            for c in range(TT * TOPK):
                i, k = divmod(c, TOPK)
                dve.wait_ge(yk_in[i], 16)
                if c > 0:
                    dve.wait_ge(s["yg_used"], c)
                dve.scalar_tensor_tensor(acc[:, i, :], yk[i][:, k, :], gate[:, i, k:k + 1], acc[:, i, :], ALU.mult, ALU.add)\
                   .then_inc(s["yg_used"], 1)

            for i in range(TT):
                dve.wait_ge(s["yg_used"], TOPK * (i + 1))
                row_stats(i, acc[:, i, :], s["v2_ready"])
                if i == 0:
                    dve.wait_ge(s["ln2_rows_in"], 32)
                dve.wait_ge(s["v2_ready"], i + 1)
                dve.scalar_tensor_tensor(acc[:, i, :], acc[:, i, :], mva[:, i, 0:1], rowvec[:, 0:D], ALU.subtract, ALU.mult)\
                   .then_inc(s["x2_ready"], 1)
                dve.wait_ge(s["s2_ready"], i + 1)
                step(dve.reciprocal(rstd[:, i:i + 1], rstd[:, i:i + 1]))
                dve.wait_ge(s["x2_ready"], 2 * i + 1)
                dve.scalar_tensor_tensor(h2[:, i, :], acc[:, i, :], rstd[:, i:i + 1], rowvec[:, D:2 * D], ALU.mult, ALU.add)\
                   .then_inc(s["x2_ready"], 1)
                dve.wait_ge(s["ss_ready"], 2 * i + 2)
                step(dve.reciprocal(rstd[:, 4 + i:5 + i], rstd[:, 4 + i:5 + i]))
                dve.tensor_scalar(un[:, i, :], h2[:, i, :], rstd[:, 4 + i:5 + i], None, ALU.mult).then_inc(s["un_ready"], 1)
            for k in range(1, KT, 2):
                dve.wait_ge(s["unT_ready"], k + 1)
                dve.tensor_scalar(uT[:, k, :], bank[k][:, :], pcol("norm1", k), None, ALU.mult).then_inc(s["uT_done_v"], 1)

            H4 = HG_HEADS
            l0, l1 = par[:, PAR["lb"]:PAR["lb"] + H4], par[:, PAR["lb"] + H4:PAR["lb"] + 2 * H4]
            e0, e1, top, lb, lb1 = (small[:, n * H4:(n + 1) * H4] for n in range(5))
            step(dve.tensor_tensor(top, l0, l1, ALU.max))
            step(dve.tensor_tensor(e0, l0, top, ALU.subtract))
            dve.tensor_tensor(e1, l1, top, ALU.subtract).then_inc(s["lb_ready"], 1)
            dve.wait_ge(s["lbe_ready"], 1)
            step(dve.tensor_tensor(top, e0, e1, ALU.add))
            step(dve.reciprocal(top, top))
            step(dve.tensor_tensor(lb, e0, top, ALU.mult))
            step(dve.tensor_tensor(lb1, e1, top, ALU.mult))

            for j in range(4):
                part = hQ[:, j * S:(j + 1) * S]
                dve.wait_ge(s["hsig_ready"], j + 1)
                dve.tensor_tensor(part, part, bank[j % 2][:, :], ALU.mult).then_inc(s["p_evac_v"], 1)
            step.mark(dve.memset(AT, 0.0))
            for j in range(4):
                part = hF[:, j * S:(j + 1) * S]
                dve.wait_ge(s["hsig_ready"], 5 + j)
                step(dve.tensor_scalar(part, part, lb1[:, j:j + 1], lb[:, j:j + 1], ALU.mult, ALU.add))
                ins = dve.tensor_scalar(hK[:, j * S:(j + 1) * S], part, -1.0, 1.0, ALU.mult, ALU.add)
            ins.then_inc(s["fK_ready"], 1)

            def rotate(m):
                dve.wait_ge(s["p_evac"], m + 1)
                if m == 0:
                    dve.wait_ge(s["c2_in"], 32)
                step.mark(dve.tensor_tensor(qkT[:, m, :], raw[:, m % 2, :], cosT, ALU.mult))
                dve.wait_ge(swap_in[m % 2], 64 * (m // 2 + 1))
                step(dve.tensor_tensor(swp[:, m % 2, :], swp[:, m % 2, :], sinT, ALU.mult))
                dve.tensor_tensor(qkT[:, m, :], qkT[:, m, :], swp[:, m % 2, :], ALU.add).then_inc(s["rot_done"], 1)

            for n in range(LEVELS + 1):
                dve.wait_ge(s["lv_ready"], n + 1)
                if n == 0:
                    dve.wait_ge(s["fK_ready"], 1)
                    dve.tensor_tensor(hQ, hQ, hF, ALU.mult).then_inc(s["lv_upd"], 1)
                    dve.wait_ge(s["c2_in"], 32)
                elif n < LEVELS:
                    L = 1 << (n - 1)
                    qv = hQ.rearrange("p (n a l) -> p n a l", a=2, l=L)
                    kv = hK.rearrange("p (n a l) -> p n a l", a=2, l=L)
                    tv = tot[n - 1].rearrange("p (n a) -> p n a", a=2)
                    N = HG_HEADS * S // (2 * L)
                    dve.wait_ge(s["lv_upd"], n)
                    step.mark(dve.tensor_tensor(tot[n], tv[:, :, 0], tv[:, :, 1], ALU.mult))
                    step.mark(dve.tensor_tensor(qv[:, :, 1, :], qv[:, :, 1, :],
                                                tv[:, :, 0:1].broadcast_to([P, N, L]), ALU.mult))
                    dve.tensor_tensor(kv[:, :, 0, :], kv[:, :, 0, :], tv[:, :, 1:2].broadcast_to([P, N, L]), ALU.mult)\
                       .then_inc(s["lv_upd"], 1)
                    step.wait()
                for h in range(HG_HEADS):
                    src = bank[2 + h]
                    if n <= TILE_LEVELS:
                        diag = AT[:, h, :, :].rearrange("p j t -> p (j t)")
                        for j in range(TT):
                            at = j * (S + P)
                            ins = dve.copy_predicated(diag[:, at:at + P], lmask[:, n, :], src[:, j * P:(j + 1) * P])
                    elif n == TILE_LEVELS + 1:
                        for j in range(2):
                            ins = dve.tensor_copy(AT[:, h, 2 * j, (2 * j + 1) * P:(2 * j + 2) * P],
                                                  src[:, j * P:(j + 1) * P])
                    else:
                        ins = dve.tensor_copy(AT[:, h, 0:2, 2 * P:4 * P], src[:, :].rearrange("p (j t) -> p j t", j=2))
                ins.then_inc(s["lv_copied"], 1)
                if n < 4:
                    dve.wait_ge(s["hsig_ready"], 9 + n)
                    dve.tensor_tensor(hG[:, n, :], hG[:, n, :], bank[n % 2][:, :], ALU.mult).then_inc(s["p_evac_v"], 1)
                if n >= 5:
                    rotate(n - 5)
            for m in range(5, 8):
                rotate(m)

            for h in range(HG_HEADS):
                dve.wait_ge(s["ostd_ready"], h + 1)
                step(dve.reciprocal(osq[:, h % 2, :], osq[:, h % 2, :]))
                step(dve.tensor_tensor(o_sb[:, h % 2, :], o_sb[:, h % 2, :], osq[:, h % 2, :], ALU.mult))
                dve.scalar_tensor_tensor(mixed[:, 4 + h, :], o_sb[:, h % 2, :], pcol("hg_norm", h), hG[:, h, :],
                                         ALU.mult, ALU.mult).then_inc(s["hmix_ready"], 1)

            def masked(u):
                i = u % TT
                w = (i + 1) * P
                a2 = u % 2
                dve.wait_ge(s["sc_ready"], u + 1)
                step(dve.tensor_tensor_reduce(sc[:, a2, 0:w], bank[a2][:, 0:w], madd[:, S - w:S], 1.0, NEG * 4,
                                              ALU.add, ALU.max, att_s[:, a2:a2 + 1]))
                dve.tensor_scalar(att_s[:, 4 + a2:5 + a2], att_s[:, a2:a2 + 1], -SCALE, None, ALU.mult)\
                   .then_inc(s["sc_done"], 1)

            def weighted(u):
                i = u % TT
                w = (i + 1) * P
                a2 = u % 2
                dve.wait_ge(s["e2_ready"], u + 1)
                step(dve.tensor_tensor_reduce(ex[:, a2, 0:w], ex[:, a2, 0:w], ctab[:, S - w:S], 1.0, 0.0,
                                              ALU.mult, ALU.add, att_s[:, 2 + a2:3 + a2]))
                step(dve.reciprocal(att_s[:, 2 + a2:3 + a2], att_s[:, 2 + a2:3 + a2]))
                dve.tensor_scalar(ex[:, a2, 0:w], ex[:, a2, 0:w], att_s[:, 2 + a2:3 + a2], None, ALU.mult)\
                   .then_inc(s["pn_ready"], 1)

            masked(0)
            for u in range(HEADS * TT):
                if u + 1 < HEADS * TT:
                    masked(u + 1)
                weighted(u)

            for i in range(TT):
                for n in range(2):
                    g = 2 * i + n
                    dve.wait_ge(s["o2_ready"], g + 1)
                    part = h2[:, i, n * 512:(n + 1) * 512]
                    dve.tensor_tensor(part, part, bank[g % 4][:, :], ALU.add).then_inc(s["h3_ready"], 1)
                dve.wait_ge(s["ss3_ready"], 2 * i + 2)
                step(dve.reciprocal(rstd[:, i:i + 1], rstd[:, i:i + 1]))
                dve.tensor_scalar(un2[:, i, :], h2[:, i, :], rstd[:, i:i + 1], None, ALU.mult).then_inc(s["un3_ready"], 1)
            for k in range(1, KT, 2):
                dve.wait_ge(s["unT3_ready"], k + 1)
                dve.tensor_scalar(u2T[:, k, :], bank[k][:, :], pcol("norm2", k), None, ALU.mult).then_inc(s["u2T_done_v"], 1)

            for f in range(FFN_T):
                dve.wait_ge(s["fs_ready"], f + 1)
                step(dve.tensor_tensor(fsig[:, f % 2, :], fsig[:, f % 2, :], bank[2 * (f % 2)][:, :], ALU.mult))
                dve.wait_ge(s["f_ready"], 2 * f + 2)
                dve.tensor_tensor(fact[:, f, :], fsig[:, f % 2, :], bank[2 * (f % 2) + 1][:, :], ALU.mult)\
                   .then_inc(s["f_evac"], 1)

            dve.wait_ge(s["fd_used"], 6)
            dve.wait_ge(s["fin_row_in"], 16)
            for i in range(TT):
                for n in range(2):
                    part = h2[:, i, n * 512:(n + 1) * 512]
                    dve.tensor_tensor(part, part, bank[2 * i + n][:, :], ALU.add).then_inc(s["h4_ready"], 1)
            for i in range(TT):
                dve.wait_ge(s["ss4_ready"], 2 * i + 2)
                step(dve.reciprocal(rstd[:, 4 + i:5 + i], rstd[:, 4 + i:5 + i]))
                dve.scalar_tensor_tensor(outt[:, i, :], h2[:, i, :], rstd[:, 4 + i:5 + i], rowvec[:, 0:D], ALU.mult, ALU.mult)\
                   .then_inc(s["out_ready"], 1)



def constants():
    f = np.float32
    p = np.arange(P)
    c = {}
    c["cst"] = np.concatenate([np.eye(P), np.ones((P, P)), p[:, None] < p[None, :]], axis=1).astype(f)
    t = np.arange(S)
    windows = np.repeat([[2, 4], [8, 16]], P // 2, axis=1).reshape(2, P)
    c["invcnt"] = (1.0 / np.minimum(t[None, None, :] + 1, windows.T[:, :, None])).astype(f).reshape(P, 2 * S)
    c["eiota"] = np.arange(E, dtype=f)[None, :]
    token = (p[:, None, None] + P * np.arange(TT)[None, :, None]) + np.zeros((1, 1, TOPK), int)
    c["pairs"] = np.stack([token + S * np.arange(TOPK), token], axis=-1).reshape(P, -1).astype(np.int32)
    c["expert"] = np.where(p < 2 * E, p % E, -1).astype(f)[:, None]
    c["blockid"] = np.arange(META, dtype=f)[None, :]
    delta = p[:, None] + (TT - 1) * P - t[None, :]
    count = np.zeros((P, S))
    for window, dilation in ((128, 1), (512, 4), (2048, 16)):
        count += (delta >= 0) & (delta <= window) & (delta % dilation == 0)
    half = DH // 2
    inv_freq = (f(10000.0) ** (-np.arange(half, dtype=f) / f(half))).astype(f)
    ang = (t.astype(f)[None, :] * inv_freq[p % half][:, None]).astype(f).astype(np.float64)
    sign = np.where(p % DH < half, -1.0, 1.0)[:, None]
    c["c2"] = np.concatenate([count, np.where(count > 0, 0.0, NEG), np.cos(ang), sign * np.sin(ang)], axis=1).astype(f)
    levels = [np.eye(P)]
    for n in range(TILE_LEVELS):
        L = 1 << n
        levels.append((p[:, None] // (2 * L) == p[None, :] // (2 * L)) & (p[:, None] // L % 2 == 0) & (p[None, :] // L % 2 == 1))
    c["lmask"] = np.concatenate(levels, axis=1).astype(np.int32)
    return c


def kernel(**inputs):
    import concourse.bacc as _bacc
    from concourse.bass_utils import run_bass_kernel_spmd as _run

    x = {k: np.asarray(val) for k, val in inputs.items()}

    def cols(w, tiles):
        w = w.reshape(w.shape[0] // P, P, -1, P)[:, :, tiles, :]
        return w.transpose(1, 0, 2, 3).reshape(P, -1)

    def per_channel(w):
        n = w.shape[0]
        return w.reshape(n, -1, P).transpose(2, 1, 0).reshape(P, -1)

    def pack(chunks):
        out = np.zeros((len(chunks), P, CH), np.float32)
        for n, c in enumerate(chunks):
            out[n, :, 0:c.shape[1]] = c
        return out

    w_in = x["w_in"][0]
    order = [0, 3, 1, 4, 2, 5, 9, 12, 10, 13, 11, 14, 6, 7, 8, 15, 16]
    w_out = x["w_out"][0]
    pg, pp = x["ple_w_gate"][0], x["ple_w_proj"][0]
    arrays = {}
    arrays["wd"] = pack([cols(w_in, order[4 * n:4 * n + 4]) for n in range(5)]
                        + [cols(w_out, list(range(4 * n, 4 * n + 4))) for n in range(2)]
                        + [cols(pg, list(range(4 * n, 4 * n + 4))) for n in range(2)]
                        + [cols(pp, list(range(8)))])
    gu = x["w_gate_up"][0].reshape(E, 2, 4, P, 2, GU_CHUNKS, 2, P)
    gu = gu.transpose(0, 5, 1, 3, 2, 4, 6, 7).reshape(E, 2 * GU_CHUNKS, P, HW)
    dn = x["w_down"][0].reshape(E, GU_CHUNKS, 2, P, D).transpose(0, 1, 3, 2, 4).reshape(E, GU_CHUNKS, P, HW)
    arrays["wmoe"] = np.concatenate([gu, dn], axis=1)
    w2 = x["w_in_2_2"][0] if "w_in_2_2" in x else x["w_in_2"][0]
    g2 = x["w_gate_up_2"][0]
    d2 = x["w_down_2"][0].reshape(FFN_T, P, D).transpose(1, 0, 2)
    arrays["wp"] = pack([cols(w2, list(range(a, a + 4))) for a in (12, 16, 24, 0, 4, 8, 20)]
                        + [cols(x["w_out_2"][0], list(range(4 * n, 4 * n + 4))) for n in range(2)]
                        + [cols(g2, [2 * n, 2 * n + 1, FFN_T + 2 * n, FFN_T + 2 * n + 1]) for n in range(FFN_T // 2)]
                        + [d2[:, 4 * n:4 * n + 4].reshape(P, -1) for n in range(6)])
    c = constants()
    arrays["par"] = np.concatenate(
        [per_channel(x["conv_a_w"][0]), per_channel(x["conv_a_b"]), per_channel(x["ln_a_g"]), per_channel(x["ln_a_b"]),
         per_channel(x["conv_b_w"][0]), per_channel(x["pool_scale"]), per_channel(x["ln1_g"]), per_channel(x["ln1_b"]),
         per_channel(x["norm1_w_2"]), per_channel(x["norm2_w_2"]), per_channel(x["hgrn_norm_w_2"]),
         per_channel(x["lb_logits_2"][0:1]), per_channel(x["lb_logits_2"][1:2]),
         np.tile(np.array([[LN_EPS, NORM_EPS]], np.float32), (P, 1)), c.pop("expert")], axis=1)
    poolw = np.zeros((2, P, P), np.float32)
    for g in range(4):
        lo = (g % 2) * 64
        poolw[g // 2, lo:lo + 64, lo:lo + 64] = x["pool_w"][0, g]
    arrays["poolw"] = poolw.transpose(1, 0, 2).reshape(P, 2 * P)
    arrays["rw"] = x["router_w"][0].reshape(KT, P, E).transpose(1, 0, 2).reshape(P, KT * E)
    arrays["rb"] = x["router_b"]
    arrays["rows"] = np.concatenate([x["ln1_g"], x["ln1_b"], x["ln2_g"], x["ln2_b"], x["final_norm_w_2"][None]], axis=0)
    arrays["xT"] = x["x"][0].reshape(S, KT, P).transpose(2, 1, 0).reshape(P, KT * S)
    arrays["xtok"] = x["x"][0].reshape(TT, P, D).transpose(1, 0, 2).reshape(P, TT * D)
    arrays["pT"] = x["p"][0, 0].reshape(S, 2, P).transpose(2, 1, 0).reshape(P, 2 * S)
    bgu = np.zeros((P, 4 * 512), np.float32)
    bgu[0:E] = bgu[E:2 * E] = x["b_gate_up"][0].reshape(E, 2, GU_CHUNKS, 256).transpose(0, 2, 1, 3).reshape(E, -1)
    arrays["bgu"] = bgu
    arrays["bdn"] = x["b_down"][0]
    arrays.update(c)

    nc = _bacc.Bacc("TRN2", target_bir_lowering=False, num_devices=1)
    handles = {}
    arrays = {f"in_{k}": np.ascontiguousarray(val) for k, val in arrays.items()}
    for k, val in arrays.items():
        handles[k[3:]] = nc.dram_tensor(k, val.shape, mybir.dt.from_np(val.dtype), kind="ExternalInput").ap()
    handles["out"] = nc.dram_tensor("out_0", (S, D), F32, kind="ExternalOutput").ap()
    build(nc, handles)
    r = _run(nc, [arrays], core_ids=[0])
    return r.results[0]["out_0"].reshape(1, S, D)
```

```python
from contextlib import ExitStack

import numpy as np

import concourse.bass as bass
from concourse import mybir

ALU = mybir.AluOpType
ACT = mybir.ActivationFunctionType
AX = mybir.AxisListType
F32 = mybir.dt.float32
F32R = mybir.dt.float32r
I32 = mybir.dt.int32
U32 = mybir.dt.uint32

P = 128
S = 512
D = 1024
KT = D // P
TT = S // P
C_CONF = 384
NC_T = C_CONF // P
D_POOL = 256
CONV_A = 31
CONV_B = 3
POOL_PAD = 16
E = 32
TOPK = 4
ALPHA = float(2 ** 0.25)
LN_EPS = 1e-5
NORM_EPS = 1e-6
LIMIT = 7.0
SW_ALPHA = 1.702

CAP = 96
BLOCKS = (S * TOPK + E * (CAP - 1)) // CAP
TABLE = BLOCKS + 2
LEAST_BLOCKS = -(-S * TOPK // CAP)
MAX_PER_EXPERT = -(-S // CAP)
META = 64
NB_META = 56
META_T = META - 1
NO_ROW = 2 * TOPK * S
META_LAST = META - 2
GU_CHUNKS = 4
HALVES = 3 * GU_CHUNKS
RAW = 6
PAIRS = 4

HEADS = 8
DH = 64
SCALE = DH ** -0.5
HG_HEADS = 4
LEVELS = 9
AHEAD = 4
TILE_LEVELS = 7
FFN = 2816
FFN_T = FFN // P
NEG = -1.0e30

RING = 6
CH = 4096
HW = CH // 2
PRE = 10
PRE_SLOT = [0, 1, 2, 3, 4, 5, 3, 4, 5, 3]
RING2 = 3
POST = 9
FFN_HALVES = FFN_T + FFN_T // 2
FRAW = 3
FPAIRS = 3

PAR = {}
_at = 0
for _name, _n in (("conv_a_w", NC_T * CONV_A), ("conv_a_b", NC_T), ("ln_a_g", NC_T), ("ln_a_b", NC_T),
                  ("conv_b_w", NC_T * CONV_B), ("pool_scale", 2), ("ln1_g", KT), ("ln1_b", KT),
                  ("norm1", KT), ("norm2", KT), ("hg_norm", HG_HEADS), ("lb", 2 * HG_HEADS),
                  ("eps", 2), ("expert", 1)):
    PAR[_name] = _at
    _at += _n
N_PAR = _at


class Steps:

    def __init__(self, eng, sem, base=0):
        self.eng, self.sem, self.base, self.n = eng, sem, base, 0

    def __call__(self, ins):
        self.mark(ins)
        self.wait()

    def mark(self, ins):
        ins.then_inc(self.sem, 1)
        self.n += 1

    def wait(self):
        self.eng.wait_ge(self.sem, self.base + self.n)


def build(nc, a):
    ctx = ExitStack()
    with ctx:
        def sb(name, shape, dt=F32):
            return ctx.enter_context(nc.sbuf_tensor(name, shape, dt))

        def sem(name):
            return ctx.enter_context(nc.semaphore(name))

        with nc.sbuf_tensor("ring_r", [P, RING * CH], F32R) as ring_r, nc.sbuf_tensor("room_r", [P, 24576], F32R) as room_r:
            pass
        ring = sb("ring", [P, RING * CH])
        room = sb("room", [P, 24576])
        rowvec = sb("rowvec", [P, 2 * D])
        par = sb("par", [P, N_PAR])
        cst = sb("cst", [P, 3 * P])
        poolw = sb("poolw", [P, 2, P])
        rw = sb("rw", [P, KT, E])
        rb = sb("rb", [P, E])
        eiota = sb("eiota", [P, E])
        pairs = sb("pairs", [P, TT * TOPK * 2], U32)
        blockid = sb("blockid", [P, META])
        meta = sb("meta", [1, META], I32)
        small = sb("small", [P, 128])
        bank = [ctx.enter_context(nc.psum_tensor(f"bank{i}", [P, 512], F32)) for i in range(8)]

        def v(at, n):
            return room[:, at:at + n]

        def vr(at, n):
            return room_r[:, at:at + n]

        def slot(n):
            return ring[:, n * CH:(n + 1) * CH]

        def pcol(name, n=0):
            return par[:, PAR[name] + n:PAR[name] + n + 1]

        eps_ln, eps_rms = pcol("eps", 0), pcol("eps", 1)
        ident = cst[:, 0:P]
        ones = cst[:, P:2 * P]
        before = cst[:, 2 * P:3 * P]

        xT = v(0, KT * S).rearrange("p (k t) -> p k t", k=KT)
        z = v(4096, 17 * S).rearrange("p (j t) -> p j t", j=17)
        UP = 544
        upad = v(12800, NC_T * UP).rearrange("p (i t) -> p i t", i=NC_T)
        cpad = v(14432, NC_T * 516).rearrange("p (i t) -> p i t", i=NC_T)
        PP = S + POOL_PAD
        ppad = v(15980, 2 * PP).rearrange("p (i t) -> p i t", i=2)
        invcnt = v(17036, 2 * S).rearrange("p (i t) -> p i t", i=2)
        pwin = v(18060, 2 * PP).rearrange("p (i t) -> p i t", i=2)
        mu_a = v(19116, S)
        rs_a = v(19628, S)
        AV, AG, CG, BV, BG, PL = [0, 2, 4], [1, 3, 5], [6, 8, 10], [7, 9, 11], [14, 15, 16], [12, 13]
        mixT = [z[:, j, :] for j in AV + BG + PL]

        hn = v(20480, TT * D).rearrange("p (i d) -> p i d", i=TT)
        acc = v(16384, TT * D).rearrange("p (i d) -> p i d", i=TT)
        hT = v(0, KT * S).rearrange("p (k t) -> p k t", k=KT)
        pT = v(15360, 2 * S).rearrange("p (k t) -> p k t", k=2)
        sgate = [v(22528 + n * S, S) for n in range(4)]
        pproj = [v(14336, S), v(14848, S), v(8192, S), v(8704, S)]
        bdn = v(11264, D)
        GT = v(9216, S)
        oh = v(9728, TT * TOPK * E).rearrange("p (i k e) -> p i k e", i=TT, k=TOPK)
        ohw = v(10240, TT * TOPK * E).rearrange("p (i k e) -> p i k e", i=TT, k=TOPK)
        mask = v(10752, TT * E).rearrange("p (i e) -> p i e", i=TT)
        gmat = v(10880, TT * E).rearrange("p (i e) -> p i e", i=TT)
        pos = v(11008, TT * E).rearrange("p (i e) -> p i e", i=TT)
        logit = v(11136, TT * E).rearrange("p (i e) -> p i e", i=TT)
        cmp_be = v(4096, NB_META * E)
        plet = v(6656, S)
        braw = v(20480, 4 * 512)
        bias_tab = vr(12288, 4 * 512)
        sel_cur = vr(7680, CAP)
        sel_all = v(7808, NB_META)
        xg = v(4096, D)
        xT_hi = vr(0, KT * P).rearrange("p (k s) -> p k s", k=KT)
        xT_lo = vr(1024, KT * P).rearrange("p (k s) -> p k s", k=KT)
        gu_sb = v(5120, 2 * 512).rearrange("p (a c) -> p a c", a=2)
        sig_sb = v(6144, 2 * 256).rearrange("p (a c) -> p a c", a=2)
        ug_sb = v(6656, 2 * 256).rearrange("p (a c) -> p a c", a=2)
        act_sb = v(7168, 2 * 256).rearrange("p (a c) -> p a c", a=2)
        actT_hi = vr(2048, KT * P).rearrange("p (k s) -> p k s", k=KT)
        actT_lo = vr(3072, KT * P).rearrange("p (k s) -> p k s", k=KT)
        y_sb = v(8192, D)
        diag_gate = v(14336, TT * TOPK * P).rearrange("p (c t) -> p c t", c=TT * TOPK)
        raw_w = [ring[:, n * HW:(n + 1) * HW] for n in range(RAW)]
        pair = [ring_r[:, n * CH:(n + 1) * CH] for n in (4, 5, 3)] + [vr(20480, CH)]
        w_hi = [q[:, 0:HW] for q in pair]
        w_lo = [q[:, HW:CH] for q in pair]
        yk = [t.rearrange("p (k d) -> p k d", k=TOPK) for t in (v(9216, CH), v(4096, CH), slot(4), slot(5))]
        idx_tok = sb("idx_tok", [P, 1], U32)
        idx_row = sb("idx_row", [P, 1], U32)
        places = sb("places", [P, TABLE, 2], U32)
        mv8 = sb("mv8", [P, TT, 8])
        mi8 = sb("mi8", [P, TT, 8], U32)
        mif = sb("mif", [P, TT, 8])
        gate = sb("gate", [P, TT, TOPK])
        gsum = sb("gsum", [P, TT])
        destf = sb("destf", [P, TT * TOPK])
        dest = sb("dest", [P, TT * TOPK], U32)
        cnt = sb("cnt", [P, 4, E])
        metaf = sb("metaf", [P, META])
        stats = sb("stats", [P, 2, 6])
        mva = sb("mva", [P, TT, 2])
        rstd = sb("rstd", [P, 8])
        att_s = sb("att_s", [P, 3 * AHEAD])

        uT = hT
        qkT = v(4096, 8 * S).rearrange("p (m t) -> p m t", m=8)
        raw = v(8192, 2 * S).rearrange("p (a t) -> p a t", a=2)
        swp = v(9216, 2 * S).rearrange("p (a t) -> p a t", a=2)
        hQ = v(10240, HG_HEADS * S)
        hK = v(12288, HG_HEADS * S)
        hF = v(14336, HG_HEADS * S)
        h2 = acc
        tot = [hF, v(20480, 1024), v(21504, 512), v(22016, 256), v(22272, 128), v(22400, 64), v(22464, 32),
               v(22496, 16), v(22512, 8)]
        hG = v(22528, HG_HEADS * S).rearrange("p (h t) -> p h t", h=HG_HEADS)
        un = hn
        AT = ring[:, 4 * CH:6 * CH].rearrange("p (h j t) -> p h j t", h=HG_HEADS, j=TT)
        c2 = slot(3)
        ctab, madd, cosT, sinT = (c2[:, n * S:(n + 1) * S] for n in range(4))
        lmask = c2[:, 4 * S:4 * S + 8 * P].bitcast(I32).rearrange("p (l s) -> p l s", l=8)
        v_tok = v(10240, TT * S).rearrange("p (j c) -> p j c", j=TT)
        i_tok = v(12288, TT * S).rearrange("p (j c) -> p j c", j=TT)
        mixed = v(0, 8 * S).rearrange("p (m t) -> p m t", m=8)
        o_sb = v(20480, 2 * S).rearrange("p (a t) -> p a t", a=2)
        osq = v(21504, 2 * S).rearrange("p (a t) -> p a t", a=2)
        sc = v(14336, AHEAD * S).rearrange("p (a t) -> p a t", a=AHEAD)
        ex = v(12288, AHEAD * S).rearrange("p (a t) -> p a t", a=AHEAD)
        pTa = v(8192, TT * S).rearrange("p (j t) -> p j t", j=TT)
        un2 = ring[:, 4 * CH:5 * CH].rearrange("p (i d) -> p i d", i=TT)
        u2T_hi = vr(0, KT * S).rearrange("p (k t) -> p k t", k=KT)
        u2T_lo = vr(20480, KT * S).rearrange("p (k t) -> p k t", k=KT)
        fraw_w = [ring[:, n * HW:(n + 1) * HW] for n in (0, 1, 6)]
        fpair = [ring_r[:, n * CH:(n + 1) * CH] for n in (5, 1, 2)]
        f_hi = [q[:, 0:HW] for q in fpair]
        f_lo = [q[:, HW:CH] for q in fpair]
        kt_hi, kt_lo = (ring_r[:, at:at + 4 * S].rearrange("p (k t) -> p k t", k=4) for at in (4 * CH, 4 * CH + HW))
        fact = v(4096, FFN_T * S).rearrange("p (f t) -> p f t", f=FFN_T)
        fsig = v(15360, 2 * S).rearrange("p (a t) -> p a t", a=2)
        outt = hn

        h_dram = nc.dram_tensor("h_rows", (S, D), F32).ap()
        y_dram = nc.dram_tensor("expert_rows", (TOPK * S, D), F32).ap()
        slot_dram = nc.dram_tensor("slot_rows", (TABLE * CAP, 2), U32).ap()

        names = """xT_in consts_in xtok_in start_in ln1_rows_in late_in table_zeroed h_out scattered y_out z_ready z_evac
            pads_ready conv_ready sq_ready mean_ready var_ready std_ready ln_a_ready sgl_ready pool_in_ready
            pool_ready pool_out_ready mixT_ready mix_ready mix_evac v1_ready s1_ready hn_ready hT_done_a
            hT_done_v hnT_ready h_ready router_ready mask_ready pos_ready e_ready ex_ready meta_ready dest_ready
            gm_ready gT_ready GT_ready pleg_ready plep_ready ple_parts ple_evac bdn_ready bdn_done idx_in
            idx_kept tok_kept rows_in bias_in bias_hi bias_split sel_ready hi_done lo_dve lo_pool half_used evac_done
            sig_done act_ready xt_ready x_hi x_lo turned act_hi act_lo y_copied diag_ready combined acc_done ln2_rows_in fin_row_in c2_in v2_ready s2_ready x2_ready ss_ready
            un_ready unT_ready uT_done_a uT_done_v p_ready p_evac hsig_ready rot_done fK_ready lv_ready lv_upd
            lv_copied asum_ready p_evac_v vt_ready vt_evac o_ready o_evac osq_ready oms_ready ostd_ready
            hmix_ready sc_ready sc_done e2_ready pn_ready pt_ready pt_evac pv_ready pv_evac o2_ready h3_ready
            ss3_ready un3_ready unT3_ready u2T_hi u2T_lo f_ready fs_ready f_evac fhi_done flo_done kt_hi kt_lo fd_ready h4_ready
            ss4_ready out_ready out_written pool_waited dve_steps act_steps pool_steps moe_dve lb_ready
            lbe_ready""".split()
        s = {n: sem(n) for n in names}
        chunk_in = [sem(f"chunk_in{n}") for n in range(RING)]
        raw_in = [sem(f"raw_in{n}") for n in range(RAW)]
        yk_in = [sem(f"yk_in{n}") for n in range(TT)]
        swap_in = [sem(f"swap_in{n}") for n in range(2)]

        pre_used = ([("z_ready", 4), ("z_ready", 8), ("z_ready", 12), ("z_ready", 16), ("z_ready", 17),
                     ("mix_ready", 7), ("mix_ready", 8), ("pleg_ready", 7), ("pleg_ready", 8), ("plep_ready", 8)])
        post_used = ([("p_ready", 4 * (c + 1)) for c in range(5)] + [("vt_ready", 4), ("vt_ready", 8)]
                     + [("o2_ready", 7), ("o2_ready", 8)])
        assert len(pre_used) == PRE and len(post_used) == POST

        def chunk_cols(n):
            return {4: KT * P, 9: 2 * D}.get(n, CH)

        def chunk(eng, n):
            q = PRE_SLOT[n]
            eng.wait_ge(chunk_in[q], 16 * PRE_SLOT[0:n + 1].count(q))
            return slot(q)

        def split_by_pool(i):
            return i % 4 == 3

        def split_count(b, i):
            if split_by_pool(i):
                return s["lo_pool"], b * (HALVES // 4) + (i // 4 + 1)
            return s["lo_dve"], b * (HALVES - HALVES // 4) + (i - i // 4 + 1)

        def chunk2(eng, n):
            q = n % RING2
            eng.wait_ge(chunk_in[q], 16 * (PRE_SLOT.count(q) + n // RING2 + 1))
            return slot(n % RING2)

        def xt_bank(b, q):
            return bank[6 + q] if isinstance(b, int) and b == 0 else bank[4 + q]

        def ffn_used(f):
            return 2 * f + 2 if f < FFN_T else 2 * FFN_T + (f - FFN_T) + 1

        block = ctx.enter_context(nc.Block())

        @block.sync
        def _(sp):
            sp.dma_start(xT[:, 0:KT // 2, :], a["xT"][:, 0:KT // 2 * S].rearrange("p (k t) -> p k t", k=KT // 2))\
              .then_inc(s["start_in"], 16)
            sp.dma_start(slot(0)[:, 0:CH // 2], a["wd"][0, :, 0:CH // 2]).then_inc(s["start_in"], 16)
            sp.dma_start(xT[:, KT // 2:KT, :], a["xT"][:, KT // 2 * S:KT * S].rearrange("p (k t) -> p k t", k=KT // 2))\
              .then_inc(s["xT_in"], 16)
            sp.dma_start(slot(0)[:, CH // 2:CH], a["wd"][0, :, CH // 2:CH]).then_inc(chunk_in[0], 16)
            for n in range(1, PRE):
                if n == 2:
                    sp.wait_ge(s["consts_in"], 16 * 9)
                q = PRE_SLOT[n]
                if q in PRE_SLOT[0:n]:
                    name, count = pre_used[max(m for m in range(n) if PRE_SLOT[m] == q)]
                    sp.wait_ge(s[name], count)
                sp.dma_start(slot(q)[:, 0:chunk_cols(n)], a["wd"][n, :, 0:chunk_cols(n)]).then_inc(chunk_in[q], 16)

            sp.wait_ge(s["meta_ready"], 3)
            T = sp.value_load(meta[0:1, META_T:META_T + 1], min_val=LEAST_BLOCKS, max_val=BLOCKS)

            last = sp.value_load(meta[0:1, META_LAST:META_LAST + 1], min_val=LEAST_BLOCKS - 1, max_val=BLOCKS - 1)

            def block_loads(b, first):
                expert = sp.value_load(meta[0:1, bass.ts(b, 1)], min_val=0, max_val=E - 1)
                for i in range(HALVES):
                    if i >= RAW:
                        sp.wait_ge(*split_count(b, i - RAW))
                    elif not first:
                        sp.wait_ge(*split_count(b - 1, i + HALVES - RAW))
                    sp.dma_start(raw_w[i % RAW], a["wmoe"][bass.ts(expert, 1), i].rearrange("o p n -> (o p) n"))\
                      .then_inc(raw_in[i % RAW], 16)

            block_loads(0, True)
            sp.wait_ge(s["h_ready"], 2 * TT)
            sp.dma_start(rowvec[:, 0:D], a["rows"][2:3, :].broadcast_to([P, D])).then_inc(s["ln2_rows_in"], 16)
            sp.dma_start(rowvec[:, D:2 * D], a["rows"][3:4, :].broadcast_to([P, D])).then_inc(s["ln2_rows_in"], 16)
            with sp.Fori(1, BLOCKS) as b:
                with sp.If(b < T):
                    block_loads(b, False)

            for n in range(POST):
                if n == 0:
                    sp.wait_ge(s["half_used"], last * HALVES + (RAW + 2))
                elif n >= RING2:
                    sp.wait_ge(s[post_used[n - RING2][0]], post_used[n - RING2][1])
                if n == 1:
                    sp.wait_ge(s["y_out"], T * 16)
                    for i in range(TT):
                        sp.dma_start(yk[i], y_dram.rearrange("(k i p) d -> i p k d", k=TOPK, p=P)[i]).then_inc(yk_in[i], 16)
                sp.dma_start(slot(n % RING2), a["wp"][n]).then_inc(chunk_in[n % RING2], 16)
                if n == 1:
                    sp.dma_start(c2[:, 0:4 * S], a["c2"]).then_inc(s["c2_in"], 16)
                    sp.dma_start(lmask, a["lmask"].rearrange("p (l s) -> p l s", l=8)).then_inc(s["c2_in"], 16)
            sp.wait_ge(s["x2_ready"], 2 * TT)
            sp.dma_start(rowvec[:, 0:D], a["rows"][4:5, :].broadcast_to([P, D])).then_inc(s["fin_row_in"], 16)
            for f in range(FFN_HALVES):
                if f == 0:
                    sp.wait_ge(s["vt_ready"], 8)
                elif f == 2:
                    sp.wait_ge(s["pn_ready"], HEADS * TT)
                elif f >= FRAW:
                    sp.wait_ge(s["flo_done"], f - FRAW + 1)
                sp.dma_start(fraw_w[f % FRAW], a["wf"][f]).then_inc(chunk_in[3 + f % FRAW], 16)

            for i in range(TT):
                sp.wait_ge(s["out_ready"], i + 1)
                sp.dma_start(a["out"][i * P:(i + 1) * P, :], outt[:, i, :]).then_inc(s["out_written"], 16)
            sp.wait_ge(s["out_written"], 16 * TT)

        @block.gpsimd
        def _(pool):
            step = Steps(pool, s["pool_steps"])
            places_row = places[0:CAP, :, :].rearrange("p n o -> p (n o)")
            step.mark(pool.memset(upad[:, :, 0:CONV_A - 1], 0.0))
            step.mark(pool.memset(cpad[:, :, 0:CONV_B - 1], 0.0))
            step.mark(pool.memset(ppad[:, :, 0:POOL_PAD], 0.0))
            pool.memset(pwin[:, :, 0:POOL_PAD], 0.0).then_inc(s["pads_ready"], 1)
            step.mark(pool.memset(places[:, :, 0:1], NO_ROW))
            step(pool.memset(places[:, :, 1:2], 0))
            pool.dma_start(slot_dram.rearrange("(p n) o -> p (n o)", p=CAP), places_row).then_inc(s["table_zeroed"], 16)
            pool.wait_ge(s["ln1_rows_in"], 32)
            for i in range(TT):
                pool.wait_ge(s["hn_ready"], i + 1)
                pool.tensor_tensor(acc[:, i, :], hn[:, i, :], rowvec[:, 0:D], ALU.mult).then_inc(s["h_ready"], 1)
                pool.wait_ge(s["h_ready"], 2 * i + 1)
                pool.tensor_tensor(acc[:, i, :], acc[:, i, :], rowvec[:, D:2 * D], ALU.add).then_inc(s["h_ready"], 1)
                pool.wait_ge(s["h_ready"], 2 * i + 2)
                pool.dma_start(h_dram[i * P:(i + 1) * P, :], acc[:, i, :]).then_inc(s["h_out"], 16)
            pool.wait_ge(s["hnT_ready"], KT)
            pool.dma_start(braw, a["bgu"]).then_inc(s["bias_in"], 16)

            pool.wait_ge(s["table_zeroed"], 16)
            pool.wait_ge(s["dest_ready"], 1)
            for i in range(TT):
                for k in range(TOPK):
                    c = i * TOPK + k
                    pool.indirect_dma_start(slot_dram, bass.IndirectOffsetOnAxis(ap=dest[:, c:c + 1], axis=0),
                                            pairs[:, 2 * c:2 * c + 2], None).then_inc(s["scattered"], 16)
            pool.wait_ge(s["scattered"], 16 * TT * TOPK)
            pool.dma_start(places_row, slot_dram.rearrange("(p n) o -> p (n o)", p=CAP)).then_inc(s["idx_in"], 16)
            pool.wait_ge(s["idx_in"], 16)
            pool.wait_ge(s["h_out"], 16 * TT)
            pool.wait_ge(s["meta_ready"], 3)
            T = pool.value_load(meta[0:1, META_T:META_T + 1], min_val=LEAST_BLOCKS, max_val=BLOCKS)

            def wait_counted(name, value):
                pool.wait_ge(s[name], value)
                pool.sem_inc(s["pool_waited"], 1)

            def gather(b):
                pool.tensor_copy(idx_tok[0:CAP, :], places[0:CAP, bass.ds(b, 1), 1]).then_inc(s["tok_kept"], 1)
                wait_counted("tok_kept", b + 1)
                pool.indirect_dma_start(xg[0:CAP, :], None, h_dram,
                                        bass.IndirectOffsetOnAxis(ap=idx_tok[0:CAP, :], axis=0))\
                    .then_inc(s["rows_in"], 16)

            def select(b):
                pool.tensor_copy(sel_cur, sel_all[:, bass.ds(b, 1)].broadcast_to([P, CAP])).then_inc(s["sel_ready"], 1)

            def split_lo(b, i):
                wait_counted("hi_done", b * HALVES + (i + 1))
                pool.tensor_tensor(w_lo[i % PAIRS], raw_w[i % RAW], w_hi[i % PAIRS].bitcast(F32), ALU.subtract)\
                    .then_inc(s["lo_pool"], 1)

            def rows_out(b):
                wait_counted("y_copied", b * 2 + 2)
                wait_counted("idx_kept", b + 1)
                pool.indirect_dma_start(y_dram, bass.IndirectOffsetOnAxis(ap=idx_row[0:CAP, :], axis=0),
                                        y_sb[0:CAP, :], None, bounds_check=TOPK * S - 1, oob_is_err=False)\
                    .then_inc(s["y_out"], 16)

            def block_pool(b, first):
                if not first:
                    rows_out(b - 1)
                split_lo(b, 3)
                wait_counted("rows_in", b * 16 + 16)
                wait_counted("xt_ready", b + 1)
                gather(b + 1)
                split_lo(b, 7)
                if not first:
                    wait_counted("y_out", b * 16)
                pool.tensor_copy(idx_row[0:CAP, :], places[0:CAP, bass.ds(b, 1), 0]).then_inc(s["idx_kept"], 1)
                wait_counted("half_used", b * HALVES + 2 * GU_CHUNKS)
                select(b + 1)
                split_lo(b, 11)

            gather(0)
            select(0)
            pool.wait_ge(s["ple_evac"], 2 * TT)
            pool.wait_ge(s["plep_ready"], 2 * TT)
            for c in range(TT * TOPK):
                i, k = divmod(c, TOPK)
                ins = pool.tensor_scalar(diag_gate[:, c, :], ident, gate[:, i, k:k + 1], None, ALU.mult)
            ins.then_inc(s["diag_ready"], 1)
            block_pool(0, True)
            with pool.Fori(1, BLOCKS + 1) as b:
                with pool.If(b <= T):
                    with pool.If(b < T):
                        block_pool(b, False)
                    with pool.If(b == T):
                        rows_out(b - 1)

        @block.scalar
        def _(act):
            step = Steps(act, s["act_steps"])
            act.dma_start(par[:, :], a["par"]).then_inc(s["consts_in"], 16)
            act.dma_start(cst[:, :], a["cst"]).then_inc(s["consts_in"], 16)
            act.dma_start(invcnt, a["invcnt"].rearrange("p (i t) -> p i t", i=2)).then_inc(s["consts_in"], 16)
            act.dma_start(poolw[:, :, :], a["poolw"].rearrange("p (i t) -> p i t", i=2)).then_inc(s["consts_in"], 16)
            act.dma_start(rw[:, :, :], a["rw"].rearrange("p (k e) -> p k e", k=KT)).then_inc(s["consts_in"], 16)
            act.dma_start(rb[:, :], a["rb"].broadcast_to([P, E])).then_inc(s["consts_in"], 16)
            act.dma_start(eiota[:, :], a["eiota"].broadcast_to([P, E])).then_inc(s["consts_in"], 16)
            act.dma_start(pairs[:, :].bitcast(I32), a["pairs"]).then_inc(s["consts_in"], 16)
            act.dma_start(blockid[:, :], a["blockid"].broadcast_to([P, META])).then_inc(s["consts_in"], 16)

            for j in range(17):
                dst = ppad[:, j - PL[0], POOL_PAD:PP] if j in PL else z[:, j, :]
                if j == PL[0]:
                    act.wait_ge(s["pads_ready"], 1)
                if j == 15:
                    for i in range(NC_T):
                        act.wait_ge(s["mean_ready"], i + 1)
                        act.activation(z[:, AG[i], :], z[:, AV[i], :], ACT.Square).then_inc(s["sq_ready"], 1)
                if j == 16:
                    act.wait_ge(s["var_ready"], 1)
                    act.activation(rs_a, bank[5][:, :], ACT.Sqrt, bias=eps_ln, scale=1.0 / C_CONF)\
                       .then_inc(s["std_ready"], 1)
                act.wait_ge(s["z_ready"], j + 1)
                act.activation(dst, bank[j % 4][:, :], ACT.Sigmoid if j in AG else ACT.Copy).then_inc(s["z_evac"], 1)
                if j == 8:
                    act.dma_start(hn, a["xtok"].rearrange("p (i d) -> p i d", i=TT)).then_inc(s["xtok_in"], 16)
                    for r in range(2):
                        act.dma_start(rowvec[:, r * D:(r + 1) * D], a["rows"][r:r + 1, :].broadcast_to([P, D]))\
                           .then_inc(s["ln1_rows_in"], 16)

            for i in range(NC_T):
                act.wait_ge(s["ln_a_ready"], i + 1)
                act.activation(z[:, AG[i], :], z[:, AV[i], :], ACT.Sigmoid).then_inc(s["sgl_ready"], 1)

            for i in range(2):
                act.wait_ge(s["pool_out_ready"], i + 1)
                act.activation(z[:, PL[i], :], bank[6 + i][:, :], ACT.Copy, scale=pcol("pool_scale", i))\
                   .then_inc(s["pool_ready"], 1)

            for i in range(TT):
                act.wait_ge(s["v1_ready"], i + 1)
                act.activation(rstd[:, i:i + 1], mva[:, i, 1:2], ACT.Sqrt, bias=eps_ln).then_inc(s["s1_ready"], 1)

            act.wait_ge(s["mix_ready"], 2 * TT)
            act.dma_start(pT, a["pT"].rearrange("p (k t) -> p k t", k=2)).then_inc(s["late_in"], 16)
            act.dma_start(bdn[0:E, :], a["bdn"]).then_inc(s["late_in"], 16)

            for k in range(0, KT, 2):
                act.wait_ge(s["hnT_ready"], k + 1)
                act.activation(hT[:, k, :], bank[k][:, :], ACT.Identity, bias=pcol("ln1_b", k), scale=pcol("ln1_g", k))\
                   .then_inc(s["hT_done_a"], 1)

            act.wait_ge(s["e_ready"], 1)
            act.activation(gate[:, :, :], gate[:, :, :], ACT.Exp).then_inc(s["ex_ready"], 1)

            def split_hi(b, i, first=False):
                act.wait_ge(raw_in[i % RAW], b * (16 * HALVES // RAW) + 16 * (i // RAW + 1))
                if not first or i >= PAIRS:
                    act.wait_ge(s["half_used"], b * HALVES + (i - PAIRS + 1))
                act.activation(w_hi[i % PAIRS], raw_w[i % RAW], ACT.Copy).then_inc(s["hi_done"], 1)

            def gathered_hi(b):
                act.wait_ge(s["xt_ready"], b + 1)
                for q in range(2):
                    ins = act.activation(xT_hi[:, 4 * q:4 * q + 4, 0:CAP],
                                         xt_bank(b, q)[:, 0:4 * CAP].rearrange("p (k s) -> p k s", k=4), ACT.Copy)
                ins.then_inc(s["x_hi"], 1)

            def ple_gate(g):
                act.wait_ge(s["pleg_ready"], g + 1)
                if g >= 4:
                    act.wait_ge(s["ple_evac"], g - 3)
                act.activation(sgate[g % 4], bank[1 + g % 2][:, :], ACT.Sigmoid)
                act.wait_ge(s["plep_ready"], g + 1)
                act.activation(pproj[g % 4], bank[3 + g % 2][:, :], ACT.Copy).then_inc(s["ple_parts"], 1)

            act.wait_ge(s["h_ready"], 2 * TT)
            act.wait_ge(s["hnT_ready"], KT)

            for g in range(2 * TT):
                ple_gate(g)
                if g == 2 * TT - 2:
                    split_hi(0, 0, True)
                if g == 4:
                    act.wait_ge(s["gT_ready"], 1)
                    act.activation(GT[0:E, :], bank[6][0:E, :], ACT.Copy).then_inc(s["GT_ready"], 1)
                if g == 1:
                    act.wait_ge(s["bias_in"], 16)
                    act.activation(bias_tab, braw, ACT.Copy).then_inc(s["bias_hi"], 1)

            act.wait_ge(s["meta_ready"], 3)
            T = act.value_load(meta[0:1, META_T:META_T + 1], min_val=LEAST_BLOCKS, max_val=BLOCKS)


            def sigmoids(b, c):
                act.wait_ge(s["evac_done"], b * GU_CHUNKS + (c + 1))
                act.activation(sig_sb[0:CAP, c % 2, :], gu_sb[0:CAP, c % 2, 0:256], ACT.Sigmoid, scale=SW_ALPHA)\
                   .then_inc(s["sig_done"], 1)

            def turned_hi(b, c):
                act.wait_ge(s["turned"], b * GU_CHUNKS + (c + 1))
                act.activation(actT_hi[:, 2 * c:2 * c + 2, 0:CAP],
                               bank[2 + c % 2][:, 0:2 * CAP].rearrange("p (k s) -> p k s", k=2), ACT.Copy)\
                   .then_inc(s["act_hi"], 1)

            def outputs(b):
                act.wait_ge(s["half_used"], b * HALVES + HALVES)
                act.wait_ge(s["idx_kept"], b + 1)
                for n in range(2):
                    act.activation(y_sb[0:CAP, n * 512:(n + 1) * 512], bank[6 + n][0:CAP, :], ACT.Copy)\
                       .then_inc(s["y_copied"], 1)

            def first_part(b, first=False):
                for i in range(9):
                    split_hi(b, i + 3, first)
                    if i >= 2 and i % 2 == 0:
                        sigmoids(b, i // 2 - 1)
                    if i >= 4 and i % 2 == 0:
                        turned_hi(b, i // 2 - 2)
                gathered_hi(b + 1)

            act.wait_ge(s["plep_ready"], 2 * TT)
            gathered_hi(0)
            for i in range(1, 3):
                split_hi(0, i, True)
            act.wait_ge(s["bias_split"], 1)
            act.wait_ge(s["ple_evac"], 2 * TT)
            first_part(0, True)
            with act.Fori(1, BLOCKS + 1) as b:
                with act.If(b <= T):
                    with act.If(b < T):
                        split_hi(b, 0)
                        turned_hi(b - 1, GU_CHUNKS - 1)
                        split_hi(b, 1)
                        split_hi(b, 2)
                        outputs(b - 1)
                        first_part(b)
                    with act.If(b == T):
                        turned_hi(b - 1, GU_CHUNKS - 1)
                        outputs(b - 1)

            for i in range(TT):
                act.wait_ge(s["v2_ready"], i + 1)
                act.activation(rstd[:, i:i + 1], mva[:, i, 1:2], ACT.Sqrt, bias=eps_ln).then_inc(s["s2_ready"], 1)
                act.wait_ge(s["x2_ready"], 2 * i + 2)
                act.activation(un[:, i, :], h2[:, i, :], ACT.Square, accum_out=rstd[:, 4 + i:5 + i]).then_inc(s["ss_ready"], 1)
                act.wait_ge(s["ss_ready"], 2 * i + 1)
                act.activation(rstd[:, 4 + i:5 + i], rstd[:, 4 + i:5 + i], ACT.Sqrt, bias=eps_rms, scale=1.0 / D)\
                   .then_inc(s["ss_ready"], 1)
            for k in range(0, KT, 2):
                act.wait_ge(s["unT_ready"], k + 1)
                act.activation(uT[:, k, :], bank[k][:, :], ACT.Copy, scale=pcol("norm1", k)).then_inc(s["uT_done_a"], 1)

            act.wait_ge(s["lb_ready"], 1)
            act.activation(small[:, 0:2 * HG_HEADS], small[:, 0:2 * HG_HEADS], ACT.Exp).then_inc(s["lbe_ready"], 1)

            for j in range(20):
                act.wait_ge(s["p_ready"], j + 1)
                if j < 4:
                    act.activation(hQ[:, j * S:(j + 1) * S], bank[j % 2][:, :], ACT.Sigmoid).then_inc(s["hsig_ready"], 1)
                elif j < 8:
                    act.activation(hF[:, (j - 4) * S:(j - 3) * S], bank[j % 2][:, :], ACT.Sigmoid).then_inc(s["hsig_ready"], 1)
                elif j < 12:
                    act.activation(hG[:, j - 8, :], bank[j % 2][:, :], ACT.Sigmoid).then_inc(s["hsig_ready"], 1)
                else:
                    m = j - 12
                    if m >= 2:
                        act.wait_ge(s["rot_done"], m - 1)
                    act.activation(raw[:, m % 2, :], bank[j % 2][:, :], ACT.Copy).then_inc(s["p_evac"], 1)
                    act.wait_ge(s["p_evac"], m + 1)
                    for q in range(4):
                        act.dma_start(swp[q * 32:(q + 1) * 32, m % 2, :], raw[(q ^ 1) * 32:(q ^ 1) * 32 + 32, m % 2, :])\
                           .then_inc(swap_in[m % 2], 16)
            for g in range(8):
                act.wait_ge(s["vt_ready"], g + 1)
                if g < 4:
                    dst = v_tok[:, g, :]
                else:
                    dst = i_tok[:, g - 4, :]
                if g == 0:
                    act.wait_ge(s["lv_ready"], LEVELS + 1)
                act.activation(dst, bank[g % 2][:, :], ACT.Copy).then_inc(s["vt_evac"], 1)

            for h in range(HG_HEADS):
                act.wait_ge(s["o_ready"], h + 1)
                if h >= 2:
                    act.wait_ge(s["hmix_ready"], h - 1)
                act.activation(o_sb[:, h % 2, :], bank[2 + h % 2][:, :], ACT.Copy).then_inc(s["o_evac"], 1)
                act.activation(osq[:, h % 2, :], bank[2 + h % 2][:, :], ACT.Square).then_inc(s["osq_ready"], 1)
                act.wait_ge(s["oms_ready"], h + 1)
                act.activation(osq[:, h % 2, :], bank[4 + h % 2][:, :], ACT.Sqrt, bias=eps_rms, scale=1.0 / P)\
                   .then_inc(s["ostd_ready"], 1)

            def probs_out(h):
                act.wait_ge(s["pt_ready"], TT * (h + 1))
                if h >= 1:
                    act.wait_ge(s["pv_ready"], h)
                for j in range(TT):
                    ins = act.activation(pTa[:, j, j * P:S], bank[2 + j][:, j * P:S], ACT.Copy)
                ins.then_inc(s["pt_evac"], 1)

            def head_out(h):
                act.wait_ge(s["pv_ready"], h + 1)
                lo = (h % 2) * DH
                act.activation(mixed[lo:lo + DH, h // 2, :], bank[6 + h % 2][lo:lo + DH, :], ACT.Copy)\
                   .then_inc(s["pv_evac"], 1)

            for u in range(HEADS * TT):
                h, i = divmod(u, TT)
                act.wait_ge(s["sc_done"], u + 1)
                if u >= AHEAD:
                    act.wait_ge(s["pt_ready"], u - AHEAD + 1)
                w = (i + 1) * P
                a4 = u % AHEAD
                act.activation(ex[:, a4, 0:w], sc[:, a4, 0:w], ACT.Exp,
                               bias=att_s[:, 2 * AHEAD + a4:2 * AHEAD + a4 + 1], scale=SCALE).then_inc(s["e2_ready"], 1)
                if i == 2 and h >= 1:
                    probs_out(h - 1)
                if i == TT - 1 and h >= 1:
                    head_out(h - 1)
            probs_out(HEADS - 1)
            head_out(HEADS - 1)

            def ffn_hi(f):
                act.wait_ge(chunk_in[3 + f % FRAW], 16 * (PRE_SLOT.count(3 + f % FRAW) + f // FRAW + 1))
                if f >= FPAIRS:
                    act.wait_ge(s["f_ready"], ffn_used(f - FPAIRS))
                elif f >= 1:
                    act.wait_ge(s["o2_ready"], 2 * TT)
                act.activation(f_hi[f % FPAIRS], fraw_w[f % FRAW], ACT.Copy).then_inc(s["fhi_done"], 1)

            def tile_hi(k):
                act.wait_ge(s["f_evac"], k + 1)
                if k >= 4:
                    act.wait_ge(s["f_ready"], ffn_used(FFN_T + (k - 4) // 2))
                act.activation(kt_hi[:, k % 4, :], fact[:, k, :], ACT.Copy).then_inc(s["kt_hi"], 1)

            ffn_hi(0)
            for i in range(TT):
                act.wait_ge(s["h3_ready"], 2 * i + 2)
                act.activation(un2[:, i, :], h2[:, i, :], ACT.Square, accum_out=rstd[:, i:i + 1]).then_inc(s["ss3_ready"], 1)
                act.wait_ge(s["ss3_ready"], 2 * i + 1)
                act.activation(rstd[:, i:i + 1], rstd[:, i:i + 1], ACT.Sqrt, bias=eps_rms, scale=1.0 / D)\
                   .then_inc(s["ss3_ready"], 1)
            for k in range(KT):
                act.wait_ge(s["unT3_ready"], k + 1)
                act.activation(u2T_hi[:, k, :], bank[k][:, :], ACT.Copy, scale=pcol("norm2", k)).then_inc(s["u2T_hi"], 1)

            for f in range(FFN_T):
                ffn_hi(f + 1)
                act.wait_ge(s["f_ready"], 2 * f + 1)
                if f >= 2:
                    act.wait_ge(s["f_evac"], f - 1)
                act.activation(fsig[:, f % 2, :], bank[2 * (f % 2)][:, :], ACT.Sigmoid).then_inc(s["fs_ready"], 1)
                if f >= FFN_T - 4:
                    tile_hi(f - (FFN_T - 4))
            for c in range(FFN_T // 2):
                if c >= 2:
                    tile_hi(2 * c)
                    tile_hi(2 * c + 1)
                if c + 1 < FFN_T // 2:
                    ffn_hi(FFN_T + c + 1)

            for i in range(TT):
                act.wait_ge(s["h4_ready"], 2 * i + 2)
                act.activation(outt[:, i, :], h2[:, i, :], ACT.Square, accum_out=rstd[:, 4 + i:5 + i])\
                   .then_inc(s["ss4_ready"], 1)
                act.wait_ge(s["ss4_ready"], 2 * i + 1)
                act.activation(rstd[:, 4 + i:5 + i], rstd[:, 4 + i:5 + i], ACT.Sqrt, bias=eps_rms, scale=1.0 / D)\
                   .then_inc(s["ss4_ready"], 1)

        @block.tensor
        def _(pe):
            def accumulate(out, pairs):
                n = len(pairs)
                for k, (lhsT, rhs) in enumerate(pairs):
                    ins = pe.matmul(out, lhsT, rhs, start=(k == 0), stop=(k == n - 1))
                return ins

            pe.wait_ge(s["start_in"], 32)
            w0 = slot(0).rearrange("p (k c) -> p k c", k=KT)
            for j in range(4):
                for k in range(KT // 2):
                    pe.matmul(bank[j][:, :], w0[:, k, j * P:(j + 1) * P], xT[:, k, :], start=(k == 0), stop=False,
                              skip_group_check=True)
            pe.wait_ge(s["xT_in"], 16)

            def z_tile(j):
                w = chunk(pe, j // 4)
                n = 4 if j < 16 else 1
                w = w[:, 0:KT * n * P].rearrange("p (k c) -> p k c", k=KT)
                if j >= 4:
                    pe.wait_ge(s["z_evac"], j - 3)
                c = (j % 4) * P if j < 16 else 0
                if j < 4:
                    for k in range(KT // 2, KT):
                        ins = pe.matmul(bank[j][:, :], w[:, k, c:c + P], xT[:, k, :], start=False, stop=(k == KT - 1),
                                        skip_group_check=True)
                    ins.then_inc(s["z_ready"], 1)
                else:
                    accumulate(bank[j % 4][:, :], [(w[:, k, c:c + P], xT[:, k, :]) for k in range(KT)])\
                        .then_inc(s["z_ready"], 1)

            for j in range(17):
                z_tile(j)
                if j == 13:
                    pe.wait_ge(s["consts_in"], 16 * 9)
                    pe.wait_ge(s["conv_ready"], NC_T)
                    accumulate(bank[4][:, :], [(ones, z[:, t, :]) for t in AV]).then_inc(s["asum_ready"], 1)
                if j == 15:
                    pe.wait_ge(s["sq_ready"], NC_T)
                    accumulate(bank[5][:, :], [(ones, z[:, t, :]) for t in AG]).then_inc(s["var_ready"], 1)
            for i in range(2):
                pe.wait_ge(s["pool_in_ready"], i + 1)
                accumulate(bank[6 + i][:, :], [(poolw[:, i, :], z[:, PL[i], :])]).then_inc(s["pool_out_ready"], 1)

            pe.wait_ge(s["z_evac"], 17)
            pe.wait_ge(s["mixT_ready"], NC_T)
            pe.wait_ge(s["pool_ready"], 2)
            for g in range(2 * TT):
                i, n = divmod(g, 2)
                w = chunk(pe, 5 + n).rearrange("p (k c) -> p k c", k=KT)
                if g >= 4:
                    pe.wait_ge(s["mix_evac"], g - 3)
                accumulate(bank[g % 4][:, :], [(mixT[k][:, i * P:(i + 1) * P], w[:, k, :]) for k in range(KT)])\
                    .then_inc(s["mix_ready"], 1)

            pe.wait_ge(s["mix_evac"], 2 * TT)
            for i in range(TT):
                pe.wait_ge(s["hn_ready"], i + 1)
                for k in range(KT):
                    ins = pe.transpose(bank[k][:, i * P:(i + 1) * P], hn[:, i, k * P:(k + 1) * P], ident)
                    if i == TT - 1:
                        ins.then_inc(s["hnT_ready"], 1)

            pe.wait_ge(s["hT_done_a"], KT // 2)
            pe.wait_ge(s["hT_done_v"], KT // 2)
            for i in range(TT):
                ins = accumulate(bank[0][:, i * E:(i + 1) * E],
                                 [(hT[:, k, i * P:(i + 1) * P], rw[:, k, :]) for k in range(KT)])
            ins.then_inc(s["router_ready"], 1)

            def ple(g):
                i, n = divmod(g, 2)
                w = chunk(pe, 7 + n).rearrange("p (k c) -> p k c", k=KT)
                if g >= 2:
                    pe.wait_ge(s["ple_parts"], g - 1)
                accumulate(bank[1 + g % 2][:, :], [(hT[:, k, i * P:(i + 1) * P], w[:, k, :]) for k in range(KT)])\
                    .then_inc(s["pleg_ready"], 1)
                w = chunk(pe, 9)[:, 0:2 * D].rearrange("p (k c) -> p k c", k=2)
                if g == 0:
                    pe.wait_ge(s["late_in"], 32)
                accumulate(bank[3 + g % 2][:, :],
                           [(pT[:, k, i * P:(i + 1) * P], w[:, k, n * 512:(n + 1) * 512]) for k in range(2)])\
                    .then_inc(s["plep_ready"], 1)

            ple(0)
            ple(1)
            pe.wait_ge(s["mask_ready"], 1)
            for i in range(TT):
                accumulate(bank[5][:, i * E:(i + 1) * E],
                           [(ones, mask[:, j, :]) for j in range(i)] + [(before, mask[:, i, :])])
            accumulate(bank[5][:, TT * E:(TT + 1) * E], [(ones, mask[:, j, :]) for j in range(TT)])\
                .then_inc(s["pos_ready"], 1)
            ple(2)
            ple(3)
            pe.wait_ge(s["gm_ready"], 1)
            for i in range(TT):
                ins = pe.transpose(bank[6][0:E, i * P:(i + 1) * P], gmat[:, i, :], ident)
            ins.then_inc(s["gT_ready"], 1)
            def gathered(b):
                pe.wait_ge(s["rows_in"], b * 16 + 16)
                for k in range(KT):
                    ins = pe.transpose(xt_bank(b, k // 4)[:, (k % 4) * CAP:(k % 4 + 1) * CAP],
                                       xg[0:CAP, k * P:(k + 1) * P], ident[0:CAP, 0:CAP])
                ins.then_inc(s["xt_ready"], 1)

            for g in range(4, 2 * TT):
                ple(g)
                if g == 2 * TT - 2:
                    pe.wait_ge(s["GT_ready"], 1)
                    gathered(0)
            pe.wait_ge(s["meta_ready"], 3)
            T = pe.value_load(meta[0:1, META_T:META_T + 1], min_val=LEAST_BLOCKS, max_val=BLOCKS)
            pe.wait_ge(s["ple_parts"], 2 * TT)

            pe.wait_ge(s["bias_split"], 1)

            def product(out, x_hi, x_lo, w_hi, w_lo, start, stop):
                pe.matmul(out, x_hi, w_hi, start=start, stop=False, skip_group_check=True)
                pe.matmul(out, x_hi, w_lo, start=False, stop=False, skip_group_check=True)
                return pe.matmul(out, x_lo, w_hi, start=False, stop=stop, skip_group_check=True)

            def turn(b, c):
                pe.wait_ge(s["act_ready"], b * GU_CHUNKS + (c + 1))
                if c >= 2:
                    pe.wait_ge(s["act_lo"], b * GU_CHUNKS + (c - 1))
                for r in range(2):
                    ins = pe.transpose(bank[2 + c % 2][:, r * CAP:(r + 1) * CAP],
                                       act_sb[0:CAP, c % 2, r * P:(r + 1) * P], ident[0:CAP, 0:CAP])
                ins.then_inc(s["turned"], 1)

            def block_pe(b, first):
                pe.wait_ge(s["x_lo"], b + 1)
                pe.wait_ge(s["sel_ready"], b + 1)
                for i in range(2 * GU_CHUNKS):
                    c = i // 2
                    out = bank[c % 2][0:CAP, :]
                    if i % 2 == 0:
                        if not first or c >= 2:
                            pe.wait_ge(s["evac_done"], b * GU_CHUNKS + (c - 1))
                        pe.matmul(out, sel_cur, bias_tab[:, c * 512:(c + 1) * 512], start=True, stop=False,
                                  skip_group_check=True)
                    pe.wait_ge(*split_count(b, i))
                    hi, lo = (w[i % PAIRS].rearrange("p (k c) -> p k c", k=4) for w in (w_hi, w_lo))
                    for q in range(4):
                        k = 4 * (i % 2) + q
                        ins = product(out, xT_hi[:, k, 0:CAP], xT_lo[:, k, 0:CAP], hi[:, q, :], lo[:, q, :],
                                      False, k == KT - 1)
                    ins.then_inc(s["half_used"], 1)
                    if first:
                        if i >= 2:
                            pe.wait_ge(s["bdn_done"], i - 1)
                        accumulate(bank[6 + i % 2][:, :], [(GT[0:E, i // 2 * P:(i // 2 + 1) * P],
                                                            bdn[0:E, (i % 2) * 512:(i % 2 + 1) * 512])])\
                            .then_inc(s["bdn_ready"], 1)
                    if i % 2 == 1 and c >= 1:
                        turn(b, c - 1)
                gathered(b + 1)
                for d in range(GU_CHUNKS):
                    i = 2 * GU_CHUNKS + d
                    if d == 0 and first:
                        pe.wait_ge(s["bdn_done"], 2 * TT)
                    elif d == 0:
                        pe.wait_ge(s["y_copied"], b * 2)
                    pe.wait_ge(s["act_lo"], b * GU_CHUNKS + (d + 1))
                    pe.wait_ge(*split_count(b, i))
                    hi, lo = (w[i % PAIRS].rearrange("p (r c) -> p r c", r=2) for w in (w_hi, w_lo))
                    for r in range(2):
                        k = 2 * d + r
                        for n in range(2):
                            ins = product(bank[6 + n][0:CAP, :], actT_hi[:, k, 0:CAP], actT_lo[:, k, 0:CAP],
                                          hi[:, r, n * 512:(n + 1) * 512], lo[:, r, n * 512:(n + 1) * 512],
                                          k == 0, k == KT - 1)
                    ins.then_inc(s["half_used"], 1)
                    if d == 1:
                        turn(b, GU_CHUNKS - 1)

            block_pe(0, True)
            with pe.Fori(1, BLOCKS) as b:
                with pe.If(b < T):
                    block_pe(b, False)

            pe.wait_ge(s["x_lo"], T + 1)
            pe.wait_ge(s["act_lo"], T * GU_CHUNKS)
            pe.wait_ge(s["y_copied"], T * 2)
            pe.wait_ge(s["diag_ready"], 1)
            for i in range(TT):
                pe.wait_ge(yk_in[i], 16)
                for n in range(2):
                    accumulate(bank[2 * i + n][:, :], [(diag_gate[:, i * TOPK + k, :], yk[i][:, k, n * 512:(n + 1) * 512])
                                                       for k in range(TOPK)]).then_inc(s["combined"], 1)
            for i in range(TT):
                pe.wait_ge(s["un_ready"], i + 1)
                if i == 0:
                    pe.wait_ge(s["acc_done"], 2 * TT)
                for k in range(KT):
                    ins = pe.transpose(bank[k][:, i * P:(i + 1) * P], un[:, i, k * P:(k + 1) * P], ident)
                    if i == TT - 1:
                        ins.then_inc(s["unT_ready"], 1)

            def p_tile(j):
                w = chunk2(pe, j // 4).rearrange("p (k c) -> p k c", k=KT)
                if 2 <= j < 6:
                    pe.wait_ge(s["p_evac_v"], j - 1)
                elif 6 <= j < 10:
                    pe.wait_ge(s["hsig_ready"], j - 1)
                elif 10 <= j < 14:
                    pe.wait_ge(s["p_evac_v"], j - 5)
                elif j >= 14:
                    pe.wait_ge(s["p_evac"], j - 13)
                c = (j % 4) * P
                for k in range(KT):
                    if j == 0:
                        pe.wait_ge(s["uT_done_v" if k % 2 else "uT_done_a"], k // 2 + 1)
                    ins = pe.matmul(bank[j % 2][:, :], w[:, k, c:c + P], uT[:, k, :], start=(k == 0), stop=(k == KT - 1))
                ins.then_inc(s["p_ready"], 1)

            def level(n):
                if n == 0:
                    pe.wait_ge(s["fK_ready"], 1)
                else:
                    pe.wait_ge(s["lv_upd"], n)
                    pe.wait_ge(s["lv_copied"], n)
                for h in range(HG_HEADS):
                    q0 = h * S
                    if n <= TILE_LEVELS:
                        for j in range(TT):
                            at = q0 + j * P
                            ins = pe.matmul(bank[2 + h][:, j * P:(j + 1) * P], hK[:, at:at + P], hQ[:, at:at + P],
                                            start=True, stop=True)
                    elif n == TILE_LEVELS + 1:
                        for j in range(2):
                            at = q0 + 2 * j * P
                            ins = pe.matmul(bank[2 + h][:, j * P:(j + 1) * P], hK[:, at:at + P],
                                            hQ[:, at + P:at + 2 * P], start=True, stop=True)
                    else:
                        for j in range(2):
                            ins = pe.matmul(bank[2 + h][:, 2 * j * P:2 * (j + 1) * P],
                                            hK[:, q0 + j * P:q0 + (j + 1) * P], hQ[:, q0 + 2 * P:q0 + 4 * P],
                                            start=True, stop=True)
                ins.then_inc(s["lv_ready"], 1)

            for j in range(8):
                p_tile(j)
            for n in range(LEVELS + 1):
                level(n)
                p_tile(8 + n)
            p_tile(18)
            p_tile(19)
            for g in range(8):
                w = chunk2(pe, 5 + g // 4).rearrange("p (k c) -> p k c", k=KT)
                if g < 2:
                    pe.wait_ge(s["p_evac"], 7 + g)
                else:
                    pe.wait_ge(s["vt_evac"], g - 1)
                i = g % 4
                accumulate(bank[g % 2][:, :], [(uT[:, k, i * P:(i + 1) * P], w[:, k, :]) for k in range(KT)])\
                    .then_inc(s["vt_ready"], 1)

            pe.wait_ge(s["lv_copied"], LEVELS + 1)
            pe.wait_ge(s["vt_evac"], 8)

            def hgrn_out(h):
                if h >= 2:
                    pe.wait_ge(s["osq_ready"], h - 1)
                for j in range(TT):
                    ins = pe.matmul(bank[2 + h % 2][:, j * P:S], i_tok[:, j, h * P:(h + 1) * P], AT[:, h, j, j * P:S],
                                    start=(j == 0), stop=(j == TT - 1), skip_group_check=True)
                ins.then_inc(s["o_ready"], 1)

            def hgrn_ms(h):
                pe.wait_ge(s["osq_ready"], h + 1)
                if h >= 2:
                    pe.wait_ge(s["ostd_ready"], h - 1)
                accumulate(bank[4 + h % 2][:, :], [(ones, osq[:, h % 2, :])]).then_inc(s["oms_ready"], 1)

            hgrn_out(0)
            for h in range(HG_HEADS):
                if h + 1 < HG_HEADS:
                    hgrn_out(h + 1)
                hgrn_ms(h)

            pe.wait_ge(s["rot_done"], 8)
            pe.wait_ge(s["ostd_ready"], HG_HEADS)

            def scores(u):
                h, i = divmod(u, TT)
                lo = (h % 2) * DH
                m = h // 2
                if u >= 2:
                    pe.wait_ge(s["sc_done"], u - 1)
                pe.matmul(bank[u % 2][:, 0:(i + 1) * P], qkT[lo:lo + DH, m, i * P:(i + 1) * P],
                          qkT[lo:lo + DH, 4 + m, 0:(i + 1) * P], start=True, stop=True).then_inc(s["sc_ready"], 1)

            def probs_T(u):
                h, i = divmod(u, TT)
                pe.wait_ge(s["pn_ready"], u + 1)
                if i == 0 and h >= 1:
                    pe.wait_ge(s["pt_evac"], h)
                for j in range(i + 1):
                    ins = pe.transpose(bank[2 + j][:, i * P:(i + 1) * P], ex[:, u % AHEAD, j * P:(j + 1) * P], ident)
                ins.then_inc(s["pt_ready"], 1)

            def head_values(h):
                lo = (h % 2) * DH
                pe.wait_ge(s["pt_evac"], h + 1)
                if h >= 2:
                    pe.wait_ge(s["pv_evac"], h - 1)
                for j in range(TT):
                    ins = pe.matmul(bank[6 + h % 2][lo:lo + DH, j * P:S], v_tok[:, j, h * DH:(h + 1) * DH],
                                    pTa[:, j, j * P:S], start=(j == 0), stop=(j == TT - 1), skip_group_check=True)
                ins.then_inc(s["pv_ready"], 1)

            for u in range(AHEAD):
                scores(u)
            for u in range(HEADS * TT):
                probs_T(u)
                if u + AHEAD < HEADS * TT:
                    scores(u + AHEAD)
                if u % TT == TT - 1:
                    head_values(u // TT)

            pe.wait_ge(s["pv_evac"], HEADS)
            pe.wait_ge(s["hmix_ready"], HG_HEADS)
            pe.wait_ge(s["sc_done"], HEADS * TT)
            for g in range(2 * TT):
                i, n = divmod(g, 2)
                w = chunk2(pe, 7 + n).rearrange("p (k c) -> p k c", k=KT)
                if g >= 4:
                    pe.wait_ge(s["h3_ready"], g - 3)
                accumulate(bank[g % 4][:, :], [(mixed[:, k, i * P:(i + 1) * P], w[:, k, :]) for k in range(KT)])\
                    .then_inc(s["o2_ready"], 1)

            pe.wait_ge(s["h3_ready"], 2 * TT)
            for i in range(TT):
                pe.wait_ge(s["un3_ready"], i + 1)
                for k in range(KT):
                    ins = pe.transpose(bank[k][:, i * P:(i + 1) * P], un2[:, i, k * P:(k + 1) * P], ident)
                    if i == TT - 1:
                        ins.then_inc(s["unT3_ready"], 1)
            for f in range(FFN_T):
                pe.wait_ge(s["flo_done"], f + 1)
                if f >= 2:
                    pe.wait_ge(s["f_evac"], f - 1)
                hi, lo = (w[f % FPAIRS].rearrange("p (k c) -> p k c", k=KT) for w in (f_hi, f_lo))
                for n in range(2):
                    for k in range(KT):
                        if f == 0 and n == 0:
                            pe.wait_ge(s["u2T_lo"], k + 1)
                        ins = product(bank[2 * (f % 2) + n][:, :], hi[:, k, n * P:(n + 1) * P], lo[:, k, n * P:(n + 1) * P],
                                      u2T_hi[:, k, :], u2T_lo[:, k, :], k == 0, k == KT - 1)
                    ins.then_inc(s["f_ready"], 1)
            pe.wait_ge(s["f_evac"], FFN_T)
            for c in range(FFN_T // 2):
                f = FFN_T + c
                pe.wait_ge(s["flo_done"], f + 1)
                pe.wait_ge(s["kt_lo"], 2 * c + 2)
                hi, lo = (w[f % FPAIRS].rearrange("p (r c) -> p r c", r=2) for w in (f_hi, f_lo))
                for i in range(TT):
                    for n in range(2):
                        for r in range(2):
                            k = 2 * c + r
                            ins = product(bank[2 * i + n][:, :], kt_hi[:, k % 4, i * P:(i + 1) * P],
                                          kt_lo[:, k % 4, i * P:(i + 1) * P], hi[:, r, n * 512:(n + 1) * 512],
                                          lo[:, r, n * 512:(n + 1) * 512], k == 0, k == FFN_T - 1)
                    if c == FFN_T // 2 - 1:
                        ins.then_inc(s["fd_ready"], 1)
                if c < FFN_T // 2 - 1:
                    ins.then_inc(s["f_ready"], 1)

        @block.vector
        def _(dve):
            step = Steps(dve, s["dve_steps"])

            def shifted_sum(out, buf, lo, shift, hi=P):
                return dve.tensor_tensor(out[lo:hi], buf[lo:hi, POOL_PAD:PP], buf[lo:hi, POOL_PAD - shift:PP - shift],
                                         ALU.add)

            dve.wait_ge(s["consts_in"], 16 * 9)
            dve.wait_ge(s["pads_ready"], 1)
            for i in range(NC_T):
                dve.wait_ge(s["z_evac"], 2 * i + 2)
                step(dve.tensor_tensor(upad[:, i, CONV_A - 1:CONV_A - 1 + S], z[:, AV[i], :], z[:, AG[i], :], ALU.mult))
                o = z[:, AV[i], :]
                for k in range(CONV_A):
                    w = pcol("conv_a_w", i * CONV_A + k)
                    if k == 0:
                        step(dve.tensor_scalar(o, upad[:, i, 0:S], w, None, ALU.mult))
                    else:
                        step(dve.scalar_tensor_tensor(o, upad[:, i, k:k + S], w, o, ALU.mult, ALU.add))
                dve.tensor_scalar(o, o, pcol("conv_a_b", i), None, ALU.add).then_inc(s["conv_ready"], 1)

            def short(i):
                dve.wait_ge(s["z_evac"], 8 + 2 * i)
                step(dve.tensor_tensor(cpad[:, i, CONV_B - 1:CONV_B - 1 + S], z[:, CG[i], :], z[:, BV[i], :], ALU.mult))
                o = z[:, CG[i], :]
                for k in range(CONV_B):
                    w = pcol("conv_b_w", i * CONV_B + k)
                    if k == 0:
                        step(dve.tensor_scalar(o, cpad[:, i, 0:S], w, None, ALU.mult))
                    else:
                        step(dve.scalar_tensor_tensor(o, cpad[:, i, k:k + S], w, o, ALU.mult, ALU.add))

            for i in range(NC_T):
                short(i)
            dve.wait_ge(s["asum_ready"], 1)
            step(dve.tensor_scalar(mu_a, bank[4][:, :], 1.0 / C_CONF, None, ALU.mult))
            for i in range(NC_T):
                dve.tensor_tensor(z[:, AV[i], :], z[:, AV[i], :], mu_a, ALU.subtract).then_inc(s["mean_ready"], 1)
            for i in range(2):
                win, src, dst = pwin[:, i, :], ppad[:, i, :], z[:, PL[i], :]
                dve.wait_ge(s["z_evac"], PL[i] + 1)
                step(shifted_sum(win[:, POOL_PAD:PP], src, 0, 1))
                if i == 1:
                    four = upad[:, 0, :]
                    step(shifted_sum(four[:, POOL_PAD:PP], win, 0, 2))
                    step(shifted_sum(win[:, POOL_PAD:PP], four, 0, 4))
                step(shifted_sum(dst, win, P // 2, 2 if i == 0 else 8))
                step.mark(dve.tensor_tensor(dst[0:P // 2], win[0:P // 2, POOL_PAD:PP], invcnt[0:P // 2, i, :], ALU.mult))
                step(dve.tensor_tensor(dst[P // 2:P], dst[P // 2:P], invcnt[P // 2:P, i, :], ALU.mult))
                dve.tensor_tensor(dst, dst, src[:, POOL_PAD:PP], ALU.subtract).then_inc(s["pool_in_ready"], 1)
            dve.wait_ge(s["std_ready"], 1)
            step(dve.reciprocal(rs_a, rs_a))
            for i in range(NC_T):
                step(dve.tensor_tensor(z[:, AV[i], :], z[:, AV[i], :], rs_a, ALU.mult))
                dve.tensor_scalar(z[:, AV[i], :], z[:, AV[i], :], pcol("ln_a_g", i), pcol("ln_a_b", i), ALU.mult, ALU.add)\
                   .then_inc(s["ln_a_ready"], 1)
            for i in range(NC_T):
                dve.wait_ge(s["z_evac"], BG[i] + 1)
                step.mark(dve.tensor_tensor(z[:, BG[i], :], z[:, BG[i], :], z[:, CG[i], :], ALU.mult))

            for i in range(NC_T):
                dve.wait_ge(s["sgl_ready"], i + 1)
                dve.tensor_tensor(z[:, AV[i], :], z[:, AV[i], :], z[:, AG[i], :], ALU.mult).then_inc(s["mixT_ready"], 1)

            dve.wait_ge(s["xtok_in"], 16)

            def row_stats(i, src, ready):
                for q in range(2):
                    step.mark(dve.bn_stats(stats[:, q, :], src[:, q * 512:(q + 1) * 512]))
                step.wait()
                dve.bn_aggr(mva[:, i, :], stats[:, :, :].rearrange("p a b -> p (a b)")).then_inc(ready, 1)

            for i in range(TT):
                for n in range(2):
                    g = 2 * i + n
                    dve.wait_ge(s["mix_ready"], g + 1)
                    part = hn[:, i, n * 512:(n + 1) * 512]
                    dve.scalar_tensor_tensor(part, part, ALPHA, bank[g % 4][:, :], ALU.mult, ALU.add)\
                       .then_inc(s["mix_evac"], 1)
                dve.wait_ge(s["mix_evac"], 2 * i + 2)
                row_stats(i, hn[:, i, :], s["v1_ready"])
                dve.wait_ge(s["s1_ready"], i + 1)
                step(dve.reciprocal(rstd[:, i:i + 1], rstd[:, i:i + 1]))
                dve.tensor_scalar(hn[:, i, :], hn[:, i, :], mva[:, i, 0:1], rstd[:, i:i + 1], ALU.subtract, ALU.mult)\
                   .then_inc(s["hn_ready"], 1)
            for k in range(1, KT, 2):
                dve.wait_ge(s["hnT_ready"], k + 1)
                dve.tensor_scalar(hT[:, k, :], bank[k][:, :], pcol("ln1_g", k), pcol("ln1_b", k), ALU.mult, ALU.add)\
                   .then_inc(s["hT_done_v"], 1)

            dve.wait_ge(s["router_ready"], 1)
            step(dve.tensor_tensor(logit, bank[0][:, 0:TT * E].rearrange("p (i e) -> p i e", i=TT),
                                   rb[:, :].unsqueeze(1).broadcast_to([P, TT, E]), ALU.add))
            for i in range(TT):
                step(dve.max(mv8[:, i, :], logit[:, i, :]))
                step(dve.max_index(mi8[:, i, :], mv8[:, i, :], logit[:, i, :]))
            step(dve.tensor_copy(mif[:, :, :], mi8[:, :, :]))
            step(dve.tensor_tensor(oh, eiota[:, :].unsqueeze(1).unsqueeze(1).broadcast_to([P, TT, TOPK, E]),
                                   mif[:, :, 0:TOPK].unsqueeze(3).broadcast_to([P, TT, TOPK, E]), ALU.is_equal))
            dve.tensor_reduce(mask, oh.rearrange("p i k e -> p i e k"), AX.X, ALU.add).then_inc(s["mask_ready"], 1)
            dve.tensor_tensor(gate[:, :, :], mv8[:, :, 0:TOPK], mv8[:, :, 0:1].broadcast_to([P, TT, TOPK]), ALU.subtract)\
               .then_inc(s["e_ready"], 1)
            dve.wait_ge(s["ex_ready"], 1)
            step(dve.tensor_reduce(gsum[:, :], gate[:, :, :], AX.X, ALU.add))
            step(dve.reciprocal(gsum[:, :], gsum[:, :]))
            step(dve.tensor_tensor(gate[:, :, :], gate[:, :, :], gsum[:, :].unsqueeze(2).broadcast_to([P, TT, TOPK]),
                                   ALU.mult))
            step(dve.tensor_tensor(ohw, oh, gate[:, :, :].unsqueeze(3).broadcast_to([P, TT, TOPK, E]), ALU.mult))
            dve.tensor_reduce(gmat, ohw.rearrange("p i k e -> p i e k"), AX.X, ALU.add).then_inc(s["gm_ready"], 1)

            dve.wait_ge(s["pos_ready"], 1)
            count, nblk, end, first_slot = (cnt[:, n, :] for n in range(4))
            step(dve.tensor_copy(count, bank[5][:, TT * E:(TT + 1) * E]))
            step(dve.tensor_scalar(nblk, count, 0.0, None, ALU.is_gt))
            for m in range(1, MAX_PER_EXPERT):
                step(dve.scalar_tensor_tensor(nblk, count, float(m * CAP), nblk, ALU.is_gt, ALU.add))
            step(dve.tensor_tensor_scan(end, ones[:, 0:E], nblk, 0.0, ALU.mult, ALU.add))
            step(dve.tensor_tensor(first_slot, end, nblk, ALU.subtract))
            step(dve.tensor_scalar(first_slot, first_slot, float(CAP), None, ALU.mult))
            step(dve.tensor_tensor(pos, bank[5][:, 0:TT * E].rearrange("p (i e) -> p i e", i=TT),
                                   first_slot.unsqueeze(1).broadcast_to([P, TT, E]), ALU.add))
            dve.wait_ge(s["gm_ready"], 1)
            step(dve.tensor_tensor(ohw, oh, pos.unsqueeze(2).broadcast_to([P, TT, TOPK, E]), ALU.mult))
            step(dve.tensor_reduce(destf[:, :].rearrange("p (i k) -> p i k", i=TT), ohw, AX.X, ALU.add))
            whole = small[:, 0:TT * TOPK]
            step(dve.tensor_scalar(whole, destf[:, :], 1.0 / CAP, 0.5 / CAP - 0.5, ALU.mult, ALU.add))
            step(dve.tensor_scalar(whole, whole, 12582912.0, None, ALU.add))
            step(dve.tensor_scalar(whole, whole, 12582912.0, None, ALU.subtract))
            step(dve.tensor_scalar(whole, whole, float(1 - CAP * TABLE), None, ALU.mult))
            step(dve.scalar_tensor_tensor(destf[:, :], destf[:, :], float(TABLE), whole, ALU.mult, ALU.add))
            dve.tensor_copy(dest[:, :], destf[:, :]).then_inc(s["dest_ready"], 1)
            be = cmp_be.rearrange("p (b e) -> p b e", e=E)
            step(dve.tensor_tensor(be, end.unsqueeze(1).broadcast_to([P, NB_META, E]),
                                   blockid[:, 0:NB_META].unsqueeze(2).broadcast_to([P, NB_META, E]), ALU.is_le))
            step(dve.tensor_reduce(metaf[:, 0:NB_META], be, AX.X, ALU.add))
            step(dve.tensor_scalar(metaf[:, 0:NB_META], metaf[:, 0:NB_META], float(E - 1), None, ALU.min))
            step(dve.tensor_scalar(sel_all, metaf[:, 0:NB_META], pcol("expert"), None, ALU.is_equal))
            dve.tensor_copy(meta[0:1, 0:NB_META], metaf[0:1, 0:NB_META]).then_inc(s["meta_ready"], 1)
            step(dve.tensor_scalar(metaf[0:1, META_LAST:META_LAST + 1], end[0:1, E - 1:E], -1.0, None, ALU.add))
            dve.tensor_copy(meta[0:1, META_LAST:META_LAST + 1], metaf[0:1, META_LAST:META_LAST + 1])\
               .then_inc(s["meta_ready"], 1)
            dve.tensor_copy(meta[0:1, META_T:META], end[0:1, E - 1:E]).then_inc(s["meta_ready"], 1)

            dve.wait_ge(s["bias_hi"], 1)
            dve.tensor_tensor(bias_tab[E:2 * E, :], braw[E:2 * E, :], bias_tab[E:2 * E, :].bitcast(F32), ALU.subtract)\
               .then_inc(s["bias_split"], 1)

            def split_lo(b, i):
                if not split_by_pool(i):
                    dve.wait_ge(s["hi_done"], b * HALVES + (i + 1))
                    dve.tensor_tensor(w_lo[i % PAIRS], raw_w[i % RAW], w_hi[i % PAIRS].bitcast(F32), ALU.subtract)\
                       .then_inc(s["lo_dve"], 1)

            dve.wait_ge(s["h_out"], 16 * TT)
            for g in range(2 * TT):
                i, n = divmod(g, 2)
                part = acc[:, i, n * 512:(n + 1) * 512]
                dve.wait_ge(s["ple_parts"], g + 1)
                dve.tensor_tensor(plet, sgate[g % 4], pproj[g % 4], ALU.mult).then_inc(s["ple_evac"], 1)
                dve.wait_ge(s["ple_evac"], g + 1)
                dve.wait_ge(s["h_ready"], 2 * i + 2)
                step(dve.scalar_tensor_tensor(part, part, ALPHA, plet, ALU.mult, ALU.add))
                if g == 2 * TT - 2:
                    split_lo(0, 0)
            dve.wait_ge(s["meta_ready"], 3)
            T = dve.value_load(meta[0:1, META_T:META_T + 1], min_val=LEAST_BLOCKS, max_val=BLOCKS)

            def gathered_lo(b):
                dve.wait_ge(s["x_hi"], b + 1)
                for q in range(2):
                    ins = dve.tensor_tensor(xT_lo[:, 4 * q:4 * q + 4, 0:CAP],
                                            xt_bank(b, q)[:, 0:4 * CAP].rearrange("p (k s) -> p k s", k=4),
                                            xT_hi[:, 4 * q:4 * q + 4, 0:CAP].bitcast(F32), ALU.subtract)
                ins.then_inc(s["x_lo"], 1)

            def turned_lo(b, c):
                dve.wait_ge(s["act_hi"], b * GU_CHUNKS + (c + 1))
                dve.tensor_tensor(actT_lo[:, 2 * c:2 * c + 2, 0:CAP],
                                  bank[2 + c % 2][:, 0:2 * CAP].rearrange("p (k s) -> p k s", k=2),
                                  actT_hi[:, 2 * c:2 * c + 2, 0:CAP].bitcast(F32), ALU.subtract)\
                   .then_inc(s["act_lo"], 1)

            def gates(b, c):
                own = Steps(dve, s["moe_dve"], b * (2 * GU_CHUNKS) + 2 * c)
                gu, ug = gu_sb[0:CAP, c % 2, :], ug_sb[0:CAP, c % 2, :]
                dve.wait_ge(s["half_used"], b * HALVES + (2 * c + 2))
                dve.tensor_scalar(gu, bank[c % 2][0:CAP, :], LIMIT, None, ALU.min).then_inc(s["evac_done"], 1)
                dve.wait_ge(s["evac_done"], b * GU_CHUNKS + (c + 1))
                own(dve.tensor_scalar(ug, gu[:, 256:512], -LIMIT, 1.0, ALU.max, ALU.add))
                own.mark(dve.tensor_tensor(ug, ug, gu[:, 0:256], ALU.mult))

            def activations(b, c):
                dve.wait_ge(s["moe_dve"], b * (2 * GU_CHUNKS) + 2 * c + 2)
                dve.wait_ge(s["sig_done"], b * GU_CHUNKS + (c + 1))
                dve.tensor_tensor(act_sb[0:CAP, c % 2, :], ug_sb[0:CAP, c % 2, :], sig_sb[0:CAP, c % 2, :], ALU.mult)\
                   .then_inc(s["act_ready"], 1)

            def first_part(b, first=False):
                for i in range(9):
                    if first and i >= 1:
                        part = acc[:, (i - 1) // 2, (i - 1) % 2 * 512:((i - 1) % 2 + 1) * 512]
                        dve.wait_ge(s["bdn_ready"], i)
                        dve.tensor_tensor(part, part, bank[6 + (i - 1) % 2][:, :], ALU.add).then_inc(s["bdn_done"], 1)
                    if i >= 2 and i % 2 == 0:
                        gates(b, i // 2 - 1)
                    split_lo(b, i + 3)
                    if i >= 2 and i % 2 == 0:
                        activations(b, i // 2 - 1)
                    if i >= 4 and i % 2 == 0:
                        turned_lo(b, i // 2 - 2)
                gathered_lo(b + 1)

            gathered_lo(0)
            for i in range(1, 3):
                split_lo(0, i)
            first_part(0, True)
            with dve.Fori(1, BLOCKS + 1) as b:
                with dve.If(b <= T):
                    with dve.If(b < T):
                        split_lo(b, 0)
                        turned_lo(b - 1, GU_CHUNKS - 1)
                        split_lo(b, 1)
                        split_lo(b, 2)
                        first_part(b)
                    with dve.If(b == T):
                        turned_lo(b - 1, GU_CHUNKS - 1)

            def combine(i):
                for n in range(2):
                    part = acc[:, i, n * 512:(n + 1) * 512]
                    dve.wait_ge(s["combined"], 2 * i + n + 1)
                    dve.tensor_tensor(part, part, bank[2 * i + n][:, :], ALU.add).then_inc(s["acc_done"], 1)
                dve.wait_ge(s["acc_done"], 2 * i + 2)
                row_stats(i, acc[:, i, :], s["v2_ready"])

            def second_norm(i):
                if i == 0:
                    dve.wait_ge(s["ln2_rows_in"], 32)
                dve.wait_ge(s["v2_ready"], i + 1)
                dve.scalar_tensor_tensor(acc[:, i, :], acc[:, i, :], mva[:, i, 0:1], rowvec[:, 0:D], ALU.subtract, ALU.mult)\
                   .then_inc(s["x2_ready"], 1)
                dve.wait_ge(s["s2_ready"], i + 1)
                step(dve.reciprocal(rstd[:, i:i + 1], rstd[:, i:i + 1]))
                dve.wait_ge(s["x2_ready"], 2 * i + 1)
                dve.scalar_tensor_tensor(h2[:, i, :], acc[:, i, :], rstd[:, i:i + 1], rowvec[:, D:2 * D], ALU.mult, ALU.add)\
                   .then_inc(s["x2_ready"], 1)

            def first_rms(i):
                dve.wait_ge(s["ss_ready"], 2 * i + 2)
                step(dve.reciprocal(rstd[:, 4 + i:5 + i], rstd[:, 4 + i:5 + i]))
                dve.tensor_scalar(un[:, i, :], h2[:, i, :], rstd[:, 4 + i:5 + i], None, ALU.mult).then_inc(s["un_ready"], 1)

            for i in range(TT):
                combine(i)
                if i >= 1:
                    first_rms(i - 1)
                second_norm(i)
            first_rms(TT - 1)
            for k in range(1, KT, 2):
                dve.wait_ge(s["unT_ready"], k + 1)
                dve.tensor_scalar(uT[:, k, :], bank[k][:, :], pcol("norm1", k), None, ALU.mult).then_inc(s["uT_done_v"], 1)

            H4 = HG_HEADS
            l0, l1 = par[:, PAR["lb"]:PAR["lb"] + H4], par[:, PAR["lb"] + H4:PAR["lb"] + 2 * H4]
            e0, e1, top, lb, lb1 = (small[:, n * H4:(n + 1) * H4] for n in range(5))
            step(dve.tensor_tensor(top, l0, l1, ALU.max))
            step(dve.tensor_tensor(e0, l0, top, ALU.subtract))
            dve.tensor_tensor(e1, l1, top, ALU.subtract).then_inc(s["lb_ready"], 1)
            dve.wait_ge(s["lbe_ready"], 1)
            step(dve.tensor_tensor(top, e0, e1, ALU.add))
            step(dve.reciprocal(top, top))
            step(dve.tensor_tensor(lb, e0, top, ALU.mult))
            step(dve.tensor_tensor(lb1, e1, top, ALU.mult))

            for j in range(4):
                part = hQ[:, j * S:(j + 1) * S]
                dve.wait_ge(s["hsig_ready"], j + 1)
                dve.tensor_tensor(part, part, bank[j % 2][:, :], ALU.mult).then_inc(s["p_evac_v"], 1)
            step.mark(dve.memset(AT, 0.0))
            for j in range(4):
                part = hF[:, j * S:(j + 1) * S]
                dve.wait_ge(s["hsig_ready"], 5 + j)
                step(dve.tensor_scalar(part, part, lb1[:, j:j + 1], lb[:, j:j + 1], ALU.mult, ALU.add))
                ins = dve.tensor_scalar(hK[:, j * S:(j + 1) * S], part, -1.0, 1.0, ALU.mult, ALU.add)
            ins.then_inc(s["fK_ready"], 1)

            def rotate(m):
                dve.wait_ge(s["p_evac"], m + 1)
                if m == 0:
                    dve.wait_ge(s["c2_in"], 32)
                step.mark(dve.tensor_tensor(qkT[:, m, :], raw[:, m % 2, :], cosT, ALU.mult))
                dve.wait_ge(swap_in[m % 2], 64 * (m // 2 + 1))
                step(dve.tensor_tensor(swp[:, m % 2, :], swp[:, m % 2, :], sinT, ALU.mult))
                dve.tensor_tensor(qkT[:, m, :], qkT[:, m, :], swp[:, m % 2, :], ALU.add).then_inc(s["rot_done"], 1)

            for n in range(LEVELS + 1):
                dve.wait_ge(s["lv_ready"], n + 1)
                if n == 0:
                    dve.wait_ge(s["fK_ready"], 1)
                    dve.tensor_tensor(hQ, hQ, hF, ALU.mult).then_inc(s["lv_upd"], 1)
                    dve.wait_ge(s["c2_in"], 32)
                elif n < LEVELS:
                    L = 1 << (n - 1)
                    qv = hQ.rearrange("p (n a l) -> p n a l", a=2, l=L)
                    kv = hK.rearrange("p (n a l) -> p n a l", a=2, l=L)
                    tv = tot[n - 1].rearrange("p (n a) -> p n a", a=2)
                    N = HG_HEADS * S // (2 * L)
                    dve.wait_ge(s["lv_upd"], n)
                    step.mark(dve.tensor_tensor(tot[n], tv[:, :, 0], tv[:, :, 1], ALU.mult))
                    step.mark(dve.tensor_tensor(qv[:, :, 1, :], qv[:, :, 1, :],
                                                tv[:, :, 0:1].broadcast_to([P, N, L]), ALU.mult))
                    dve.tensor_tensor(kv[:, :, 0, :], kv[:, :, 0, :], tv[:, :, 1:2].broadcast_to([P, N, L]), ALU.mult)\
                       .then_inc(s["lv_upd"], 1)
                    step.wait()
                for h in range(HG_HEADS):
                    src = bank[2 + h]
                    if n <= TILE_LEVELS:
                        diag = AT[:, h, :, :].rearrange("p j t -> p (j t)")
                        for j in range(TT):
                            at = j * (S + P)
                            ins = dve.copy_predicated(diag[:, at:at + P], lmask[:, n, :], src[:, j * P:(j + 1) * P])
                    elif n == TILE_LEVELS + 1:
                        for j in range(2):
                            ins = dve.tensor_copy(AT[:, h, 2 * j, (2 * j + 1) * P:(2 * j + 2) * P],
                                                  src[:, j * P:(j + 1) * P])
                    else:
                        ins = dve.tensor_copy(AT[:, h, 0:2, 2 * P:4 * P], src[:, :].rearrange("p (j t) -> p j t", j=2))
                ins.then_inc(s["lv_copied"], 1)
                if n < 4:
                    dve.wait_ge(s["hsig_ready"], 9 + n)
                    dve.tensor_tensor(hG[:, n, :], hG[:, n, :], bank[n % 2][:, :], ALU.mult).then_inc(s["p_evac_v"], 1)
                if n >= 5:
                    rotate(n - 5)
            for m in range(5, 8):
                rotate(m)

            for h in range(HG_HEADS):
                dve.wait_ge(s["ostd_ready"], h + 1)
                step(dve.reciprocal(osq[:, h % 2, :], osq[:, h % 2, :]))
                step(dve.tensor_tensor(o_sb[:, h % 2, :], o_sb[:, h % 2, :], osq[:, h % 2, :], ALU.mult))
                dve.scalar_tensor_tensor(mixed[:, 4 + h, :], o_sb[:, h % 2, :], pcol("hg_norm", h), hG[:, h, :],
                                         ALU.mult, ALU.mult).then_inc(s["hmix_ready"], 1)

            def masked(u):
                i = u % TT
                w = (i + 1) * P
                a4 = u % AHEAD
                top, bias = att_s[:, a4:a4 + 1], att_s[:, 2 * AHEAD + a4:2 * AHEAD + a4 + 1]
                dve.wait_ge(s["sc_ready"], u + 1)
                step(dve.tensor_tensor_reduce(sc[:, a4, 0:w], bank[u % 2][:, 0:w], madd[:, S - w:S], 1.0, NEG * 4,
                                              ALU.add, ALU.max, top))
                dve.tensor_scalar(bias, top, -SCALE, None, ALU.mult).then_inc(s["sc_done"], 1)

            def weighted(u):
                i = u % TT
                w = (i + 1) * P
                a4 = u % AHEAD
                total = att_s[:, AHEAD + a4:AHEAD + a4 + 1]
                dve.wait_ge(s["e2_ready"], u + 1)
                step(dve.tensor_tensor_reduce(ex[:, a4, 0:w], ex[:, a4, 0:w], ctab[:, S - w:S], 1.0, 0.0,
                                              ALU.mult, ALU.add, total))
                step(dve.reciprocal(total, total))
                dve.tensor_scalar(ex[:, a4, 0:w], ex[:, a4, 0:w], total, None, ALU.mult).then_inc(s["pn_ready"], 1)

            for u in range(AHEAD - 2):
                masked(u)
            for u in range(HEADS * TT):
                if u + AHEAD - 2 < HEADS * TT:
                    masked(u + AHEAD - 2)
                weighted(u)

            def ffn_lo(f):
                dve.wait_ge(s["fhi_done"], f + 1)
                dve.tensor_tensor(f_lo[f % FPAIRS], fraw_w[f % FRAW], f_hi[f % FPAIRS].bitcast(F32), ALU.subtract)\
                   .then_inc(s["flo_done"], 1)

            def tile_lo(k):
                dve.wait_ge(s["kt_hi"], k + 1)
                dve.tensor_tensor(kt_lo[:, k % 4, :], fact[:, k, :], kt_hi[:, k % 4, :].bitcast(F32), ALU.subtract)\
                   .then_inc(s["kt_lo"], 1)

            ffn_lo(0)
            for i in range(TT):
                for n in range(2):
                    g = 2 * i + n
                    dve.wait_ge(s["o2_ready"], g + 1)
                    part = h2[:, i, n * 512:(n + 1) * 512]
                    dve.tensor_tensor(part, part, bank[g % 4][:, :], ALU.add).then_inc(s["h3_ready"], 1)
                dve.wait_ge(s["ss3_ready"], 2 * i + 2)
                step(dve.reciprocal(rstd[:, i:i + 1], rstd[:, i:i + 1]))
                dve.tensor_scalar(un2[:, i, :], h2[:, i, :], rstd[:, i:i + 1], None, ALU.mult).then_inc(s["un3_ready"], 1)
            for k in range(KT):
                dve.wait_ge(s["u2T_hi"], k + 1)
                dve.scalar_tensor_tensor(u2T_lo[:, k, :], bank[k][:, :], pcol("norm2", k), u2T_hi[:, k, :].bitcast(F32),
                                         ALU.mult, ALU.subtract).then_inc(s["u2T_lo"], 1)

            for f in range(FFN_T):
                ffn_lo(f + 1)
                dve.wait_ge(s["fs_ready"], f + 1)
                step(dve.tensor_tensor(fsig[:, f % 2, :], fsig[:, f % 2, :], bank[2 * (f % 2)][:, :], ALU.mult))
                dve.wait_ge(s["f_ready"], 2 * f + 2)
                dve.tensor_tensor(fact[:, f, :], fsig[:, f % 2, :], bank[2 * (f % 2) + 1][:, :], ALU.mult)\
                   .then_inc(s["f_evac"], 1)
                if f >= FFN_T - 4:
                    tile_lo(f - (FFN_T - 4))
            for c in range(FFN_T // 2):
                if c >= 2:
                    tile_lo(2 * c)
                    tile_lo(2 * c + 1)
                if c + 1 < FFN_T // 2:
                    ffn_lo(FFN_T + c + 1)

            dve.wait_ge(s["fin_row_in"], 16)
            for i in range(TT):
                dve.wait_ge(s["fd_ready"], i + 1)
                for n in range(2):
                    part = h2[:, i, n * 512:(n + 1) * 512]
                    dve.tensor_tensor(part, part, bank[2 * i + n][:, :], ALU.add).then_inc(s["h4_ready"], 1)
            for i in range(TT):
                dve.wait_ge(s["ss4_ready"], 2 * i + 2)
                step(dve.reciprocal(rstd[:, 4 + i:5 + i], rstd[:, 4 + i:5 + i]))
                dve.scalar_tensor_tensor(outt[:, i, :], h2[:, i, :], rstd[:, 4 + i:5 + i], rowvec[:, 0:D], ALU.mult, ALU.mult)\
                   .then_inc(s["out_ready"], 1)



def constants():
    f = np.float32
    p = np.arange(P)
    c = {}
    c["cst"] = np.concatenate([np.eye(P), np.ones((P, P)), p[:, None] < p[None, :]], axis=1).astype(f)
    t = np.arange(S)
    windows = np.repeat([[2, 4], [8, 16]], P // 2, axis=1).reshape(2, P)
    c["invcnt"] = (1.0 / np.minimum(t[None, None, :] + 1, windows.T[:, :, None])).astype(f).reshape(P, 2 * S)
    c["eiota"] = np.arange(E, dtype=f)[None, :]
    token = (p[:, None, None] + P * np.arange(TT)[None, :, None]) + np.zeros((1, 1, TOPK), int)
    c["pairs"] = np.stack([token + S * np.arange(TOPK), token], axis=-1).reshape(P, -1).astype(np.int32)
    c["expert"] = np.where(p < 2 * E, p % E, -1).astype(f)[:, None]
    c["blockid"] = np.arange(META, dtype=f)[None, :]
    delta = p[:, None] + (TT - 1) * P - t[None, :]
    count = np.zeros((P, S))
    for window, dilation in ((128, 1), (512, 4), (2048, 16)):
        count += (delta >= 0) & (delta <= window) & (delta % dilation == 0)
    half = DH // 2
    inv_freq = (f(10000.0) ** (-np.arange(half, dtype=f) / f(half))).astype(f)
    ang = (t.astype(f)[None, :] * inv_freq[p % half][:, None]).astype(f).astype(np.float64)
    sign = np.where(p % DH < half, -1.0, 1.0)[:, None]
    c["c2"] = np.concatenate([count, np.where(count > 0, 0.0, NEG), np.cos(ang), sign * np.sin(ang)], axis=1).astype(f)
    levels = [np.eye(P)]
    for n in range(TILE_LEVELS):
        L = 1 << n
        levels.append((p[:, None] // (2 * L) == p[None, :] // (2 * L)) & (p[:, None] // L % 2 == 0) & (p[None, :] // L % 2 == 1))
    c["lmask"] = np.concatenate(levels, axis=1).astype(np.int32)
    return c


def kernel(**inputs):
    import concourse.bacc as _bacc
    from concourse.bass_utils import run_bass_kernel_spmd as _run

    x = {k: np.asarray(val) for k, val in inputs.items()}

    def cols(w, tiles):
        w = w.reshape(w.shape[0] // P, P, -1, P)[:, :, tiles, :]
        return w.transpose(1, 0, 2, 3).reshape(P, -1)

    def per_channel(w):
        n = w.shape[0]
        return w.reshape(n, -1, P).transpose(2, 1, 0).reshape(P, -1)

    def pack(chunks):
        out = np.zeros((len(chunks), P, CH), np.float32)
        for n, c in enumerate(chunks):
            out[n, :, 0:c.shape[1]] = c
        return out

    w_in = x["w_in"][0]
    order = [0, 3, 1, 4, 2, 5, 9, 12, 10, 13, 11, 14, 15, 16, 6, 7, 8]
    w_out = x["w_out"][0]
    pg, pp = x["ple_w_gate"][0], x["ple_w_proj"][0]
    arrays = {}
    arrays["wd"] = pack([cols(w_in, order[4 * n:4 * n + 4]) for n in range(5)]
                        + [cols(w_out, list(range(4 * n, 4 * n + 4))) for n in range(2)]
                        + [cols(pg, list(range(4 * n, 4 * n + 4))) for n in range(2)]
                        + [cols(pp, list(range(8)))])
    gu = x["w_gate_up"][0].reshape(E, 2, 4, P, 2, GU_CHUNKS, 2, P)
    gu = gu.transpose(0, 5, 1, 3, 2, 4, 6, 7).reshape(E, 2 * GU_CHUNKS, P, HW)
    dn = x["w_down"][0].reshape(E, GU_CHUNKS, 2, P, D).transpose(0, 1, 3, 2, 4).reshape(E, GU_CHUNKS, P, HW)
    arrays["wmoe"] = np.concatenate([gu, dn], axis=1)
    w2 = x["w_in_2_2"][0] if "w_in_2_2" in x else x["w_in_2"][0]
    g2 = x["w_gate_up_2"][0]
    d2 = x["w_down_2"][0].reshape(FFN_T, P, D).transpose(1, 0, 2)
    arrays["wp"] = pack([cols(w2, list(range(a, a + 4))) for a in (12, 16, 24, 0, 4, 8, 20)]
                        + [cols(x["w_out_2"][0], list(range(4 * n, 4 * n + 4))) for n in range(2)])
    d2 = d2.reshape(P, FFN_T // 2, 2 * D)
    arrays["wf"] = np.concatenate([np.stack([cols(g2, [f, FFN_T + f]) for f in range(FFN_T)]), d2.transpose(1, 0, 2)])
    c = constants()
    arrays["par"] = np.concatenate(
        [per_channel(x["conv_a_w"][0]), per_channel(x["conv_a_b"]), per_channel(x["ln_a_g"]), per_channel(x["ln_a_b"]),
         per_channel(x["conv_b_w"][0]), per_channel(x["pool_scale"]), per_channel(x["ln1_g"]), per_channel(x["ln1_b"]),
         per_channel(x["norm1_w_2"]), per_channel(x["norm2_w_2"]), per_channel(x["hgrn_norm_w_2"]),
         per_channel(x["lb_logits_2"][0:1]), per_channel(x["lb_logits_2"][1:2]),
         np.tile(np.array([[LN_EPS, NORM_EPS]], np.float32), (P, 1)), c.pop("expert")], axis=1)
    poolw = np.zeros((2, P, P), np.float32)
    for g in range(4):
        lo = (g % 2) * 64
        poolw[g // 2, lo:lo + 64, lo:lo + 64] = x["pool_w"][0, g]
    arrays["poolw"] = poolw.transpose(1, 0, 2).reshape(P, 2 * P)
    arrays["rw"] = x["router_w"][0].reshape(KT, P, E).transpose(1, 0, 2).reshape(P, KT * E)
    arrays["rb"] = x["router_b"]
    arrays["rows"] = np.concatenate([x["ln1_g"], x["ln1_b"], x["ln2_g"], x["ln2_b"], x["final_norm_w_2"][None]], axis=0)
    arrays["xT"] = x["x"][0].reshape(S, KT, P).transpose(2, 1, 0).reshape(P, KT * S)
    arrays["xtok"] = x["x"][0].reshape(TT, P, D).transpose(1, 0, 2).reshape(P, TT * D)
    arrays["pT"] = x["p"][0, 0].reshape(S, 2, P).transpose(2, 1, 0).reshape(P, 2 * S)
    bgu = np.zeros((P, 4 * 512), np.float32)
    bgu[0:E] = bgu[E:2 * E] = x["b_gate_up"][0].reshape(E, 2, GU_CHUNKS, 256).transpose(0, 2, 1, 3).reshape(E, -1)
    arrays["bgu"] = bgu
    arrays["bdn"] = x["b_down"][0]
    arrays.update(c)

    nc = _bacc.Bacc("TRN2", target_bir_lowering=False, num_devices=1)
    handles = {}
    arrays = {f"in_{k}": np.ascontiguousarray(val) for k, val in arrays.items()}
    for k, val in arrays.items():
        handles[k[3:]] = nc.dram_tensor(k, val.shape, mybir.dt.from_np(val.dtype), kind="ExternalInput").ap()
    handles["out"] = nc.dram_tensor("out_0", (S, D), F32, kind="ExternalOutput").ap()
    build(nc, handles)
    r = _run(nc, [arrays], core_ids=[0])
    return r.results[0]["out_0"].reshape(1, S, D)
```
